# Optimizing a Trainium2 kernel written in Bass

```python
import math
import jax, jax.numpy as jnp
from jax import lax
import numpy as np

D_MODEL = 1024
BATCH = 1
SEQ = 2048
DEPTH = 1
DEC_BATCH = 8
DEC_SEQ = 8
PAST_LEN = 512
PAGE_SIZE = 128

D_ATTN = D_MODEL // 2
D_HGRN = D_MODEL - D_ATTN
D_MIX = D_ATTN + D_HGRN
A_HEADS = 4
A_DV = D_ATTN // A_HEADS
A_DQK = A_DV // 2
ROT_DIM = A_DQK // 4
ROPE_THETA = 500000.0
H_HEADS = 4
H_DK = D_HGRN // H_HEADS
H_DV = D_HGRN // H_HEADS
HGRN_CHUNK = 64
Q_BLOCK = 128
EPS = 1e-6

kernel_name = "hymba_diffattn_hgrn2_step"

def _split_points():
    sizes = [A_HEADS * 2 * A_DQK, A_HEADS * 2 * A_DQK, A_HEADS * A_DV, D_ATTN,
             H_HEADS * H_DK, H_HEADS * H_DK, H_HEADS * H_DV, D_HGRN]
    return [int(c) for c in np.cumsum(sizes)[:-1]]

def _rms_norm(x, g):
    xf = x.astype(jnp.float32)
    y = xf * lax.rsqrt(jnp.mean(xf * xf, axis=-1, keepdims=True) + EPS)
    return (y * g.astype(jnp.float32)).astype(x.dtype)

def _rope(x, pos):
    inv = ROPE_THETA ** (-jnp.arange(0, ROT_DIM, 2, dtype=jnp.float32) / ROT_DIM)
    ang = pos.astype(jnp.float32)[:, None] * inv[None, :]
    cos = jnp.cos(ang)[None, :, None, None, :]
    sin = jnp.sin(ang)[None, :, None, None, :]
    xf = x.astype(jnp.float32)
    half = ROT_DIM // 2
    x1, x2 = xf[..., :half], xf[..., half:ROT_DIM]
    out = jnp.concatenate([x1 * cos - x2 * sin, x2 * cos + x1 * sin, xf[..., ROT_DIM:]], axis=-1)
    return out.astype(x.dtype)

def _mixer_inputs(x, pos, norm_g, w_in, q_norm_g, k_norm_g, lb):
    B, T, _ = x.shape
    h = _rms_norm(x, norm_g)
    aq, ak, av, ag, hq, hf, hi, hg = jnp.split(h @ w_in, _split_points(), axis=-1)
    aq = _rope(_rms_norm(aq.reshape(B, T, A_HEADS, 2, A_DQK), q_norm_g), pos)
    ak = _rope(_rms_norm(ak.reshape(B, T, A_HEADS, 2, A_DQK), k_norm_g), pos)
    av = av.reshape(B, T, A_HEADS, A_DV)
    hq = jax.nn.silu(hq).reshape(B, T, H_HEADS, H_DK)
    f = lb + (1.0 - lb) * jax.nn.sigmoid(hf.astype(jnp.float32))
    logf = jnp.log(f).reshape(B, T, H_HEADS, H_DK)
    hk = (1.0 - f).reshape(B, T, H_HEADS, H_DK)
    hi = hi.reshape(B, T, H_HEADS, H_DV)
    return aq, ak, av, ag, hq, hk, logf, hi, hg

def _diff_attend(q, k, v, q_pos, k_pos, lam):
    s = jnp.einsum('bqhmd,bshmd->bhmqs', q.astype(jnp.float32), k.astype(jnp.float32)) * (A_DQK ** -0.5)
    mask = k_pos[None, :] <= q_pos[:, None]
    s = jnp.where(mask, s, -jnp.inf)
    p = jax.nn.softmax(s, axis=-1)
    w = p[:, :, 0] - lam * p[:, :, 1]
    return jnp.einsum('bhqs,bshd->bqhd', w, v.astype(jnp.float32))

def _prompt_attend(q, k, v, pos, lam):
    B, T = q.shape[:2]
    nb = T // Q_BLOCK
    qb = q.reshape(B, nb, Q_BLOCK, A_HEADS, 2, A_DQK).swapaxes(0, 1)
    pb = pos.reshape(nb, Q_BLOCK)
    o = lax.map(lambda a: _diff_attend(a[0], k, v, a[1], pos, lam), (qb, pb))
    return o.swapaxes(0, 1).reshape(B, T, A_HEADS, A_DV)

def _hgrn2(q, k, logf, v, S0):
    B, T, H, DK = q.shape
    DV = v.shape[-1]
    C = HGRN_CHUNK if T % HGRN_CHUNK == 0 else T
    n = T // C
    def to_chunks(a):
        return a.astype(jnp.float32).reshape(B, n, C, H, a.shape[-1]).swapaxes(0, 1)
    xs = (to_chunks(q), to_chunks(k), to_chunks(logf), to_chunks(v))
    tri = jnp.tril(jnp.ones((C, C), dtype=bool))[None, :, :, None, None]
    def step(S, inp):
        qc, kc, lfc, vc = inp
        b = jnp.cumsum(lfc, axis=1)
        diff = b[:, :, None] - b[:, None, :]
        decay = jnp.exp(jnp.where(tri, diff, -jnp.inf))
        att = jnp.einsum('bthd,bshd,btshd->bhts', qc, kc, decay)
        o = jnp.einsum('bhts,bshv->bthv', att, vc) + jnp.einsum('bthd,bhdv->bthv', qc * jnp.exp(b), S)
        bC = b[:, -1]
        S_new = jnp.exp(bC)[..., None] * S + jnp.einsum('bshd,bshv->bhdv', kc * jnp.exp(bC[:, None] - b), vc)
        return S_new, o
    S_fin, o = lax.scan(step, S0.astype(jnp.float32), xs)
    return o.swapaxes(0, 1).reshape(B, T, H, DV), S_fin

def _merge(x, o_attn, ag, o_hgrn, hg, subln_g, hgrn_norm_g, lam_init, w_out):
    B, T, _ = x.shape
    a = (_rms_norm(o_attn, subln_g) * (1.0 - lam_init)).reshape(B, T, D_ATTN) * jax.nn.silu(ag.astype(jnp.float32))
    r = _rms_norm(o_hgrn, hgrn_norm_g).reshape(B, T, D_HGRN) * jax.nn.silu(hg.astype(jnp.float32))
    mix = jnp.concatenate([a, r], axis=-1).astype(x.dtype)
    return x + mix @ w_out

def setup_inputs(seed: int = 0) -> dict:
    key = jax.random.key(seed)
    ks = jax.random.split(key, 20)
    n_pages = PAST_LEN // PAGE_SIZE
    n_used = DEC_BATCH * n_pages
    n_pool = n_used + max(1, n_used // 4)
    f32 = jnp.float32
    d_in = 2 * A_HEADS * 2 * A_DQK + A_HEADS * A_DV + D_ATTN + 2 * H_HEADS * H_DK + H_HEADS * H_DV + D_HGRN
    page_table = jax.random.permutation(ks[5], n_pool)[:n_used].reshape(DEC_BATCH, n_pages).astype(jnp.int32)
    return {
        "x_prompt": jax.random.normal(ks[0], (BATCH, SEQ, D_MODEL), f32),
        "x_sample": jax.random.normal(ks[1], (DEC_BATCH, DEC_SEQ, D_MODEL), f32),
        "cache_k": jax.random.normal(ks[2], (DEPTH, n_pool, PAGE_SIZE, A_HEADS, 2 * A_DQK), f32),
        "cache_v": jax.random.normal(ks[3], (DEPTH, n_pool, PAGE_SIZE, A_HEADS, A_DV), f32),
        "state_hgrn": 0.5 * jax.random.normal(ks[4], (DEPTH, DEC_BATCH, H_HEADS, H_DK, H_DV), f32),
        "page_table": page_table,
        "norm_g": 1.0 + 0.02 * jax.random.normal(ks[6], (DEPTH, D_MODEL), f32),
        "w_in": jax.random.normal(ks[7], (DEPTH, D_MODEL, d_in), f32) * D_MODEL ** -0.5,
        "q_norm_g": 1.0 + 0.02 * jax.random.normal(ks[8], (DEPTH, A_DQK), f32),
        "k_norm_g": 1.0 + 0.02 * jax.random.normal(ks[9], (DEPTH, A_DQK), f32),
        "lambda_q1": 0.1 * jax.random.normal(ks[10], (DEPTH, A_DQK), f32),
        "lambda_k1": 0.1 * jax.random.normal(ks[11], (DEPTH, A_DQK), f32),
        "lambda_q2": 0.1 * jax.random.normal(ks[12], (DEPTH, A_DQK), f32),
        "lambda_k2": 0.1 * jax.random.normal(ks[13], (DEPTH, A_DQK), f32),
        "subln_g": 1.0 + 0.02 * jax.random.normal(ks[14], (DEPTH, A_DV), f32),
        "hgrn_lb_logits": 0.1 * jax.random.normal(ks[15], (DEPTH + 1, H_HEADS * H_DK), f32),
        "hgrn_norm_g": 1.0 + 0.02 * jax.random.normal(ks[16], (DEPTH, H_DV), f32),
        "w_out": jax.random.normal(ks[17], (DEPTH, D_MIX, D_MODEL), f32) * D_MIX ** -0.5,
    }

def reference(x_prompt, x_sample, cache_k, cache_v, state_hgrn, page_table, norm_g, w_in, q_norm_g,
              k_norm_g, lambda_q1, lambda_k1, lambda_q2, lambda_k2, subln_g, hgrn_lb_logits,
              hgrn_norm_g, w_out):
    Bp, Tp, _ = x_prompt.shape
    Bs, Ts, _ = x_sample.shape
    past_len = page_table.shape[1] * cache_k.shape[2]
    pos_p = jnp.arange(Tp, dtype=jnp.int32)
    pos_s = past_len + jnp.arange(Ts, dtype=jnp.int32)
    kpos_s = jnp.arange(past_len + Ts, dtype=jnp.int32)
    lb_all = jnp.cumsum(jax.nn.softmax(hgrn_lb_logits.astype(jnp.float32), axis=0), axis=0)
    xp, xs = x_prompt, x_sample
    nk_p, nv_p, ns_p, nk_s, nv_s, ns_s = [], [], [], [], [], []
    for l in range(DEPTH):
        lam_init = 0.8 - 0.6 * math.exp(-0.3 * l)
        lam = (jnp.exp(jnp.sum(lambda_q1[l].astype(jnp.float32) * lambda_k1[l].astype(jnp.float32)))
               - jnp.exp(jnp.sum(lambda_q2[l].astype(jnp.float32) * lambda_k2[l].astype(jnp.float32)))
               + lam_init)
        lb = lb_all[l]
        aq, ak, av, ag, hq, hk, lf, hi, hg = _mixer_inputs(xp, pos_p, norm_g[l], w_in[l], q_norm_g[l], k_norm_g[l], lb)
        o_a = _prompt_attend(aq, ak, av, pos_p, lam)
        S0 = jnp.zeros((Bp, H_HEADS, H_DK, H_DV), jnp.float32)
        o_h, S_p = _hgrn2(hq, hk, lf, hi, S0)
        xp = _merge(xp, o_a, ag, o_h, hg, subln_g[l], hgrn_norm_g[l], lam_init, w_out[l])
        nk_p.append(ak.reshape(Bp, Tp, A_HEADS, 2 * A_DQK))
        nv_p.append(av)
        ns_p.append(S_p)
        saq, sak, sav, sag, shq, shk, slf, shi, shg = _mixer_inputs(xs, pos_s, norm_g[l], w_in[l], q_norm_g[l], k_norm_g[l], lb)
        pk = cache_k[l][page_table].reshape(Bs, past_len, A_HEADS, 2, A_DQK)
        pv = cache_v[l][page_table].reshape(Bs, past_len, A_HEADS, A_DV)
        k_all = jnp.concatenate([pk, sak.astype(pk.dtype)], axis=1)
        v_all = jnp.concatenate([pv, sav.astype(pv.dtype)], axis=1)
        so_a = _diff_attend(saq, k_all, v_all, pos_s, kpos_s, lam)
        so_h, S_s = _hgrn2(shq, shk, slf, shi, state_hgrn[l])
        xs = _merge(xs, so_a, sag, so_h, shg, subln_g[l], hgrn_norm_g[l], lam_init, w_out[l])
        nk_s.append(sak.reshape(Bs, Ts, A_HEADS, 2 * A_DQK))
        nv_s.append(sav)
        ns_s.append(S_s)
    return (xp, xs, jnp.stack(nk_p), jnp.stack(nv_p), jnp.stack(ns_p),
            jnp.stack(nk_s), jnp.stack(nv_s), jnp.stack(ns_s))


_drawn_inputs = setup_inputs


def setup_inputs(seed=0):
    import zlib

    import numpy as np

    out = dict(_drawn_inputs(seed))
    spreads = {}
    factors = {'q_norm_g': 8.0,
     'lambda_q1': 200.0,
     'lambda_q2': 59.648,
     'subln_g': 138.518,
     'hgrn_norm_g': 103.83,
     'lambda_k2': 8.0}
    for name, (base, spread) in spreads.items():
        noise = np.random.default_rng([zlib.crc32(name.encode()), seed]).standard_normal(out[name].shape)
        drawn = base * np.exp(spread * noise) if base else spread * noise
        out[name] = __import__('jax').numpy.asarray(drawn.astype(out[name].dtype))
    for name, factor in factors.items():
        out[name] = (out[name] * factor).astype(out[name].dtype)
    return out
```

```python
from contextlib import ExitStack

import numpy as np

import concourse.bass as bass
from concourse import mybir

ALU = mybir.AluOpType
ACT = mybir.ActivationFunctionType
AX = mybir.AxisListType
F32 = mybir.dt.float32
F32R = mybir.dt.float32r
BF16 = mybir.dt.bfloat16
I32 = mybir.dt.int32

P = 128
D = 1024
KD = D // P
SEQ, DEC_B, DEC_T = 2048, 8, 8
NS = DEC_B * DEC_T
NP = SEQ // P
NT = NP + 1
GW = 512
NG = 8
H = 4
DQ = 64
DV = 128
HALF = 8
PAST, PAGE = 512, 128
NPG = PAST // PAGE
N_POOL = 40
EPS = 1e-6
LAM_INIT = 0.2
SCALE = DQ ** -0.5


def f32(ap):
    return ap.bitcast(F32)


def handles(sems):
    for x in sems:
        if isinstance(x, (list, tuple)):
            yield from handles(x)
        else:
            yield x


def clear_semaphores(nc, sems):
    nums = sorted(x.num for x in handles(sems))
    while nums:
        n = 1
        while n < len(nums) and nums[n] == nums[0] + n:
            n += 1
        nc.all_engine_barrier(sems_to_clear=range(nums[0], nums[0] + n))
        nums = nums[n:]


def open_block(nc, ctx, sems):
    ctx.callback(clear_semaphores, nc, sems)
    return ctx.enter_context(nc.Block())


def split_weights(eng_kind, eng, n_halves, s, bufs):
    stage, wg, w_hi, w_lo = bufs
    for n in range(n_halves):
        g, b = n // 2, n % 2
        ks = slice(4 * b, 4 * b + 4)
        cols = slice(g * GW, (g + 1) * GW)
        if eng_kind == "act":
            eng.wait_ge(s["w_scaled"], n + 1)
            eng.activation(w_hi[:, ks, cols], stage[:, b], ACT.Copy).then_inc(s["w_hi"], 1)
        else:
            eng.wait_ge(s["w_staged"][b], 16 * (g + 1))
            if n == 0:
                eng.wait_ge(s["w_norm"], 16)
            eng.tensor_tensor(stage[:, b], stage[:, b],
                              wg[:, ks, None].broadcast_to([P, 4, GW]), ALU.mult).then_inc(s["w_scaled"], 1)
            eng.wait_ge(s["w_hi"], n + 1)
            eng.tensor_tensor(w_lo[:, ks, cols], stage[:, b], f32(w_hi[:, ks, cols]),
                              ALU.subtract).then_inc(s["w_lo"], 1)


def stage_weights(eng, w_dram, first_col, n_halves, s, bufs):
    stage = bufs[0]
    for n in range(n_halves):
        g, b = n // 2, n % 2
        if n >= 2:
            eng.wait_ge(s["w_lo"], n - 1)
        src = w_dram.rearrange("(k p) n -> p k n", p=P)[:, 4 * b:4 * b + 4,
                                                        first_col + g * GW:first_col + (g + 1) * GW]
        eng.dma_start(stage[:, b], src).then_inc(s["w_staged"][b], 16)


def product3(eng, out, x_hi, x_lo, w_hi, w_lo, cols):
    for k in range(KD):
        for a, b in ((x_hi, w_hi), (x_hi, w_lo), (x_lo, w_hi)):
            mm = eng.matmul(out, a[:, k, :], b[:, k, cols], start=(k == 0 and a is x_hi and b is w_hi),
                            stop=(k == KD - 1 and a is x_lo))
    return mm


def pass_attention_inputs(nc, io, keep):
    with ExitStack() as ctx:
        def sb(name, shape, dt=F32):
            return ctx.enter_context(nc.sbuf_tensor("a_" + name, shape, dt))

        def sem(name):
            return ctx.enter_context(nc.semaphore("a_" + name))

        w_hi = sb("w_hi", [P, KD, 4 * GW], F32R)
        w_lo = sb("w_lo", [P, KD, 4 * GW], F32R)
        stage = sb("stage", [P, 2, 4, GW])
        wg = sb("wg", [P, KD])
        xt = sb("xt", [P, 2, D])
        xT_hi = [sb(f"xT_hi{p}", [P, KD, P], F32R) for p in range(2)]
        xT_lo = [sb(f"xT_lo{p}", [P, KD, P], F32R) for p in range(2)]
        ident, rstd = keep[:2]
        rope = sb("rope", [P, NT, 4 * HALF])
        qkg = sb("qkg", [P, 2, DQ])
        eps = sb("eps", [P, 1])
        ssx = sb("ssx", [P, 4])
        sq = sb("sq", [P, 2 * GW])
        ss = sb("ss", [P, 3, 16])
        qk = sb("qk", [P, 2, 16, DQ])
        rot = sb("rot", [P, 2, 16, 2 * HALF])
        vb = sb("vb", [P, 2, GW])
        gb = sb("gb", [P, 2, GW])
        proj = [ctx.enter_context(nc.psum_tensor(f"a_proj{g}", [P, GW], F32)) for g in range(4)]
        xps = [ctx.enter_context(nc.psum_tensor(f"a_xps{b}", [P, 4, P], F32)) for b in range(2)]

        s = {n: sem(n) for n in ("w_norm", "w_scaled", "w_hi", "w_lo", "consts", "eps", "x_ss", "x_root",
                                 "x_rs", "x_norm", "xT_ps", "xT_hi", "xT_lo", "qk_sq", "qk_ss", "qk_root", "qk_rs",
                                 "qk_norm", "qk_g", "qk_t1", "qk_t2", "qk_rot", "v_ready", "g_ready")}
        s["w_staged"] = [sem(f"w_staged{b}") for b in range(2)]
        s["x_load"] = [sem(f"x_load{p}") for p in range(2)]
        s["proj"] = [sem(f"proj{g}") for g in range(4)]
        s["store"] = [[sem(f"store{n}{p}") for p in range(2)] for n in range(4)]
        bufs = (stage, wg, w_hi, w_lo)
        block = open_block(nc, ctx, s.values())

        @block.sync
        def _(sp):
            sp.dma_start(wg[:, :], io["norm_g"]).then_inc(s["w_norm"], 16)
            for p in range(2):
                sp.dma_start(xt[:, p], io["x"][p * P:(p + 1) * P, :]).then_inc(s["x_load"][p], 16)
            stage_weights(sp, io["w_in"], 0, 8, s, bufs)
            sp.dma_start(rope[:, :, :], io["rope"]).then_inc(s["consts"], 16)
            for n, name in enumerate(("q_norm_g", "k_norm_g")):
                sp.dma_start(qkg[:, n], io[name].partition_broadcast(P).rearrange("p a b -> p (a b)")).then_inc(s["consts"], 16)

            def stores(i, j, p, rows, dst_q, dst_k, dst_v, dst_g):
                sp.wait_ge(s["qk_rot"], i + 1)
                sp.dma_start(dst_q, qk[0:rows, p, 0:8].rearrange("p a b -> p (a b)")).then_inc(s["store"][0][p], 16)
                sp.dma_start(dst_k, qk[0:rows, p, 8:16].rearrange("p a b -> p (a b)")).then_inc(s["store"][1][p], 16)
                sp.wait_ge(s["v_ready"], i + 1)
                sp.dma_start(dst_v, vb[0:rows, p]).then_inc(s["store"][2][p], 16)
                sp.wait_ge(s["g_ready"], i + 1)
                sp.dma_start(dst_g, gb[0:rows, p]).then_inc(s["store"][3][p], 16)

            def prompt_stores(i, j, p):
                r = bass.ds(i * P, P)
                stores(i, j, p, P, io["q_s"][r, :], io["k_p"][r, :], io["v_p"][r, :], io["ga_s"][r, :])

            with sp.Fori(0, NP // 2 - 1) as j:
                for p in range(2):
                    i = j * 2 + p
                    sp.wait_ge(s["xT_ps"], 2 * (i + 1))
                    sp.dma_start(xt[:, p], io["x"][bass.ds((i + 2) * P, P), :]).then_inc(s["x_load"][p], 16)
                    prompt_stores(i, j, p)
            for i in (NP - 2, NP - 1):
                if i == NP - 2:
                    sp.wait_ge(s["xT_ps"], 2 * (i + 1))
                    sp.dma_start(xt[:, 0], io["x"][NP * P:NT * P, :]).then_inc(s["x_load"][0], 16)
                prompt_stores(i, i // 2, i % 2)
            r = slice(NP * P, NP * P + NS)
            stores(NP, NP // 2, 0, NS, io["q_s"][r, :], io["k_s"], io["v_s"], io["ga_s"][r, :])
            for n in range(4):
                sp.wait_ge(s["store"][n][0], 16 * (NP // 2 + 1))
                sp.wait_ge(s["store"][n][1], 16 * (NP // 2))

        @block.gpsimd
        def _(pool):
            pool.wait_ge(s["consts"], 48)

            def rotate(i, p):
                q = qk[:, p]
                pool.wait_ge(s["qk_norm"], 2 * i + 2)
                pool.tensor_tensor(q.rearrange("p (a h) d -> p a h d", a=2), q.rearrange("p (a h) d -> p a h d", a=2),
                                   qkg[:, :, None, :].broadcast_to([P, 2, 8, DQ]), ALU.mult).then_inc(s["qk_g"], 1)
                pool.wait_ge(s["qk_g"], i + 1)
                tile = rope[:, bass.ds(i, 1), :] if not isinstance(i, int) else rope[:, i:i + 1, :]
                cc = tile[:, :, 0:2 * HALF].broadcast_to([P, 16, 2 * HALF])
                lo = tile[:, :, 2 * HALF:3 * HALF].broadcast_to([P, 16, HALF])
                hi = tile[:, :, 3 * HALF:4 * HALF].broadcast_to([P, 16, HALF])
                pool.tensor_tensor(rot[:, 0], q[:, :, 0:2 * HALF], cc, ALU.mult).then_inc(s["qk_t1"], 1)
                pool.tensor_tensor(rot[:, 1, :, 0:HALF], q[:, :, HALF:2 * HALF], lo, ALU.mult).then_inc(s["qk_t2"], 1)
                pool.tensor_tensor(rot[:, 1, :, HALF:], q[:, :, 0:HALF], hi, ALU.mult).then_inc(s["qk_t2"], 1)
                pool.wait_ge(s["qk_t1"], i + 1)
                pool.wait_ge(s["qk_t2"], 2 * i + 2)
                pool.tensor_tensor(q[:, :, 0:2 * HALF], rot[:, 0], rot[:, 1], ALU.add).then_inc(s["qk_rot"], 1)

            with pool.Fori(0, NP // 2) as j:
                for p in range(2):
                    rotate(j * 2 + p, p)
            rotate(NP, 0)

        @block.scalar
        def _(act):
            def x_stats(i, p, load, seen):
                act.wait_ge(s["x_load"][p], load)
                act.wait_ge(s["qk_ss"], seen)
                act.activation(sq[:, :], xt[:, p], ACT.Square, accum_out=ssx[:, p:p + 1]).then_inc(s["x_ss"], 1)
                act.wait_ge(s["x_ss"], i + 1)
                act.activation(ssx[:, 2 + p:3 + p], ssx[:, p:p + 1], ACT.Sqrt, bias=eps[:, 0:1], scale=1.0 / D).then_inc(s["x_root"], 1)

            def hi_parts(i, p):
                for b in range(2):
                    act.wait_ge(s["xT_ps"], 2 * i + b + 1)
                    act.activation(xT_hi[p][:, 4 * b:4 * b + 4, :], xps[b][:, :, :], ACT.Copy).then_inc(s["xT_hi"], 1)

            def outputs(i, j, p, nxt):
                act.wait_ge(s["x_ss"], i + 1 + int(nxt))
                for g in range(2):
                    act.wait_ge(s["proj"][g], i + 1)
                    act.activation(sq[:, g * GW:(g + 1) * GW], proj[g][:, :], ACT.Square).then_inc(s["qk_sq"], 1)
                if nxt:
                    hi_parts(i + 1, 1 - p)
                act.wait_ge(s["qk_ss"], 2 * i + 2)
                act.activation(ss[:, 1], ss[:, 0], ACT.Sqrt, bias=eps[:, 0:1], scale=1.0 / DQ).then_inc(s["qk_root"], 1)
                act.wait_ge(s["proj"][2], i + 1)
                act.wait_ge(s["store"][2][p], 16 * j)
                act.activation(vb[:, p], proj[2][:, :], ACT.Copy).then_inc(s["v_ready"], 1)
                act.wait_ge(s["proj"][3], i + 1)
                act.wait_ge(s["store"][3][p], 16 * j)
                act.activation(gb[:, p], proj[3][:, :], ACT.Silu).then_inc(s["g_ready"], 1)

            act.wait_ge(s["eps"], 1)
            x_stats(0, 0, 16, 0)
            split_weights("act", act, 2, s, bufs)
            hi_parts(0, 0)
            split_rest = [2]
            for n in range(2, 8):
                g, b = n // 2, n % 2
                act.wait_ge(s["w_scaled"], n + 1)
                act.activation(w_hi[:, 4 * b:4 * b + 4, g * GW:(g + 1) * GW], stage[:, b], ACT.Copy).then_inc(s["w_hi"], 1)
            with act.Fori(0, NP // 2) as j:
                for p in range(2):
                    i = j * 2 + p
                    x_stats(i + 1, 1 - p, j * 16 + 16 * (1 + p), 2 * i)
                    outputs(i, j, p, True)
            outputs(NP, NP // 2, 0, False)

        @block.vector
        def _(dve):
            def x_norm(i, p):
                dve.wait_ge(s["x_root"], i + 1)
                col = slice(i, i + 1) if isinstance(i, int) else bass.ds(i, 1)
                dve.reciprocal(rstd[:, col], ssx[:, 2 + p:3 + p]).then_inc(s["x_rs"], 1)
                dve.wait_ge(s["x_rs"], i + 1)
                dve.tensor_scalar(xt[:, p], xt[:, p], rstd[:, col], None, ALU.mult).then_inc(s["x_norm"], 1)

            def lo_parts(i, p):
                for b in range(2):
                    dve.wait_ge(s["xT_hi"], 2 * i + b + 1)
                    dve.tensor_tensor(xT_lo[p][:, 4 * b:4 * b + 4, :], xps[b][:, :, :],
                                      f32(xT_hi[p][:, 4 * b:4 * b + 4, :]), ALU.subtract).then_inc(s["xT_lo"], 1)

            def outputs(i, j, p, nxt):
                for g in range(2):
                    dve.wait_ge(s["qk_sq"], 2 * i + g + 1)
                    dve.tensor_reduce(ss[:, 0, 8 * g:8 * g + 8], sq[:, g * GW:(g + 1) * GW].rearrange("p (a b) -> p a b", b=DQ),
                                      AX.X, ALU.add).then_inc(s["qk_ss"], 1)
                if nxt:
                    lo_parts(i + 1, 1 - p)
                dve.wait_ge(s["qk_root"], i + 1)
                dve.reciprocal(ss[:, 2], ss[:, 1]).then_inc(s["qk_rs"], 1)
                dve.wait_ge(s["qk_rs"], i + 1)
                dve.wait_ge(s["store"][0][p], 16 * j)
                dve.wait_ge(s["store"][1][p], 16 * j)
                for g in range(2):
                    dve.tensor_tensor(qk[:, p, 8 * g:8 * g + 8], proj[g][:, :].rearrange("p (a b) -> p a b", b=DQ),
                                      ss[:, 2, 8 * g:8 * g + 8, None].broadcast_to([P, 8, DQ]), ALU.mult).then_inc(s["qk_norm"], 1)

            dve.memset(eps[:, :], EPS).then_inc(s["eps"], 1)
            x_norm(0, 0)
            split_weights("dve", dve, 2, s, bufs)
            lo_parts(0, 0)
            for n in range(2, 8):
                g, b = n // 2, n % 2
                ks, cols = slice(4 * b, 4 * b + 4), slice(g * GW, (g + 1) * GW)
                dve.wait_ge(s["w_staged"][b], 16 * (g + 1))
                dve.tensor_tensor(stage[:, b], stage[:, b], wg[:, ks, None].broadcast_to([P, 4, GW]),
                                  ALU.mult).then_inc(s["w_scaled"], 1)
                dve.wait_ge(s["w_hi"], n + 1)
                dve.tensor_tensor(w_lo[:, ks, cols], stage[:, b], f32(w_hi[:, ks, cols]),
                                  ALU.subtract).then_inc(s["w_lo"], 1)
            with dve.Fori(0, NP // 2) as j:
                for p in range(2):
                    i = j * 2 + p
                    x_norm(i + 1, 1 - p)
                    outputs(i, j, p, True)
            outputs(NP, NP // 2, 0, False)

        @block.tensor
        def _(pe):
            def transposes(i, p):
                pe.wait_ge(s["x_norm"], i + 1)
                pe.wait_ge(s["xT_lo"], 2 * i)
                for b in range(2):
                    for k in range(4):
                        mm = pe.transpose(xps[b][:, k, :], xt[:, p, (4 * b + k) * P:(4 * b + k + 1) * P], ident[:, :])
                    mm.then_inc(s["xT_ps"], 1)

            def group(i, p, g, first):
                pe.wait_ge(s["xT_lo"], 2 * i + 2)
                if first:
                    pe.wait_ge(s["w_lo"], 2 * g + 2)
                if g < 2:
                    pe.wait_ge(s["qk_norm"], 2 * i)
                elif g == 2:
                    pe.wait_ge(s["v_ready"], i)
                else:
                    pe.wait_ge(s["g_ready"], i)
                product3(pe, proj[g][:, :], xT_hi[p], xT_lo[p], w_hi, w_lo,
                         slice(g * GW, (g + 1) * GW)).then_inc(s["proj"][g], 1)

            transposes(0, 0)
            with pe.Fori(0, NP // 2) as j:
                for p in range(2):
                    i = j * 2 + p
                    group(i, p, 0, p == 0)
                    group(i, p, 1, p == 0)
                    transposes(i + 1, 1 - p)
                    group(i, p, 2, p == 0)
                    group(i, p, 3, p == 0)
            for g in range(4):
                group(NP, 0, g, False)


def make_identity(pool, ident, done):
    pool.memset(ident[:, :], 0.0).then_inc(done, 1)
    pool.wait_ge(done, 1)
    pool.affine_select(out=ident[:, :], in_=ident[:, :], compare_op=ALU.not_equal, fill=1.0, base=0,
                       pattern=[[-1, P]], channel_multiplier=1).then_inc(done, 1)


CH = P
BLOCKS = (128, 64, 32, 16, 8, 4)
NL = len(BLOCKS) + 1
LEAF_Q, LEAF_QE, LEAF_K, LEAF_KD = 6, 7, 8, 9
SLOTS = 10
F_MIN = 2.0 ** -62


def level_views(ap, width):
    v = ap.rearrange("p (n two w) -> p n two w", two=2, w=width // 2)
    n = v.shape[1]
    ref = v[:, :, 0, width // 2 - 1:width // 2].broadcast_to([P, n, width // 2])
    return v[:, :, 0, :], v[:, :, 1, :], ref


def decay_differences(dve, b, lv, blocks, last, n0=0):
    for slot, width in blocks:
        b_lo, b_up, ref = level_views(b, width)
        d_lo, d_up, _ = level_views(lv[:, slot - n0, :], width)
        dve.tensor_tensor(d_up, b_up, ref, ALU.subtract)
        dve.tensor_tensor(d_lo, ref, b_lo, ALU.subtract)
    pair = b.rearrange("p (n w) -> p n w", w=2)
    first = pair[:, :, 0:1].broadcast_to([P, pair.shape[1], 2])
    dve.tensor_tensor(lv[:, LEAF_Q - n0, :].rearrange("p (n w) -> p n w", w=2), pair, first, ALU.subtract)
    dve.tensor_tensor(lv[:, LEAF_K - n0, :].rearrange("p (n w) -> p n w", w=2), first, pair, ALU.subtract)
    dve.tensor_copy(lv[:, LEAF_QE - n0, :], b)
    run = b.rearrange("p (n w) -> p n w", w=last)
    end = run[:, :, last - 1:last].broadcast_to([P, run.shape[1], last])
    return dve.tensor_tensor(lv[:, LEAF_KD - n0, :].rearrange("p (n w) -> p n w", w=last), end, run, ALU.subtract)


def decay_products(pool, lv, q, k, blocks, n0=0):
    for slot, width in blocks:
        e_lo, e_up, _ = level_views(lv[:, slot - n0, :], width)
        _, q_up, _ = level_views(q, width)
        k_lo, _, _ = level_views(k, width)
        pool.tensor_tensor(e_up, e_up, q_up, ALU.mult)
        pool.tensor_tensor(e_lo, e_lo, k_lo, ALU.mult)
    n = q.shape[1]
    pool.tensor_tensor(lv[:, LEAF_Q - n0:LEAF_QE + 1 - n0, :], lv[:, LEAF_Q - n0:LEAF_QE + 1 - n0, :],
                       q[:, None, :].broadcast_to([P, 2, n]), ALU.mult)
    return pool.tensor_tensor(lv[:, LEAF_K - n0:LEAF_KD + 1 - n0, :], lv[:, LEAF_K - n0:LEAF_KD + 1 - n0, :],
                              k[:, None, :].broadcast_to([P, 2, n]), ALU.mult)


def pass_hgrn(nc, io, keep):
    with ExitStack() as ctx:
        def sb(name, shape, dt=F32):
            return ctx.enter_context(nc.sbuf_tensor("h_" + name, shape, dt))

        def sem(name):
            return ctx.enter_context(nc.semaphore("h_" + name))

        def ps(name, shape):
            return ctx.enter_context(nc.psum_tensor("h_" + name, shape, F32))

        ident, rstd = keep[:2]
        w_hi = sb("w_hi", [P, KD, 4 * GW], F32R)
        w_lo = sb("w_lo", [P, KD, 4 * GW], F32R)
        shared = sb("stage_or_levels", [P, 2, SLOTS * 2 * P])
        stage = shared[:, :, 0:4 * GW].rearrange("p b (k n) -> p b k n", k=4)
        lv = [shared[:, hf, :].rearrange("p (s n) -> p s n", s=SLOTS) for hf in range(2)]
        wg = sb("wg", [P, KD])
        xt = sb("xt", [P, D])
        xT_hi = [sb(f"xT_hi{p}", [P, KD, P], F32R) for p in range(2)]
        xT_lo = [sb(f"xT_lo{p}", [P, KD, P], F32R) for p in range(2)]
        q_tok, s_tok = sb("q_tok", [P, GW]), sb("s_tok", [P, GW])
        qT, kT, lfT, bT = (sb(n, [P, GW]) for n in ("qT", "kT", "lfT", "bT"))
        v_tok, gate = sb("v_tok", [P, 2, GW]), sb("gate", [P, 2, GW])
        mask = sb("mask", [P, NL, P], BF16)
        masked = sb("masked", [P, NL, P])
        att = sb("att", [P, 2, P])
        kd_tok = sb("kd_tok", [P, GW])
        state = sb("state", [P, H, DV])
        ebc = sb("ebc", [P, 2, H])
        o_out = sb("o_out", [P, GW])
        oss = sb("oss", [P, 3, H])
        ng = sb("ng", [P, DV])
        eps = sb("eps", [P, 1])
        lbt = sb("lbt", [P, 6, H])
        proj = [ps(f"proj{b}", [P, GW]) for b in range(2)]
        xps = [ps(f"xps{b}", [P, 4, P]) for b in range(2)]
        lps = ps("lps", [P, 8, P])
        tps = ps("tps", [P, 4, P])
        ops = ps("ops", [P, H, DV])
        s = {n: sem(n) for n in (
            "w_norm", "w_scaled", "w_hi", "w_lo", "consts", "lb_load", "mask_load", "mask", "eps", "lb", "lb_exp", "x_load",
            "x_norm", "xT_ps", "xT_hi", "xT_lo", "q_tok", "s_tok", "v_tok", "gate", "qT_ps", "sT_ps", "qT", "f",
            "f_clamped", "log_f", "cumsum", "diff", "decay", "ebc", "operands", "levels", "masked", "att", "av", "kdT_ps",
            "kd_tok", "gain_ps", "state", "o_sq", "o_ss", "o_root", "o_rs", "o_norm", "o_g", "o_out", "store", "tail")}
        s["w_staged"] = [sem(f"w_staged{b}") for b in range(2)]
        s["proj"] = [sem(f"proj{g}") for g in range(4)]
        bufs = (stage, wg, w_hi, w_lo)
        block = open_block(nc, ctx, s.values())
        all_levels = tuple(enumerate(BLOCKS))

        def half(ap, hf):
            return ap[:, hf * 2 * P:(hf + 1) * 2 * P]

        @block.sync
        def _(sp):
            sp.dma_start(wg[:, :], io["norm_g"]).then_inc(s["w_norm"], 16)
            sp.dma_start(xt[:, :], io["x"][0:P, :]).then_inc(s["x_load"], 16)
            sp.dma_start(lbt[:, 0:2, :], io["lb"]).then_inc(s["lb_load"], 16)
            sp.dma_start(masked[:, :, :], io["level_mask"]).then_inc(s["mask_load"], 16)
            sp.dma_start(ng[:, :], io["hgrn_norm_g"].partition_broadcast(P).rearrange("p a b -> p (a b)")).then_inc(s["consts"], 16)
            stage_weights(sp, io["w_in"], 4 * GW, 8, s, bufs)
            with sp.Fori(1, NT) as i:
                sp.wait_ge(s["xT_ps"], 2 * i)
                sp.dma_start(xt[:, :], io["x"][bass.ds(i * P, P), :]).then_inc(s["x_load"], 16)
                sp.wait_ge(s["o_out"], i)
                sp.dma_start(io["mr_s"][bass.ds((i - 1) * P, P), :], o_out[:, :]).then_inc(s["store"], 16)
            sp.wait_ge(s["state"], NP + 1)
            sp.dma_start(io["s_p"].rearrange("h d v -> d h v"), state[:, :, :]).then_inc(s["tail"], 16)
            sp.wait_ge(s["qT"], NT)
            sp.dma_start(io["hq_s"], qT[:, :]).then_inc(s["tail"], 16)
            sp.wait_ge(s["f_clamped"], NT)
            sp.dma_start(io["hk_s"], kT[:, :]).then_inc(s["tail"], 16)
            sp.wait_ge(s["log_f"], NT)
            sp.dma_start(io["hl_s"], lfT[:, :]).then_inc(s["tail"], 16)
            sp.wait_ge(s["v_tok"], NT)
            sp.dma_start(io["hv_s"], v_tok[:, 0]).then_inc(s["tail"], 16)
            sp.wait_ge(s["gate"], NT)
            sp.dma_start(io["hg_s"], gate[:, 0]).then_inc(s["tail"], 16)
            sp.wait_ge(s["tail"], 96)
            sp.wait_ge(s["store"], 16 * NP)

        @block.gpsimd
        def _(pool):
            pool.wait_ge(s["consts"], 16)

            def operands(i):
                for hf in range(2):
                    pool.wait_ge(s["decay"], 2 * i + hf + 1)
                    pool.wait_ge(s["qT"], i + 1)
                    pool.wait_ge(s["f_clamped"], i + 1)
                    decay_products(pool, lv[hf], half(qT, hf), half(kT, hf), all_levels).then_inc(s["operands"], 1)

            def gated(t, pt):
                pool.wait_ge(s["o_norm"], t + 1)
                o3 = o_out[:, :].rearrange("p (h v) -> p h v", h=H)
                pool.tensor_tensor(o3, o3, ng[:, None, :].broadcast_to([P, H, DV]), ALU.mult).then_inc(s["o_g"], 1)
                pool.wait_ge(s["o_g"], t + 1)
                pool.wait_ge(s["gate"], t + 1)
                pool.tensor_tensor(o_out[:, :], o_out[:, :], gate[:, pt], ALU.mult).then_inc(s["o_out"], 1)

            operands(0)
            with pool.Fori(0, NP // 2) as j:
                for pt in range(2):
                    t = j * 2 + pt
                    operands(t + 1)
                    gated(t, pt)

        @block.scalar
        def _(act):
            def hi_parts(i, p):
                for b in range(2):
                    act.wait_ge(s["xT_ps"], 2 * i + b + 1)
                    act.activation(xT_hi[p][:, 4 * b:4 * b + 4, :], xps[b][:, :, :], ACT.Copy).then_inc(s["xT_hi"], 1)

            def inputs_qf(i):
                act.wait_ge(s["proj"][0], i + 1)
                act.wait_ge(s["qT_ps"], i)
                act.activation(q_tok[:, :], proj[0][:, :], ACT.Silu).then_inc(s["q_tok"], 1)
                act.wait_ge(s["proj"][1], i + 1)
                act.wait_ge(s["sT_ps"], i)
                act.activation(s_tok[:, :], proj[1][:, :], ACT.Sigmoid).then_inc(s["s_tok"], 1)

            def q_columns(i):
                act.wait_ge(s["qT_ps"], i + 1)
                act.wait_ge(s["operands"], 2 * i)
                act.activation(qT[:, :], tps[:, :, :].rearrange("p h t -> p (h t)"), ACT.Copy).then_inc(s["qT"], 1)

            def inputs_vg(i, p, j):
                act.wait_ge(s["proj"][2], i + 1)
                act.activation(v_tok[:, p], proj[0][:, :], ACT.Copy).then_inc(s["v_tok"], 1)
                act.wait_ge(s["proj"][3], i + 1)
                act.activation(gate[:, p], proj[1][:, :], ACT.Silu).then_inc(s["gate"], 1)

            def decays(i, p):
                act.wait_ge(s["f_clamped"], i + 1)
                act.activation(lfT[:, :], lfT[:, :], ACT.Ln).then_inc(s["log_f"], 1)

            def exps(i, p):
                for hf in range(2):
                    act.wait_ge(s["diff"], 2 * i + hf + 1)
                    act.activation(lv[hf], lv[hf], ACT.Exp).then_inc(s["decay"], 1)
                act.activation(ebc[:, p], bT[:, :].rearrange("p (h t) -> p h t", h=H)[:, :, P - 1], ACT.Exp).then_inc(s["ebc"], 1)

            def o_stats(t):
                act.wait_ge(s["av"], 4 * t + 4)
                act.wait_ge(s["o_ss"], t)
                act.wait_ge(s["store"], 16 * t)
                act.activation(o_out[:, :], ops[:, :, :].rearrange("p h v -> p (h v)"), ACT.Square).then_inc(s["o_sq"], 1)
                act.wait_ge(s["o_ss"], t + 1)
                act.activation(oss[:, 1], oss[:, 0], ACT.Sqrt, bias=eps[:, 0:1], scale=1.0 / DV).then_inc(s["o_root"], 1)

            act.wait_ge(s["lb"], 2)
            act.activation(lbt[:, 3:5, :], lbt[:, 3:5, :], ACT.Exp).then_inc(s["lb_exp"], 1)
            split_weights("act", act, 8, s, bufs)
            hi_parts(0, 0)
            inputs_qf(0)
            q_columns(0)
            decays(0, 0)
            inputs_vg(0, 0, None)
            exps(0, 0)
            with act.Fori(0, NP // 2) as j:
                for pt in range(2):
                    t = j * 2 + pt
                    i, p = t + 1, 1 - pt
                    hi_parts(i, p)
                    inputs_qf(i)
                    act.wait_ge(s["kdT_ps"], t + 1)
                    act.wait_ge(s["gain_ps"], t)
                    act.activation(kd_tok[:, :], xps[1][:, :, :].rearrange("p h d -> p (h d)"), ACT.Copy).then_inc(s["kd_tok"], 1)
                    q_columns(i)
                    decays(i, p)
                    inputs_vg(i, p, j)
                    exps(i, p)
                    o_stats(t)

        @block.vector
        def _(dve):
            def x_norm(i):
                dve.wait_ge(s["x_load"], 16 * i + 16)
                col = slice(i, i + 1) if isinstance(i, int) else bass.ds(i, 1)
                dve.tensor_scalar(xt[:, :], xt[:, :], rstd[:, col], None, ALU.mult).then_inc(s["x_norm"], 1)

            def lo_parts(i, p):
                for b in range(2):
                    dve.wait_ge(s["xT_hi"], 2 * i + b + 1)
                    dve.tensor_tensor(xT_lo[p][:, 4 * b:4 * b + 4, :], xps[b][:, :, :],
                                      f32(xT_hi[p][:, 4 * b:4 * b + 4, :]), ALU.subtract).then_inc(s["xT_lo"], 1)

            def keep_pairs(t, h):
                n = 4 * t + h
                dve.wait_ge(s["levels"], n + 1)
                dve.wait_ge(s["att"], n)
                dve.tensor_tensor(masked[:, :, :], lps[:, 0:NL, :], mask[:, :, :], ALU.mult).then_inc(s["masked"], 1)
                dve.wait_ge(s["masked"], n + 1)
                if h >= 2:
                    dve.wait_ge(s["av"], n - 1)
                dve.tensor_reduce(att[:, h % 2], masked[:, :, :].rearrange("p l t -> p t l"), AX.X, ALU.add).then_inc(s["att"], 1)

            def forget(i):
                dve.wait_ge(s["sT_ps"], i + 1)
                dve.wait_ge(s["operands"], 2 * i)
                for h in range(H):
                    last = dve.tensor_scalar(lfT[:, h * P:(h + 1) * P], xps[0][:, h, :], lbt[:, 4, h:h + 1], lbt[:, 3, h:h + 1],
                                             ALU.mult, ALU.add)
                last.then_inc(s["f"], 1)
                dve.wait_ge(s["f"], i + 1)
                dve.tensor_scalar(kT[:, :], lfT[:, :], -1.0, 1.0, ALU.mult, ALU.add)
                dve.tensor_scalar(lfT[:, :], lfT[:, :], F_MIN, None, ALU.max).then_inc(s["f_clamped"], 1)

            def cumulate(i):
                dve.wait_ge(s["log_f"], i + 1)
                dve.wait_ge(s["ebc"], i)
                for h in range(H):
                    cols = slice(h * P, (h + 1) * P)
                    last = dve.tensor_tensor_scan(bT[:, cols], lfT[:, cols], lfT[:, cols], 0.0, ALU.add, ALU.bypass)
                last.then_inc(s["cumsum"], 1)
                dve.wait_ge(s["cumsum"], i + 1)

            def differences(i, t):
                for hf in range(2):
                    if t is not None:
                        dve.wait_ge(s["av"], 4 * t + 2 * hf + 2)
                        dve.wait_ge(s["kdT_ps"], t + 1)
                    decay_differences(dve, half(bT, hf), lv[hf], all_levels, P).then_inc(s["diff"], 1)

            def o_norm(t):
                o3 = o_out[:, :].rearrange("p (h v) -> p h v", h=H)
                dve.wait_ge(s["o_sq"], t + 1)
                dve.tensor_reduce(oss[:, 0], o3, AX.X, ALU.add).then_inc(s["o_ss"], 1)
                dve.wait_ge(s["o_root"], t + 1)
                dve.reciprocal(oss[:, 2], oss[:, 1]).then_inc(s["o_rs"], 1)
                dve.wait_ge(s["o_rs"], t + 1)
                dve.tensor_tensor(o3, ops[:, :, :], oss[:, 2, :, None].broadcast_to([P, H, DV]), ALU.mult).then_inc(s["o_norm"], 1)

            def carry(t, pt):
                dve.wait_ge(s["gain_ps"], t + 1)
                dve.wait_ge(s["ebc"], t + 1)
                for h in range(H):
                    last = dve.scalar_tensor_tensor(out=state[:, h], in0=state[:, h], scalar=ebc[:, pt, h:h + 1], in1=tps[:, h, :],
                                                    op0=ALU.mult, op1=ALU.add)
                last.then_inc(s["state"], 1)

            dve.memset(eps[:, :], EPS).then_inc(s["eps"], 1)
            dve.memset(state[:, :, :], 0.0).then_inc(s["state"], 1)
            dve.wait_ge(s["mask_load"], 16)
            dve.tensor_copy(mask[:, :, :], masked[:, :, :]).then_inc(s["mask"], 1)
            dve.wait_ge(s["mask"], 1)
            dve.wait_ge(s["lb_load"], 16)
            dve.tensor_tensor(lbt[:, 2], lbt[:, 0], lbt[:, 1], ALU.max).then_inc(s["lb"], 1)
            dve.wait_ge(s["lb"], 1)
            dve.tensor_tensor(lbt[:, 3:5], lbt[:, 0:2], lbt[:, 2, None, :].broadcast_to([P, 2, H]), ALU.subtract).then_inc(s["lb"], 1)
            dve.wait_ge(s["lb_exp"], 1)
            dve.tensor_tensor(lbt[:, 2], lbt[:, 3], lbt[:, 4], ALU.add).then_inc(s["lb"], 1)
            dve.wait_ge(s["lb"], 3)
            dve.reciprocal(lbt[:, 5], lbt[:, 2]).then_inc(s["lb"], 1)
            dve.wait_ge(s["lb"], 4)
            dve.tensor_tensor(lbt[:, 3:5], lbt[:, 3:5], lbt[:, 5, None, :].broadcast_to([P, 2, H]), ALU.mult).then_inc(s["lb"], 1)
            dve.wait_ge(s["lb"], 5)
            x_norm(0)
            split_weights("dve", dve, 8, s, bufs)
            lo_parts(0, 0)
            forget(0)
            cumulate(0)
            differences(0, None)
            with dve.Fori(0, NP // 2) as j:
                for pt in range(2):
                    t = j * 2 + pt
                    i, p = t + 1, 1 - pt
                    x_norm(i)
                    keep_pairs(t, 0)
                    lo_parts(i, p)
                    keep_pairs(t, 1)
                    keep_pairs(t, 2)
                    forget(i)
                    keep_pairs(t, 3)
                    cumulate(i)
                    differences(i, t)
                    o_norm(t)
                    carry(t, pt)

        @block.tensor
        def _(pe):
            def x_columns(i, p):
                pe.wait_ge(s["x_norm"], i + 1)
                pe.wait_ge(s["xT_lo"], 2 * i)
                pe.wait_ge(s["f"], i)
                pe.wait_ge(s["kd_tok"], i if isinstance(i, int) and i == 0 else i - 1)
                for b in range(2):
                    for k in range(4):
                        mm = pe.transpose(xps[b][:, k, :], xt[:, (4 * b + k) * P:(4 * b + k + 1) * P], ident[:, :])
                    mm.then_inc(s["xT_ps"], 1)

            def group(i, p, g, first):
                pe.wait_ge(s["xT_lo"], 2 * i + 2)
                if first:
                    pe.wait_ge(s["w_lo"], 2 * g + 2)
                pe.wait_ge(s[("v_tok", "gate", "q_tok", "s_tok")[g]], i if g < 2 else i + 1)
                product3(pe, proj[g % 2][:, :], xT_hi[p], xT_lo[p], w_hi, w_lo,
                         slice(g * GW, (g + 1) * GW)).then_inc(s["proj"][g], 1)

            def head_columns(i, t):
                pe.wait_ge(s["q_tok"], i + 1)
                pe.wait_ge(s["state"], i)
                for h in range(H):
                    mm = pe.transpose(tps[:, h, :], q_tok[:, h * P:(h + 1) * P], ident[:, :])
                mm.then_inc(s["qT_ps"], 1)
                pe.wait_ge(s["s_tok"], i + 1)
                for h in range(H):
                    mm = pe.transpose(xps[0][:, h, :], s_tok[:, h * P:(h + 1) * P], ident[:, :])
                mm.then_inc(s["sT_ps"], 1)

            def levels(t, h):
                c = slice((h % 2) * P, (h % 2) * P + P)
                l = lv[h // 2]
                pe.wait_ge(s["operands"], 2 * t + h // 2 + 1)
                pe.wait_ge(s["masked"], 4 * t + h)
                for n in range(NL - 1):
                    pe.matmul(lps[:, n, :], l[:, n, c], l[:, n, c], start=True, stop=True)
                pe.matmul(lps[:, NL - 1, :], l[:, LEAF_K, c], l[:, LEAF_Q, c], start=True, stop=True).then_inc(s["levels"], 1)

            def out_rows(t, pt, h):
                c = slice((h % 2) * P, (h % 2) * P + P)
                pe.wait_ge(s["att"], 4 * t + h + 1)
                pe.wait_ge(s["state"], t + 1)
                pe.wait_ge(s["o_norm"], t)
                pe.wait_ge(s["v_tok"], t + 1)
                pe.matmul(ops[:, h, :], att[:, h % 2], v_tok[:, pt, h * DV:(h + 1) * DV], start=True, stop=False)
                pe.matmul(ops[:, h, :], lv[h // 2][:, LEAF_QE, c], state[:, h], start=False, stop=True).then_inc(s["av"], 1)

            def key_rows(t):
                pe.wait_ge(s["operands"], 2 * t + 2)
                for h in range(H):
                    c = slice((h % 2) * P, (h % 2) * P + P)
                    mm = pe.transpose(xps[1][:, h, :], lv[h // 2][:, LEAF_KD, c], ident[:, :])
                mm.then_inc(s["kdT_ps"], 1)

            def gains(t, pt):
                pe.wait_ge(s["kd_tok"], t + 1)
                pe.wait_ge(s["qT"], t + 2)
                for h in range(H):
                    mm = pe.matmul(tps[:, h, :], kd_tok[:, h * P:(h + 1) * P], v_tok[:, pt, h * DV:(h + 1) * DV],
                                   start=True, stop=True)
                mm.then_inc(s["gain_ps"], 1)

            x_columns(0, 0)
            group(0, 0, 0, True)
            group(0, 0, 1, True)
            head_columns(0, None)
            group(0, 0, 2, True)
            group(0, 0, 3, True)
            with pe.Fori(0, NP // 2) as j:
                for pt in range(2):
                    t = j * 2 + pt
                    i, p = t + 1, 1 - pt
                    levels(t, 0)
                    x_columns(i, p)
                    levels(t, 1)
                    out_rows(t, pt, 0)
                    group(i, p, 0, False)
                    out_rows(t, pt, 1)
                    group(i, p, 1, False)
                    levels(t, 2)
                    key_rows(t)
                    head_columns(i, t)
                    group(i, p, 2, False)
                    levels(t, 3)
                    out_rows(t, pt, 2)
                    group(i, p, 3, False)
                    out_rows(t, pt, 3)
                    gains(t, pt)


NEG = -1e30


def pass_attention(nc, io, keep):
    with ExitStack() as ctx:
        def sb(name, shape, dt=F32):
            return ctx.enter_context(nc.sbuf_tensor("p_" + name, shape, dt))

        def sem(name):
            return ctx.enter_context(nc.semaphore("p_" + name))

        def ps(name, shape):
            return ctx.enter_context(nc.psum_tensor("p_" + name, shape, F32))

        ident, nlam = keep[0], keep[2]
        M = 2 * H
        KT = sb("KT", [P, M, SEQ], F32R)
        V = sb("V", [P, NP, H * DV])
        qk_in = sb("qk_in", [P, 2, 2, GW])
        k_hl = sb("k_hl", [P, M, 2, DQ], F32R)
        q_hl = sb("q_hl", [P, 2, M, 2, DQ], F32R)
        QS = [[sb(f"Q{part}{p}", [P, M, P], F32R) for part in "hl"] for p in range(2)]
        sc = [sb(f"scores{m}", [P, 2, SEQ]) for m in range(2)]
        WT = sb("WT", [P, 2, 4, P])
        mask = sb("mask", [P, 4 * P])
        zero = sb("zero", [P, 4 * P])
        mx = sb("mx", [P, 2, 2, 4])
        nmx = sb("nmx", [P, 2, 2])
        ls = sb("ls", [P, 2, 2, H])
        rl = sb("rl", [P, 2, H])
        coef = sb("coef", [P, 2])
        r0 = sb("r0", [P, H])
        ob = sb("ob", [P, 2, H * DV])
        sps = [ps(f"sps{n}", [P, 512]) for n in range(4)]
        tps = [ps(f"tps{n}", [P, 4, P]) for n in range(2)]
        ops = [ps(f"ops{n}", [P, H, DV]) for n in range(2)]
        s = {n: sem(n) for n in ("v_load0", "v_load1", "v_load2", "v_load3", "mask_load", "zero", "q_hi", "k_hi", "q_lo", "k_lo",
                                 "prep_ps", "prep_out", "scores", "row_max", "neg_max", "exp", "recip", "coef",
                                 "weights", "wT_ps", "wT", "out_ps", "r0", "out")}
        s["qk_load"] = [sem(f"qk_load{p}") for p in range(2)]
        s["store"] = [sem(f"store{p}") for p in range(2)]
        block = open_block(nc, ctx, s.values())
        chunks = [[(c, min(512, (i + 1) * P - c)) for c in range(0, (i + 1) * P, 512)] for i in range(NP)]
        first_sc, first_wt, n_sc, n_wt = {}, {}, 0, 0
        for i in range(NP):
            for h in range(H):
                first_sc[i, h], first_wt[i, h] = n_sc, n_wt
                n_sc += 2 * len(chunks[i])
                n_wt += len(chunks[i])
        n_heads = NP * H
        tile_head = [(i, h) for i in range(NP) for h in range(H)]

        def twice(q):
            return q.rearrange("p (m d) -> p m d", d=DQ)[:, :, None, :].broadcast_to([P, M, 2, DQ])

        @block.sync
        def _(sp):
            def load(i):
                r = slice(i * P, (i + 1) * P)
                if i >= 2:
                    sp.wait_ge(s["q_lo"], i - 1)
                    sp.wait_ge(s["k_lo"], i - 1)
                sp.dma_start(qk_in[:, i % 2, 0], io["q_s"][r, :]).then_inc(s["qk_load"][i % 2], 16)
                sp.dma_start(qk_in[:, i % 2, 1], io["k_p"][r, :]).then_inc(s["qk_load"][i % 2], 16)

            load(0)
            sp.dma_start(mask[:, :], io["causal"]).then_inc(s["mask_load"], 16)
            load(1)
            for q in range(4):
                sp.dma_start(V[:, 4 * q:4 * q + 4, :], io["v_p"].rearrange("(b p) n -> p b n", p=P)[:, 4 * q:4 * q + 4, :])\
                  .then_inc(s[f"v_load{q}"], 16)
            for i in range(NP):
                if i + 2 < NP:
                    load(i + 2)
                sp.wait_ge(s["out"], i + 1)
                sp.dma_start(io["o_s"][i * P:(i + 1) * P, :], ob[:, i % 2]).then_inc(s["store"][i % 2], 16)
            for p in range(2):
                sp.wait_ge(s["store"][p], 16 * NP // 2)

        @block.gpsimd
        def _(pool):
            pool.memset(zero[:, :], 0.0).then_inc(s["zero"], 1)
            for i in range(NP):
                pool.wait_ge(s["k_hi"], i + 1)
                if i >= 1:
                    pool.wait_ge(s["prep_ps"], 6 * i)
                pool.tensor_tensor(k_hl[:, :, 1], qk_in[:, i % 2, 1].rearrange("p (m d) -> p m d", d=DQ),
                                   f32(k_hl[:, :, 0]), ALU.subtract).then_inc(s["k_lo"], 1)
                pool.wait_ge(s["q_hi"], i + 1)
                pool.tensor_tensor(q_hl[:, 1], twice(qk_in[:, i % 2, 0]),
                                   f32(q_hl[:, 0]), ALU.subtract).then_inc(s["q_lo"], 1)

        @block.scalar
        def _(act):
            def split_hi(i):
                act.wait_ge(s["qk_load"][i % 2], 32 * (i // 2 + 1))
                if i >= 1:
                    act.wait_ge(s["prep_ps"], 6 * i)
                act.activation(k_hl[:, :, 0], qk_in[:, i % 2, 1].rearrange("p (m d) -> p m d", d=DQ), ACT.Copy).then_inc(s["k_hi"], 1)
                act.activation(q_hl[:, 0], twice(qk_in[:, i % 2, 0]), ACT.Copy).then_inc(s["q_hi"], 1)

            def exps(n):
                i, h = tile_head[n]
                act.wait_ge(s["neg_max"], n + 1)
                for m in range(2):
                    row = sc[m][:, n % 2, 0:(i + 1) * P]
                    act.activation(row, row, ACT.Exp, bias=nmx[:, n % 2, m:m + 1],
                                   accum_out=ls[:, i % 2, m, h:h + 1]).then_inc(s["exp"], 1)

            def weights_out(n):
                i, h = tile_head[n]
                for c in range(len(chunks[i])):
                    g = first_wt[i, h] + c
                    act.wait_ge(s["wT_ps"], g + 1)
                    if g >= 2:
                        act.wait_ge(s["out_ps"], g - 1)
                    w = chunks[i][c][1]
                    act.activation(WT[:, g % 2, 0:w // P, :], tps[g % 2][:, 0:w // P, :], ACT.Copy).then_inc(s["wT"], 1)

            split_hi(0)
            for n in range(n_heads + 1):
                if n < n_heads:
                    i, h = tile_head[n]
                    exps(n)
                    if h == 1 and i + 1 < NP:
                        split_hi(i + 1)
                if n >= 1:
                    weights_out(n - 1)

        @block.vector
        def _(dve):
            def prep_out(i):
                if i >= 2:
                    dve.wait_ge(s["scores"], first_sc[i - 1, 0])
                for n in range(6):
                    dve.wait_ge(s["prep_ps"], 6 * i + n + 1)
                    src = sps[n % 4][:, :].rearrange("p (m t) -> p m t", m=4)
                    dst = KT[:, 4 * n:4 * n + 4, i * P:(i + 1) * P] if n < 2 else QS[i % 2][(n - 2) // 2][:, 4 * (n % 2):4 * (n % 2) + 4, :]
                    dve.tensor_copy(dst, src).then_inc(s["prep_out"], 1)

            def rows(n):
                i, h = tile_head[n]
                last = len(chunks[i]) - 1
                if n >= 2:
                    dve.wait_ge(s["wT_ps"], first_wt[i, h] - (len(chunks[tile_head[n - 1][0]])))
                for c, (c0, w) in enumerate(chunks[i]):
                    for m in range(2):
                        k = first_sc[i, h] + 2 * c + m
                        dve.wait_ge(s["scores"], k + 1)
                        add = mask[:, 4 * P - w:4 * P] if c == last else zero[:, 0:w]
                        red = dve.tensor_tensor_reduce(sc[m][:, n % 2, c0:c0 + w], sps[k % 4][:, 0:w], add, SCALE, -3e38,
                                                       ALU.add, ALU.max, mx[:, n % 2, m, c:c + 1]).then_inc(s["row_max"], 1)
                dve.wait_ge(s["row_max"], first_sc[i, h] + 2 * len(chunks[i]))
                if n >= 2:
                    dve.wait_ge(s["exp"], 2 * n - 2)
                dve.tensor_reduce(nmx[:, n % 2, :], mx[:, n % 2, :, 0:last + 1], AX.X, ALU.max, negate=True).then_inc(s["neg_max"], 1)

            def combine(n):
                i, h = tile_head[n]
                dve.wait_ge(s["exp"], 2 * n + 2)
                dve.reciprocal(rl[:, 0, h:h + 1], ls[:, i % 2, 1, h:h + 1]).then_inc(s["recip"], 1)
                dve.wait_ge(s["recip"], n + 1)
                dve.scalar_tensor_tensor(out=coef[:, n % 2:n % 2 + 1], in0=ls[:, i % 2, 0, h:h + 1], scalar=nlam[:, 0:1],
                                         in1=rl[:, 0, h:h + 1], op0=ALU.mult, op1=ALU.mult).then_inc(s["coef"], 1)
                dve.wait_ge(s["coef"], n + 1)
                w = (i + 1) * P
                dve.scalar_tensor_tensor(out=sc[0][:, n % 2, 0:w], in0=sc[1][:, n % 2, 0:w], scalar=coef[:, n % 2:n % 2 + 1],
                                         in1=sc[0][:, n % 2, 0:w], op0=ALU.mult, op1=ALU.add).then_inc(s["weights"], 1)

            def out_rows(i):
                dve.reciprocal(r0[:, :], ls[:, i % 2, 0, :]).then_inc(s["r0"], 1)
                dve.wait_ge(s["r0"], i + 1)
                dve.wait_ge(s["out_ps"], first_wt[i, H - 1] + len(chunks[i]))
                if i >= 2:
                    dve.wait_ge(s["store"][i % 2], 16 * (i // 2))
                dve.tensor_tensor(ob[:, i % 2].rearrange("p (h v) -> p h v", h=H), ops[i % 2][:, :, :],
                                  r0[:, :, None].broadcast_to([P, H, DV]), ALU.mult).then_inc(s["out"], 1)

            dve.wait_ge(s["zero"], 1)
            dve.wait_ge(s["mask_load"], 16)
            prep_out(0)
            for n in range(n_heads + 2):
                if n < n_heads:
                    i, h = tile_head[n]
                    if h == 0 and i >= 1:
                        prep_out(i)
                    rows(n)
                if 1 <= n <= n_heads:
                    combine(n - 1)
                if n >= 2 and tile_head[n - 2][1] == H - 1:
                    out_rows(tile_head[n - 2][0])

        @block.tensor
        def _(pe):
            def prep(i):
                pe.wait_ge(s["k_lo"], i + 1)
                pe.wait_ge(s["q_lo"], i + 1)
                if i >= 1:
                    pe.wait_ge(s["row_max"], first_sc[i, 0])
                for n in range(6):
                    if n >= 4:
                        pe.wait_ge(s["prep_out"], 6 * i + n - 3)
                    for a in range(4):
                        m = 4 * (n % 2) + a
                        if n < 2:
                            src = f32(k_hl[:, m, :, :]).rearrange("p a b -> p (a b)")
                        else:
                            src = f32(q_hl[:, (n - 2) // 2, m]).rearrange("p a b -> p (a b)")
                        mm = pe.transpose(sps[n % 4][:, a * P:(a + 1) * P], src, ident[:, :])
                    mm.then_inc(s["prep_ps"], 1)

            def scores(n):
                i, h = tile_head[n]
                for c, (c0, w) in enumerate(chunks[i]):
                    for m in range(2):
                        k = first_sc[i, h] + 2 * c + m
                        if k >= 4:
                            pe.wait_ge(s["row_max"], k - 3)
                        if c == 0 and m == 0:
                            pe.wait_ge(s["prep_out"], 6 * i + 6)
                        for part in range(2):
                            mm = pe.matmul(sps[k % 4][:, 0:w], QS[i % 2][part][:, 2 * h + m, :], KT[:, 2 * h + m, c0:c0 + w],
                                           start=(part == 0), stop=(part == 1))
                        mm.then_inc(s["scores"], 1)

            def weight_columns(n, c):
                i, h = tile_head[n]
                g = first_wt[i, h] + c
                if c == 0:
                    pe.wait_ge(s["weights"], n + 1)
                if g >= 2:
                    pe.wait_ge(s["wT"], g - 1)
                c0, w = chunks[i][c]
                for b in range(w // P):
                    mm = pe.transpose(tps[g % 2][:, b, :], sc[0][:, n % 2, c0 + b * P:c0 + (b + 1) * P], ident[:, :])
                mm.then_inc(s["wT_ps"], 1)

            def values(n, c):
                i, h = tile_head[n]
                g = first_wt[i, h] + c
                c0, w = chunks[i][c]
                pe.wait_ge(s["wT"], g + 1)
                pe.wait_ge(s[f"v_load{c}"], 16)
                if h == 0 and c == 0 and i >= 2:
                    pe.wait_ge(s["out"], i - 1)
                for b in range(w // P):
                    kb = c0 // P + b
                    mm = pe.matmul(ops[i % 2][:, h, :], WT[:, g % 2, b, :], V[:, kb, h * DV:(h + 1) * DV],
                                   start=(kb == 0), stop=(kb == i))
                mm.then_inc(s["out_ps"], 1)

            prep(0)
            for n in range(n_heads + 1):
                if n < n_heads:
                    if tile_head[n][1] == 0 and n:
                        prep(tile_head[n][0])
                    scores(n)
                if n >= 1:
                    nc_ = len(chunks[tile_head[n - 1][0]])
                    weight_columns(n - 1, 0)
                    for c in range(nc_):
                        if c + 1 < nc_:
                            weight_columns(n - 1, c + 1)
                        values(n - 1, c)


def pass_lambda(nc, io, keep):
    ident, nlam = keep[0], keep[2]
    with ExitStack() as ctx:
        lam = ctx.enter_context(nc.sbuf_tensor("l_lam", [P, 4, DQ], F32))
        prod = ctx.enter_context(nc.sbuf_tensor("l_prod", [P, 2, DQ], F32))
        red = ctx.enter_context(nc.sbuf_tensor("l_sum", [P, 4], F32))
        load, step, idr = (ctx.enter_context(nc.semaphore("l_" + n)) for n in ("load", "step", "ident"))
        block = open_block(nc, ctx, (load, step, idr))

        @block.gpsimd
        def _(pool):
            make_identity(pool, ident, idr)
            pool.wait_ge(idr, 2)

        @block.sync
        def _(sp):
            for n, name in enumerate(("lambda_q1", "lambda_q2", "lambda_k1", "lambda_k2")):
                sp.dma_start(lam[:, n], io[name].partition_broadcast(P).rearrange("p a b -> p (a b)")).then_inc(load, 16)

        @block.vector
        def _(dve):
            dve.wait_ge(load, 64)
            dve.tensor_tensor(prod[:, :], lam[:, 0:2], lam[:, 2:4], ALU.mult).then_inc(step, 1)
            dve.wait_ge(step, 1)
            dve.tensor_reduce(red[:, 0:2], prod[:, :, :], AX.X, ALU.add).then_inc(step, 1)
            dve.wait_ge(step, 3)
            dve.tensor_tensor(red[:, 2:3], red[:, 1:2], red[:, 0:1], ALU.subtract).then_inc(step, 1)
            dve.wait_ge(step, 4)
            dve.tensor_scalar(nlam[:, 0:1], red[:, 2:3], LAM_INIT, None, ALU.subtract).then_inc(step, 1)
            dve.wait_ge(step, 5)

        @block.scalar
        def _(act):
            act.wait_ge(step, 2)
            act.activation(red[:, 0:2], red[:, 0:2], ACT.Exp).then_inc(step, 1)


def pass_sample_attention(nc, io, keep):
    with ExitStack() as ctx:
        def sb(name, shape, dt=F32):
            return ctx.enter_context(nc.sbuf_tensor("s_" + name, shape, dt))

        def sem(name):
            return ctx.enter_context(nc.semaphore("s_" + name))

        def ps(name, shape):
            return ctx.enter_context(nc.psum_tensor("s_" + name, shape, F32))

        ident, nlam = keep[0], keep[2]
        NK = PAST + DEC_T
        pages = sb("pages", [1, DEC_B * NPG], I32)
        kc = sb("kc", [P, 2, NPG, GW])
        vc = sb("vc", [P, 2, NPG, GW])
        v_new = sb("v_new", [DEC_T, DEC_B, GW])
        qk_new = sb("qk_new", [NS, 2, GW])
        Q = sb("Q", [P, DEC_B, H, 32])
        K_new = sb("K_new", [P, H, NS])
        KT = sb("KT", [P, 2, H, PAST])
        sc = sb("sc", [P, 2, NK])
        PT = sb("PT", [P, 2, NPG + 1, P])
        mask = sb("mask", [P, DEC_T])
        zero = sb("zero", [P, PAST])
        is_map = sb("is_map", [P, 2])
        sign = sb("sign", [P, 1])
        mx = sb("mx", [P, 2, 2])
        nmx = sb("nmx", [P, 2])
        l = sb("l", [P, 2])
        rl = sb("rl", [P, 2])
        coef = sb("coef", [P, 2])
        part = sb("part", [P, 2, DV])
        maps = sb("maps", [NS, 2, H, DV])
        rows = sb("rows", [NS, H * DV])
        tps = [ps(f"tps{n}", [P, 4, P]) for n in range(2)]
        sps = [ps(f"sps{n}", [P, PAST]) for n in range(2)]
        nps = ps("nps", [P, 2, 256])
        pps = [ps(f"pps{n}", [P, 4, P]) for n in range(2)]
        ops = ps("ops", [P, 2, 256])
        s = {n: sem(n) for n in ("pages", "new", "consts", "zero", "sign", "new_ps", "Q", "K_new", "kT_ps", "kT", "scores", "row_max",
                                 "neg_max", "exp", "recip", "coef", "pT_ps", "pT", "outs", "part", "maps", "sum", "store")}
        s["kc"] = [sem(f"kc{p}") for p in range(2)]
        s["vc"] = [sem(f"vc{p}") for p in range(2)]
        s["part_store"] = [sem(f"part_store{p}") for p in range(2)]
        block = open_block(nc, ctx, s.values())

        @block.sync
        def _(sp):
            sp.dma_start(pages[:, :], io["page_table"]).then_inc(s["pages"], 16)
            sp.dma_start(qk_new[:, 0], io["q_s"][NP * P:NP * P + NS, :]).then_inc(s["new"], 16)
            sp.dma_start(qk_new[:, 1], io["k_s"]).then_inc(s["new"], 16)
            sp.dma_start(v_new[:, :, :], io["v_s"].rearrange("(b t) n -> t b n", t=DEC_T)).then_inc(s["new"], 16)
            sp.dma_start(mask[:, :], io["new_mask"]).then_inc(s["consts"], 16)
            sp.dma_start(is_map[:, :], io["is_map"]).then_inc(s["consts"], 16)
            sp.wait_ge(s["pages"], 16)

            def store_part(j):
                sp.wait_ge(s["part"], j + 1)
                sp.dma_start(io["part_s"][j], part[:, j % 2]).then_inc(s["part_store"][j % 2], 16)

            for j in range(DEC_B):
                if j >= 2:
                    store_part(j - 2)
                    sp.wait_ge(s["kT_ps"], 4 * (j - 1))
                    sp.wait_ge(s["outs"], j - 1)
                for g in range(NPG):
                    page = sp.value_load(pages[0:1, j * NPG + g:j * NPG + g + 1], min_val=0, max_val=N_POOL - 1)
                    sp.dma_start(kc[:, j % 2, g], io["cache_k"][bass.ds(page * PAGE, PAGE), :]).then_inc(s["kc"][j % 2], 16)
                    sp.dma_start(vc[:, j % 2, g], io["cache_v"][bass.ds(page * PAGE, PAGE), :]).then_inc(s["vc"][j % 2], 16)
            store_part(DEC_B - 2)
            store_part(DEC_B - 1)
            for p in range(2):
                sp.wait_ge(s["part_store"][p], 16 * DEC_B // 2)
            for j in range(DEC_B):
                for m in range(2):
                    src = io["part_s"][j].rearrange("(h x) v -> x h v", h=H)[m * DEC_T:(m + 1) * DEC_T]
                    sp.dma_start(maps[j * DEC_T:(j + 1) * DEC_T, m], src).then_inc(s["maps"], 16)
            sp.wait_ge(s["sum"], 1)
            sp.dma_start(io["o_s"][NP * P:NP * P + NS, :], rows[:, :]).then_inc(s["store"], 16)
            sp.wait_ge(s["store"], 16)

        @block.gpsimd
        def _(pool):
            pool.memset(Q[:, :, :, :], 0.0).then_inc(s["zero"], 1)
            pool.memset(zero[:, :], 0.0).then_inc(s["zero"], 1)
            pool.wait_ge(s["zero"], 2)

        @block.scalar
        def _(act):
            def keys_out(j):
                for g in range(NPG):
                    act.wait_ge(s["kT_ps"], 4 * j + g + 1)
                    if j >= 2:
                        act.wait_ge(s["scores"], 2 * (j - 1))
                    act.activation(KT[:, j % 2, :, g * PAGE:(g + 1) * PAGE], tps[g % 2][:, :, :], ACT.Copy).then_inc(s["kT"], 1)

            keys_out(0)
            for j in range(DEC_B):
                if j + 1 < DEC_B:
                    keys_out(j + 1)
                act.wait_ge(s["neg_max"], j + 1)
                act.activation(sc[:, j % 2, :], sc[:, j % 2, :], ACT.Exp, bias=nmx[:, j % 2:j % 2 + 1],
                               accum_out=l[:, j % 2:j % 2 + 1]).then_inc(s["exp"], 1)

        @block.vector
        def _(dve):
            dve.wait_ge(s["consts"], 32)
            dve.wait_ge(s["zero"], 2)
            dve.scalar_tensor_tensor(out=sign[:, :], in0=is_map[:, 1:2], scalar=nlam[:, 0:1], in1=is_map[:, 0:1],
                                     op0=ALU.mult, op1=ALU.add).then_inc(s["sign"], 1)
            dve.wait_ge(s["new_ps"], 1)
            for m in range(2):
                r = slice(m * DQ, (m + 1) * DQ)
                for h in range(H):
                    last = dve.tensor_copy(Q[r, :, h, m * DEC_T:(m + 1) * DEC_T],
                                           pps[0][r, h, 0:NS].rearrange("p (b t) -> p b t", b=DEC_B))
            last.then_inc(s["Q"], 1)
            dve.wait_ge(s["new_ps"], 2)
            dve.tensor_copy(K_new[:, :, :], pps[1][:, :, 0:NS]).then_inc(s["K_new"], 1)
            dve.wait_ge(s["sign"], 1)

            def weights_out(j):
                for a in range(2):
                    dve.wait_ge(s["pT_ps"], 2 * j + a + 1)
                    if j >= 2:
                        dve.wait_ge(s["outs"], j - 1)
                    if a == 0:
                        dve.tensor_copy(PT[:, j % 2, 0:NPG], pps[0][:, :, :]).then_inc(s["pT"], 1)
                    else:
                        dve.tensor_copy(PT[0:DEC_T, j % 2, NPG], pps[1][0:DEC_T, 0, :]).then_inc(s["pT"], 1)

            def out_part(j):
                b = j % 2
                dve.wait_ge(s["exp"], j + 1)
                dve.reciprocal(rl[:, b:b + 1], l[:, b:b + 1]).then_inc(s["recip"], 1)
                dve.wait_ge(s["recip"], j + 1)
                dve.tensor_tensor(coef[:, b:b + 1], rl[:, b:b + 1], sign[:, :], ALU.mult).then_inc(s["coef"], 1)
                dve.wait_ge(s["coef"], j + 1)
                dve.wait_ge(s["outs"], j + 1)
                if j >= 2:
                    dve.wait_ge(s["part_store"][b], 16 * (j // 2))
                dve.tensor_scalar(part[:, b], ops[:, b, 0:DV], coef[:, b:b + 1], None, ALU.mult).then_inc(s["part"], 1)

            for j in range(DEC_B + 1):
                if j < DEC_B:
                    b = j % 2
                    dve.wait_ge(s["scores"], 2 * j + 1)
                    if j >= 2:
                        dve.wait_ge(s["pT_ps"], 2 * j - 2)
                    dve.tensor_tensor_reduce(sc[:, b, 0:PAST], sps[b][:, :], zero[:, :], SCALE, -3e38, ALU.add, ALU.max,
                                             mx[:, b, 0:1]).then_inc(s["row_max"], 1)
                    dve.wait_ge(s["scores"], 2 * j + 2)
                    dve.tensor_tensor_reduce(sc[:, b, PAST:NK], nps[:, b, 0:DEC_T], mask[:, :], SCALE, -3e38, ALU.add, ALU.max,
                                             mx[:, b, 1:2]).then_inc(s["row_max"], 1)
                    dve.wait_ge(s["row_max"], 2 * j + 2)
                    if j >= 2:
                        dve.wait_ge(s["exp"], j - 1)
                    dve.tensor_reduce(nmx[:, b:b + 1], mx[:, b, :], AX.X, ALU.max, negate=True).then_inc(s["neg_max"], 1)
                if j >= 1:
                    weights_out(j - 1)
                    out_part(j - 1)
            dve.wait_ge(s["maps"], 16 * 2 * DEC_B)
            dve.tensor_tensor(rows[:, :].rearrange("p (h v) -> p h v", h=H), maps[:, 0], maps[:, 1], ALU.add).then_inc(s["sum"], 1)

        @block.tensor
        def _(pe):
            pe.wait_ge(s["new"], 48)
            for n in range(2):
                for h in range(H):
                    mm = pe.transpose(pps[n][:, h, 0:NS], qk_new[:, n, h * P:(h + 1) * P], ident[0:NS, 0:NS])
                mm.then_inc(s["new_ps"], 1)

            def key_columns(j):
                pe.wait_ge(s["kc"][j % 2], 64 * (j // 2 + 1))
                for g in range(NPG):
                    n = 4 * j + g
                    if n >= 2:
                        pe.wait_ge(s["kT"], n - 1)
                    for h in range(H):
                        mm = pe.transpose(tps[g % 2][:, h, :], kc[:, j % 2, g, h * P:(h + 1) * P], ident[:, :])
                    mm.then_inc(s["kT_ps"], 1)

            def scores(j):
                b = j % 2
                pe.wait_ge(s["kT"], 4 * j + 4)
                if j >= 2:
                    pe.wait_ge(s["row_max"], 2 * j - 2)
                for h in range(H):
                    mm = pe.matmul(sps[b][32 * h:32 * h + 32, :], Q[:, j, h, :], KT[:, b, h, :], start=True, stop=True)
                mm.then_inc(s["scores"], 1)
                if j >= 1:
                    pe.wait_ge(s["row_max"], 2 * j)
                for h in range(H):
                    mm = pe.matmul(nps[32 * h:32 * h + 32, b, 0:DEC_T], Q[:, j, h, :], K_new[:, h, j * DEC_T:(j + 1) * DEC_T],
                                   start=True, stop=True)
                mm.then_inc(s["scores"], 1)

            def weight_columns(j):
                pe.wait_ge(s["exp"], j + 1)
                if j >= 1:
                    pe.wait_ge(s["pT"], 2 * j)
                for g in range(NPG):
                    mm = pe.transpose(pps[0][:, g, :], sc[:, j % 2, g * PAGE:(g + 1) * PAGE], ident[:, :])
                mm.then_inc(s["pT_ps"], 1)
                pe.transpose(pps[1][0:DEC_T, 0, :], sc[:, j % 2, PAST:NK], ident[:, :]).then_inc(s["pT_ps"], 1)

            def values(j):
                b = j % 2
                pe.wait_ge(s["pT"], 2 * j + 2)
                pe.wait_ge(s["vc"][b], 64 * (j // 2 + 1))
                if j >= 1:
                    pe.wait_ge(s["part"], j)
                for h in range(H):
                    out = ops[32 * h:32 * h + 32, b, 0:DV]
                    for g in range(NPG):
                        pe.matmul(out, PT[:, b, g, 32 * h:32 * h + 32], vc[:, b, g, h * DV:(h + 1) * DV], start=(g == 0), stop=False)
                    mm = pe.matmul(out, PT[0:DEC_T, b, NPG, 32 * h:32 * h + 32], v_new[:, j, h * DV:(h + 1) * DV],
                                   start=False, stop=True)
                mm.then_inc(s["outs"], 1)

            key_columns(0)
            pe.wait_ge(s["Q"], 1)
            pe.wait_ge(s["K_new"], 1)
            for j in range(DEC_B + 1):
                if j < DEC_B:
                    scores(j)
                if j >= 1:
                    weight_columns(j - 1)
                    values(j - 1)
                if j + 1 < DEC_B:
                    key_columns(j + 1)


def pass_sample_hgrn(nc, io, keep):
    with ExitStack() as ctx:
        def sb(name, shape, dt=F32):
            return ctx.enter_context(nc.sbuf_tensor("r_" + name, shape, dt))

        def sem(name):
            return ctx.enter_context(nc.semaphore("r_" + name))

        def ps(name, shape):
            return ctx.enter_context(nc.psum_tensor("r_" + name, shape, F32))

        ident = keep[0]
        levels = tuple((n, w) for n, w in enumerate(BLOCKS) if w <= DEC_T)
        n0 = levels[0][0]
        qT, kT, lfT, bT = (sb(n, [P, GW]) for n in ("qT", "kT", "lfT", "bT"))
        v_tok, gate = sb("v_tok", [P, GW]), sb("gate", [P, GW])
        go = sb("go", [P, P])
        lv = sb("lv", [P, SLOTS - n0, GW])
        runs = sb("runs", [P, DEC_B])
        own = sb("own", [P, DEC_B, P])
        S0 = sb("S0", [P, DEC_B, H, DV])
        S1 = sb("S1", [P, DEC_B, H, DV])
        qe = sb("qe", [P, 2, DEC_B, P])
        v_own = sb("v_own", [P, 2, DEC_B, DV])
        ebc = sb("ebc", [P, H, DEC_B])
        mask = sb("mask", [P, NL, P])
        masked = sb("masked", [P, 3, P])
        att = sb("att", [P, H, P])
        kd_tok = sb("kd_tok", [P, GW])
        rows = sb("rows", [P, GW])
        sq = sb("sq", [P, GW])
        oss = sb("oss", [P, 3, H])
        ng = sb("ng", [P, DV])
        eps = sb("eps", [P, 1])
        lps = ps("lps", [P, 4, P])
        tps = ps("tps", [P, 4, P])
        ops = ps("ops", [P, H, DV])
        ups = [[ps(f"ups{a}{b}", [P, 4, DV]) for b in range(2)] for a in range(2)]
        s = {n: sem(n) for n in ("load", "state_load", "eps", "cumsum", "diff", "decay", "ebc", "operands", "levels", "masked", "att",
                                 "kdT_ps", "kd_tok", "qe", "v_own", "av", "gain_ps", "scaled", "state", "o_sq", "o_ss", "o_root",
                                 "o_rs", "o_norm", "o_g", "o_out", "store")}
        block = open_block(nc, ctx, s.values())

        @block.sync
        def _(sp):
            loads = ((lfT[:, :], io["hl_s"]), (go[:, :], io["run_go"]), (qT[:, :], io["hq_s"]), (kT[:, :], io["hk_s"]),
                     (v_tok[:, :], io["hv_s"]), (gate[:, :], io["hg_s"]), (mask[:, :, :], io["level_mask"]),
                     (runs[:, :], io["runs"]), (own[:, :, :], io["own"]),
                     (ng[:, :], io["hgrn_norm_g"].partition_broadcast(P).rearrange("p a b -> p (a b)")))
            for dst, src in loads:
                sp.dma_start(dst, src).then_inc(s["load"], 16)
            sp.dma_start(S0[:, :, :, :].rearrange("p b h v -> p (b h) v"), io["state"].rearrange("b h d v -> d (b h) v")).then_inc(s["state_load"], 16)
            sp.wait_ge(s["state"], H)
            sp.dma_start(io["s_s"].rearrange("b h d v -> d (b h) v"), S1[:, :, :, :].rearrange("p b h v -> p (b h) v")).then_inc(s["store"], 16)
            sp.wait_ge(s["o_out"], 1)
            sp.dma_start(io["mr_s"][NP * P:NP * P + NS, :], rows[0:NS, :]).then_inc(s["store"], 16)
            sp.wait_ge(s["store"], 32)

        @block.gpsimd
        def _(pool):
            pool.wait_ge(s["decay"], 1)
            decay_products(pool, lv, qT[:, :], kT[:, :], levels, n0).then_inc(s["operands"], 1)
            for h in range(H):
                if h >= 2:
                    pool.wait_ge(s["gain_ps"], h - 1)
                pool.tensor_tensor(v_own[:, h % 2], v_tok[:, None, h * DV:(h + 1) * DV].broadcast_to([P, DEC_B, DV]),
                                   runs[:, :, None].broadcast_to([P, DEC_B, DV]), ALU.mult).then_inc(s["v_own"], 1)
            pool.wait_ge(s["o_norm"], 1)
            r3 = rows[:, :].rearrange("p (h v) -> p h v", h=H)
            pool.tensor_tensor(r3, r3, ng[:, None, :].broadcast_to([P, H, DV]), ALU.mult).then_inc(s["o_g"], 1)
            pool.wait_ge(s["o_g"], 1)
            pool.tensor_tensor(rows[:, :], rows[:, :], gate[:, :], ALU.mult).then_inc(s["o_out"], 1)

        @block.scalar
        def _(act):
            act.wait_ge(s["diff"], 1)
            act.activation(lv[:, :, :], lv[:, :, :], ACT.Exp).then_inc(s["decay"], 1)
            act.activation(ebc[:, :, :], bT[:, :].rearrange("p (h b t) -> p h b t", h=H, t=DEC_T)[:, :, 0:DEC_B, DEC_T - 1],
                           ACT.Exp).then_inc(s["ebc"], 1)
            act.wait_ge(s["kdT_ps"], 1)
            act.activation(kd_tok[:, :], tps[:, :, :].rearrange("p h d -> p (h d)"), ACT.Copy).then_inc(s["kd_tok"], 1)
            act.wait_ge(s["av"], H)
            act.wait_ge(s["eps"], 1)
            act.activation(sq[:, :], ops[:, :, :].rearrange("p h v -> p (h v)"), ACT.Square).then_inc(s["o_sq"], 1)
            act.wait_ge(s["o_ss"], 1)
            act.activation(oss[:, 1], oss[:, 0], ACT.Sqrt, bias=eps[:, 0:1], scale=1.0 / DV).then_inc(s["o_root"], 1)

        @block.vector
        def _(dve):
            dve.memset(eps[:, :], EPS).then_inc(s["eps"], 1)
            dve.wait_ge(s["load"], 160)
            for h in range(H):
                cols = slice(h * P, (h + 1) * P)
                last = dve.tensor_tensor_scan(bT[:, cols], go[:, :], lfT[:, cols], 0.0, ALU.mult, ALU.add)
            last.then_inc(s["cumsum"], 1)
            dve.wait_ge(s["cumsum"], 1)
            decay_differences(dve, bT[:, :], lv, levels, DEC_T, n0).then_inc(s["diff"], 1)
            dve.wait_ge(s["operands"], 1)
            for h in range(H):
                dve.wait_ge(s["levels"], h + 1)
                dve.wait_ge(s["att"], h)
                dve.tensor_tensor(masked[:, :, :], lps[:, 0:3, :], mask[:, n0:, :], ALU.mult).then_inc(s["masked"], 1)
                dve.wait_ge(s["masked"], h + 1)
                dve.tensor_reduce(att[:, h], masked[:, :, :].rearrange("p l t -> p t l"), AX.X, ALU.add).then_inc(s["att"], 1)
                if h >= 2:
                    dve.wait_ge(s["av"], h - 1)
                dve.tensor_tensor(qe[:, h % 2], lv[:, LEAF_QE - n0, None, h * P:(h + 1) * P].broadcast_to([P, DEC_B, P]), own[:, :, :],
                                  ALU.mult).then_inc(s["qe"], 1)
            dve.wait_ge(s["state_load"], 16)
            dve.wait_ge(s["ebc"], 1)
            for h in range(H):
                dve.tensor_tensor(S1[:, :, h], S0[:, :, h], ebc[:, h, :, None].broadcast_to([P, DEC_B, DV]), ALU.mult).then_inc(s["scaled"], 1)
                dve.wait_ge(s["scaled"], h + 1)
                dve.wait_ge(s["gain_ps"], h + 1)
                for b in range(2):
                    last = dve.tensor_tensor(S1[:, 4 * b:4 * b + 4, h], S1[:, 4 * b:4 * b + 4, h], ups[h % 2][b][:, :, :], ALU.add)
                last.then_inc(s["state"], 1)
            r3 = rows[:, :].rearrange("p (h v) -> p h v", h=H)
            dve.wait_ge(s["o_sq"], 1)
            dve.tensor_reduce(oss[:, 0], sq[:, :].rearrange("p (h v) -> p h v", h=H), AX.X, ALU.add).then_inc(s["o_ss"], 1)
            dve.wait_ge(s["o_root"], 1)
            dve.reciprocal(oss[:, 2], oss[:, 1]).then_inc(s["o_rs"], 1)
            dve.wait_ge(s["o_rs"], 1)
            dve.tensor_tensor(r3, ops[:, :, :], oss[:, 2, :, None].broadcast_to([P, H, DV]), ALU.mult).then_inc(s["o_norm"], 1)

        @block.tensor
        def _(pe):
            pe.wait_ge(s["operands"], 1)
            for h in range(H):
                mm = pe.transpose(tps[:, h, :], lv[:, LEAF_KD - n0, h * P:(h + 1) * P], ident[:, :])
            mm.then_inc(s["kdT_ps"], 1)

            def products(h):
                c = slice(h * P, (h + 1) * P)
                if h >= 1:
                    pe.wait_ge(s["masked"], h)
                for a, (n, _) in enumerate(levels):
                    pe.matmul(lps[:, a, :], lv[:, n - n0, c], lv[:, n - n0, c], start=True, stop=True)
                pe.matmul(lps[:, 2, :], lv[:, LEAF_K - n0, c], lv[:, LEAF_Q - n0, c], start=True, stop=True).then_inc(s["levels"], 1)

            products(0)
            for h in range(H):
                if h + 1 < H:
                    products(h + 1)
                pe.wait_ge(s["att"], h + 1)
                pe.wait_ge(s["qe"], h + 1)
                pe.wait_ge(s["state_load"], 16)
                pe.matmul(ops[:, h, :], att[:, h, :], v_tok[:, h * DV:(h + 1) * DV], start=True, stop=False)
                for b in range(DEC_B):
                    mm = pe.matmul(ops[:, h, :], qe[:, h % 2, b, :], S0[:, b, h, :], start=False, stop=(b == DEC_B - 1))
                mm.then_inc(s["av"], 1)
            pe.wait_ge(s["kd_tok"], 1)
            for h in range(H):
                pe.wait_ge(s["v_own"], h + 1)
                if h >= 2:
                    pe.wait_ge(s["state"], h - 1)
                for b in range(2):
                    mm = pe.matmul(ups[h % 2][b][:, :, :].rearrange("p b v -> p (b v)"), kd_tok[:, h * P:(h + 1) * P],
                                   v_own[:, h % 2, 4 * b:4 * b + 4, :].rearrange("p b v -> p (b v)"), start=True, stop=True)
                mm.then_inc(s["gain_ps"], 1)


def pass_output(nc, io, keep):
    with ExitStack() as ctx:
        def sb(name, shape, dt=F32):
            return ctx.enter_context(nc.sbuf_tensor("y_" + name, shape, dt))

        def sem(name):
            return ctx.enter_context(nc.semaphore("y_" + name))

        def ps(name, shape):
            return ctx.enter_context(nc.psum_tensor("y_" + name, shape, F32))

        ident = keep[0]
        w_hi, w_lo = sb("w_hi", [P, KD, D], F32R), sb("w_lo", [P, KD, D], F32R)
        stage = sb("stage", [P, 2, KD, GW])
        o_in, ga, mr = (sb(n, [P, 2, GW]) for n in ("o_in", "ga", "mr"))
        xt = sb("xt", [P, 2, D])
        yt = sb("yt", [P, 2, D])
        sq = sb("sq", [P, GW])
        oss = sb("oss", [P, 3, H])
        ng = sb("ng", [P, 2, DV])
        eps = sb("eps", [P, 1])
        mT_hi = [sb(f"mT_hi{p}", [P, KD, P], F32R) for p in range(2)]
        mT_lo = [sb(f"mT_lo{p}", [P, KD, P], F32R) for p in range(2)]
        yps = [[ps(f"yps{p}{g}", [P, GW]) for g in range(2)] for p in range(2)]
        tps = [ps(f"tps{b}", [P, 4, P]) for b in range(2)]
        s = {n: sem(n) for n in ("w_hi", "w_lo", "ng", "ng_scaled", "eps", "o_sq", "o_ss", "o_root", "o_rs", "o_norm",
                                 "o_g", "gated", "mT_ps", "mT_hi", "mT_lo", "y_ps", "y")}
        for n in ("w_load", "o_load", "ga_load", "mr_load", "x_load", "store"):
            s[n] = [sem(f"{n}{p}") for p in range(2)]
        block = open_block(nc, ctx, s.values())

        def over_tiles(eng, step):
            with eng.Fori(0, NP // 2) as j:
                for p in range(2):
                    step(j * 2 + p, p, j, True)
            step(NP, 0, NP // 2, False)

        @block.sync
        def _(sp):
            def load(i, p, rows=P):
                r = bass.ds(i * P, rows)
                sp.dma_start(o_in[0:rows, p], io["o_s"][r, :]).then_inc(s["o_load"][p], 16)
                sp.dma_start(ga[0:rows, p], io["ga_s"][r, :]).then_inc(s["ga_load"][p], 16)
                sp.dma_start(mr[0:rows, p], io["mr_s"][r, :]).then_inc(s["mr_load"][p], 16)
                sp.dma_start(xt[0:rows, p], io["x"][r, :]).then_inc(s["x_load"][p], 16)

            sp.dma_start(ng[:, 0], io["subln_g"].partition_broadcast(P).rearrange("p a b -> p (a b)")).then_inc(s["ng"], 16)
            load(0, 0)
            for g in range(2):
                sp.dma_start(stage[:, g], io["w_out"].rearrange("(k p) n -> p k n", p=P)[:, :, g * GW:(g + 1) * GW]).then_inc(s["w_load"][g], 16)
            load(1, 1)

            def store(i, p, rows, dst):
                sp.wait_ge(s["y"], 2 * i + 2)
                sp.dma_start(dst, yt[0:rows, p]).then_inc(s["store"][p], 16)

            with sp.Fori(0, NP // 2 - 1) as j:
                for p in range(2):
                    i = j * 2 + p
                    store(i, p, P, io["y_p"][bass.ds(i * P, P), :])
                    load(i + 2, p)
            store(NP - 2, 0, P, io["y_p"][(NP - 2) * P:(NP - 1) * P, :])
            load(NP, 0, NS)
            store(NP - 1, 1, P, io["y_p"][(NP - 1) * P:NP * P, :])
            store(NP, 0, NS, io["y_s"])
            sp.wait_ge(s["store"][0], 16 * (NP // 2 + 1))
            sp.wait_ge(s["store"][1], 16 * (NP // 2))

        @block.gpsimd
        def _(pool):
            def gates(i, p, j):
                o3 = o_in[:, p].rearrange("p (h v) -> p h v", h=H)
                pool.wait_ge(s["o_norm"], i + 1)
                pool.tensor_tensor(o3, o3, ng[:, 1, None, :].broadcast_to([P, H, DV]), ALU.mult).then_inc(s["o_g"], 1)
                pool.wait_ge(s["o_g"], i + 1)
                pool.wait_ge(s["ga_load"][p], j * 16 + 16)
                pool.tensor_tensor(o_in[:, p], o_in[:, p], ga[:, p], ALU.mult).then_inc(s["gated"], 1)

            pool.wait_ge(s["ng_scaled"], 1)
            over_tiles(pool, lambda i, p, j, more: gates(i, p, j))

        @block.scalar
        def _(act):
            def squares(i, p, load):
                act.wait_ge(s["o_load"][p], load)
                act.wait_ge(s["o_ss"], i)
                act.activation(sq[:, :], o_in[:, p], ACT.Square).then_inc(s["o_sq"], 1)
                act.wait_ge(s["o_ss"], i + 1)
                act.activation(oss[:, 1], oss[:, 0], ACT.Sqrt, bias=eps[:, 0:1], scale=1.0 / DV).then_inc(s["o_root"], 1)

            def hi_parts(i, p):
                for b in range(2):
                    act.wait_ge(s["mT_ps"], 2 * i + b + 1)
                    act.activation(mT_hi[p][:, 4 * b:4 * b + 4, :], tps[b][:, :, :], ACT.Copy).then_inc(s["mT_hi"], 1)

            def step(i, p, j, more):
                if more:
                    squares(i + 1, 1 - p, (j + p) * 16 + 16)
                    hi_parts(i + 1, 1 - p)

            act.wait_ge(s["eps"], 1)
            squares(0, 0, 16)
            for g in range(2):
                act.wait_ge(s["w_load"][g], 16)
                act.activation(w_hi[:, :, g * GW:(g + 1) * GW], stage[:, g], ACT.Copy).then_inc(s["w_hi"], 1)
                if g == 0:
                    hi_parts(0, 0)
            over_tiles(act, step)

        @block.vector
        def _(dve):
            def norm(i, p):
                o3 = o_in[:, p].rearrange("p (h v) -> p h v", h=H)
                dve.wait_ge(s["o_sq"], i + 1)
                dve.tensor_reduce(oss[:, 0], sq[:, :].rearrange("p (h v) -> p h v", h=H), AX.X, ALU.add).then_inc(s["o_ss"], 1)
                dve.wait_ge(s["o_root"], i + 1)
                dve.reciprocal(oss[:, 2], oss[:, 1]).then_inc(s["o_rs"], 1)
                dve.wait_ge(s["o_rs"], i + 1)
                dve.tensor_tensor(o3, o3, oss[:, 2, :, None].broadcast_to([P, H, DV]), ALU.mult).then_inc(s["o_norm"], 1)

            def lo_parts(i, p):
                for b in range(2):
                    dve.wait_ge(s["mT_hi"], 2 * i + b + 1)
                    dve.tensor_tensor(mT_lo[p][:, 4 * b:4 * b + 4, :], tps[b][:, :, :],
                                      f32(mT_hi[p][:, 4 * b:4 * b + 4, :]), ALU.subtract).then_inc(s["mT_lo"], 1)

            def step(i, p, j, more):
                if more:
                    norm(i + 1, 1 - p)
                    lo_parts(i + 1, 1 - p)
                dve.wait_ge(s["x_load"][p], j * 16 + 16)
                dve.wait_ge(s["store"][p], j * 16)
                for g in range(2):
                    dve.wait_ge(s["y_ps"], 2 * i + g + 1)
                    dve.tensor_tensor(yt[:, p, g * GW:(g + 1) * GW], yps[p][g][:, :], xt[:, p, g * GW:(g + 1) * GW],
                                      ALU.add).then_inc(s["y"], 1)

            dve.memset(eps[:, :], EPS).then_inc(s["eps"], 1)
            dve.wait_ge(s["ng"], 16)
            dve.tensor_scalar(ng[:, 1], ng[:, 0], 1.0 - LAM_INIT, None, ALU.mult).then_inc(s["ng_scaled"], 1)
            norm(0, 0)
            for g in range(2):
                dve.wait_ge(s["w_hi"], g + 1)
                cols = slice(g * GW, (g + 1) * GW)
                dve.tensor_tensor(w_lo[:, :, cols], stage[:, g], f32(w_hi[:, :, cols]), ALU.subtract).then_inc(s["w_lo"], 1)
                if g == 0:
                    lo_parts(0, 0)
            over_tiles(dve, step)

        @block.tensor
        def _(pe):
            def columns(i, p, load):
                pe.wait_ge(s["mT_lo"], 2 * i)
                pe.wait_ge(s["mr_load"][p], load)
                for b, src in ((0, o_in), (1, mr)):
                    if b == 0:
                        pe.wait_ge(s["gated"], i + 1)
                    for k in range(4):
                        mm = pe.transpose(tps[b][:, k, :], src[:, p, k * P:(k + 1) * P], ident[:, :])
                    mm.then_inc(s["mT_ps"], 1)

            def step(i, p, j, more):
                pe.wait_ge(s["mT_lo"], 2 * i + 2)
                for g in range(2):
                    if p == 0:
                        pe.wait_ge(s["w_lo"], g + 1)
                    if not (isinstance(i, int)) or i >= 2:
                        pe.wait_ge(s["y"], 2 * j * 2)
                    product3(pe, yps[p][g][:, :], mT_hi[p], mT_lo[p], w_hi, w_lo, slice(g * GW, (g + 1) * GW)).then_inc(s["y_ps"], 1)
                    if g == 0 and more:
                        columns(i + 1, 1 - p, (j + p) * 16 + 16)

            columns(0, 0, 16)
            over_tiles(pe, step)


def build_program(nc, io):
    with ExitStack() as ctx:
        ident = ctx.enter_context(nc.sbuf_tensor("ident", [P, P], F32))
        rstd = ctx.enter_context(nc.sbuf_tensor("rstd", [P, 32], F32))
        nlam = ctx.enter_context(nc.sbuf_tensor("nlam", [P, 16], F32))
        keep = (ident, rstd, nlam)
        pass_lambda(nc, io, keep)
        pass_attention_inputs(nc, io, keep)
        pass_hgrn(nc, io, keep)
        pass_sample_hgrn(nc, io, keep)
        pass_attention(nc, io, keep)
        pass_sample_attention(nc, io, keep)
        pass_output(nc, io, keep)


def rotary_table():
    inv = (np.float32(500000.0) ** (-np.arange(0, 2 * HALF, 2, dtype=np.float32) / np.float32(2 * HALF))).astype(np.float32)
    pos = np.concatenate([np.arange(SEQ), PAST + np.tile(np.arange(DEC_T), DEC_B), np.zeros(P - NS)]).astype(np.float32)
    ang = (pos[:, None] * inv[None, :]).astype(np.float32)
    c, n = np.cos(ang), np.sin(ang)
    table = np.concatenate([c, c, -n, n], axis=1).astype(np.float32)
    return np.ascontiguousarray(table.reshape(NT, P, 4 * HALF).transpose(1, 0, 2))


def shape_constants():
    t = np.arange(P)
    level = np.zeros((P, NL, P), np.float32)
    for n, w in enumerate(BLOCKS):
        same = (t[:, None] // w) == (t[None] // w)
        level[:, n] = same & (t[:, None] % w < w // 2) & (t[None] % w >= w // 2)
    level[:, NL - 1] = (t[:, None] // 2 == t[None] // 2) & (t[:, None] <= t[None])
    causal = np.zeros((P, 4 * P), np.float32)
    causal[:, 3 * P:] = np.where(t[None] > t[:, None], NEG, 0.0)
    new_mask = np.where(np.arange(DEC_T)[None] > (t % DEC_T)[:, None], NEG, 0.0).astype(np.float32)
    is_map = np.stack([(t % 32) // DEC_T == 0, (t % 32) // DEC_T == 1], 1).astype(np.float32)
    return {
        "rope": rotary_table(), "level_mask": level, "causal": causal, "new_mask": new_mask, "is_map": is_map,
        "run_go": np.tile((t % DEC_T != 0).astype(np.float32)[None], (P, 1)),
        "runs": (t[:, None] // DEC_T == np.arange(DEC_B)[None]).astype(np.float32),
        "own": np.tile((t[None] // DEC_T == np.arange(DEC_B)[:, None]).astype(np.float32)[None], (P, 1, 1)),
    }


_OUTS = {"y_p": (SEQ, D), "y_s": (NS, D), "k_p": (SEQ, GW), "v_p": (SEQ, GW), "s_p": (H, P, DV),
         "k_s": (NS, GW), "v_s": (NS, GW), "s_s": (DEC_B, H, P, DV)}
_SCRATCH = {"q_s": (NT * P, GW), "ga_s": (NT * P, GW), "o_s": (NT * P, GW), "mr_s": (NT * P, GW), "part_s": (DEC_B, P, DV),
            "hq_s": (P, GW), "hk_s": (P, GW), "hl_s": (P, GW), "hv_s": (P, GW), "hg_s": (P, GW)}


def kernel(**inputs):
    import concourse.bacc as _bacc
    from concourse.bass_utils import run_bass_kernel_spmd as _run

    a = {k: np.asarray(v) for k, v in inputs.items()}
    arrays = {
        "x": np.concatenate([a["x_prompt"].reshape(SEQ, D), a["x_sample"].reshape(NS, D), np.zeros((P - NS, D), np.float32)]),
        "cache_k": a["cache_k"].reshape(N_POOL * PAGE, GW),
        "cache_v": a["cache_v"].reshape(N_POOL * PAGE, GW),
        "state": a["state_hgrn"].reshape(DEC_B, H, P, DV),
        "page_table": a["page_table"].reshape(1, DEC_B * NPG),
        "norm_g": a["norm_g"].reshape(KD, P).T,
        "w_in": a["w_in"].reshape(D, NG * GW),
        "lb": a["hgrn_lb_logits"].reshape(2, H, P).transpose(2, 0, 1),
        "w_out": a["w_out"].reshape(D, D),
    }
    for name in ("q_norm_g", "k_norm_g", "lambda_q1", "lambda_k1", "lambda_q2", "lambda_k2", "subln_g", "hgrn_norm_g"):
        arrays[name] = a[name]
    arrays.update(shape_constants())
    nc = _bacc.Bacc("TRN2", target_bir_lowering=False, num_devices=1)
    io, fed = {}, {}
    for name, v in arrays.items():
        v = np.ascontiguousarray(v)
        fed[f"in_{name}"] = v
        io[name] = nc.dram_tensor(f"in_{name}", v.shape, mybir.dt.from_np(v.dtype), kind="ExternalInput").ap()
    for name, shape in _OUTS.items():
        io[name] = nc.dram_tensor(f"out_{name}", shape, F32, kind="ExternalOutput").ap()
    for name, shape in _SCRATCH.items():
        io[name] = nc.dram_tensor(f"tmp_{name}", shape, F32, kind="Internal").ap()
    build_program(nc, io)
    r = _run(nc, [fed], core_ids=[0]).results[0]
    o = {name: r[f"out_{name}"] for name in _OUTS}
    return (o["y_p"].reshape(1, SEQ, D), o["y_s"].reshape(DEC_B, DEC_T, D),
            o["k_p"].reshape(1, 1, SEQ, H, P), o["v_p"].reshape(1, 1, SEQ, H, DV), o["s_p"].reshape(1, 1, H, P, DV),
            o["k_s"].reshape(1, DEC_B, DEC_T, H, P), o["v_s"].reshape(1, DEC_B, DEC_T, H, DV),
            o["s_s"].reshape(1, DEC_B, H, P, DV))
```

```python
from contextlib import ExitStack

import numpy as np

import concourse.bass as bass
from concourse import mybir

ALU = mybir.AluOpType
ACT = mybir.ActivationFunctionType
AX = mybir.AxisListType
F32 = mybir.dt.float32
F32R = mybir.dt.float32r
BF16 = mybir.dt.bfloat16
I32 = mybir.dt.int32

P = 128
D = 1024
KD = D // P
SEQ, DEC_B, DEC_T = 2048, 8, 8
NS = DEC_B * DEC_T
NP = SEQ // P
NT = NP + 1
GW = 512
NG = 8
H = 4
DQ = 64
DV = 128
HALF = 8
PAST, PAGE = 512, 128
NPG = PAST // PAGE
N_POOL = 40
EPS = 1e-6
LAM_INIT = 0.2
SCALE = DQ ** -0.5


def f32(ap):
    return ap.bitcast(F32)


def handles(sems):
    for x in sems:
        if isinstance(x, (list, tuple)):
            yield from handles(x)
        else:
            yield x


def clear_semaphores(nc, sems):
    nums = sorted(x.num for x in handles(sems))
    while nums:
        n = 1
        while n < len(nums) and nums[n] == nums[0] + n:
            n += 1
        nc.all_engine_barrier(sems_to_clear=range(nums[0], nums[0] + n))
        nums = nums[n:]


def open_block(nc, ctx, sems):
    ctx.callback(clear_semaphores, nc, sems)
    return ctx.enter_context(nc.Block())


def split_weights(eng_kind, eng, n_halves, s, bufs):
    stage, wg, w_hi, w_lo = bufs
    for n in range(n_halves):
        g, b = n // 2, n % 2
        ks = slice(4 * b, 4 * b + 4)
        cols = slice(g * GW, (g + 1) * GW)
        if eng_kind == "act":
            eng.wait_ge(s["w_scaled"], n + 1)
            eng.activation(w_hi[:, ks, cols], stage[:, b], ACT.Copy).then_inc(s["w_hi"], 1)
        else:
            eng.wait_ge(s["w_staged"][b], 16 * (g + 1))
            if n == 0:
                eng.wait_ge(s["w_norm"], 16)
            eng.tensor_tensor(stage[:, b], stage[:, b],
                              wg[:, ks, None].broadcast_to([P, 4, GW]), ALU.mult).then_inc(s["w_scaled"], 1)
            eng.wait_ge(s["w_hi"], n + 1)
            eng.tensor_tensor(w_lo[:, ks, cols], stage[:, b], f32(w_hi[:, ks, cols]),
                              ALU.subtract).then_inc(s["w_lo"], 1)


def stage_weights(eng, w_dram, first_col, n_halves, s, bufs):
    stage = bufs[0]
    for n in range(n_halves):
        g, b = n // 2, n % 2
        if n >= 2:
            eng.wait_ge(s["w_lo"], n - 1)
        src = w_dram.rearrange("(k p) n -> p k n", p=P)[:, 4 * b:4 * b + 4,
                                                        first_col + g * GW:first_col + (g + 1) * GW]
        eng.dma_start(stage[:, b], src).then_inc(s["w_staged"][b], 16)


def after(eng, sem, count):
    if not isinstance(count, int) or count > 0:
        eng.wait_ge(sem, count)


def product3(eng, out, x_hi, x_lo, w_hi, w_lo, cols, halves=(0, 1)):
    for k in range(KD // 2 * halves[0], KD // 2 * (halves[-1] + 1)):
        for a, b in ((x_hi, w_hi), (x_hi, w_lo), (x_lo, w_hi)):
            mm = eng.matmul(out, a[:, k, :], b[:, k, cols], start=(k == 0 and a is x_hi and b is w_hi),
                            stop=(k == KD - 1 and a is x_lo))
    return mm


def pass_attention_inputs(nc, io, keep):
    with ExitStack() as ctx:
        def sb(name, shape, dt=F32):
            return ctx.enter_context(nc.sbuf_tensor("a_" + name, shape, dt))

        def sem(name):
            return ctx.enter_context(nc.semaphore("a_" + name))

        w_hi = sb("w_hi", [P, KD, 4 * GW], F32R)
        w_lo = sb("w_lo", [P, KD, 4 * GW], F32R)
        stage = sb("stage", [P, 2, 4, GW])
        wg = sb("wg", [P, KD])
        xt = sb("xt", [P, 2, D])
        xT_hi = [sb(f"xT_hi{p}", [P, KD, P], F32R) for p in range(2)]
        xT_lo = [sb(f"xT_lo{p}", [P, KD, P], F32R) for p in range(2)]
        ident, rstd = keep[:2]
        rope = sb("rope", [P, NT, 4 * HALF])
        qkg = sb("qkg", [P, 2, DQ])
        eps = sb("eps", [P, 1])
        ssx = sb("ssx", [P, 4])
        sq = sb("sq", [P, 2 * GW])
        ss = sb("ss", [P, 3, 16])
        qk = sb("qk", [P, 2, 16, DQ])
        rot = sb("rot", [P, 2, 16, 2 * HALF])
        vb = sb("vb", [P, 2, GW])
        gb = sb("gb", [P, 2, GW])
        proj = [ctx.enter_context(nc.psum_tensor(f"a_proj{g}", [P, GW], F32)) for g in range(4)]
        xps = [ctx.enter_context(nc.psum_tensor(f"a_xps{b}", [P, 4, P], F32)) for b in range(2)]

        s = {n: sem(n) for n in ("w_norm", "w_scaled", "w_hi", "w_lo", "consts", "eps", "x_ss", "x_root",
                                 "x_rs", "x_norm", "xT_ps", "xT_hi", "xT_lo", "qk_sq", "qk_ss", "qk_root", "qk_rs",
                                 "qk_norm", "qk_g", "qk_t1", "qk_t2", "qk_rot", "v_ready", "g_ready")}
        s["w_staged"] = [sem(f"w_staged{b}") for b in range(2)]
        s["x_load"] = [sem(f"x_load{p}") for p in range(2)]
        s["proj"] = [sem(f"proj{g}") for g in range(4)]
        s["store"] = [[sem(f"store{n}{p}") for p in range(2)] for n in range(4)]
        bufs = (stage, wg, w_hi, w_lo)
        block = open_block(nc, ctx, s.values())

        def over_tiles(eng, step):
            step(0, 0, 0)
            step(1, 0, 1)
            with eng.Fori(1, NP // 2) as j:
                for p in range(2):
                    step(j * 2 + p, j, p)

        @block.sync
        def _(sp):
            sp.dma_start(wg[:, :], io["norm_g"]).then_inc(s["w_norm"], 16)
            for p in range(2):
                sp.dma_start(xt[:, p], io["x"][p * P:(p + 1) * P, :]).then_inc(s["x_load"][p], 16)
            stage_weights(sp, io["w_in"], 0, 8, s, bufs)
            sp.dma_start(rope[:, :, :], io["rope"]).then_inc(s["consts"], 16)
            for n, name in enumerate(("q_norm_g", "k_norm_g")):
                sp.dma_start(qkg[:, n], io[name].partition_broadcast(P).rearrange("p a b -> p (a b)")).then_inc(s["consts"], 16)

            def stores(i, j, p, rows, dst_q, dst_k, dst_v, dst_g):
                sp.wait_ge(s["qk_rot"], i + 1)
                sp.dma_start(dst_q, qk[0:rows, p, 0:8].rearrange("p a b -> p (a b)")).then_inc(s["store"][0][p], 16)
                sp.dma_start(dst_k, qk[0:rows, p, 8:16].rearrange("p a b -> p (a b)")).then_inc(s["store"][1][p], 16)
                sp.wait_ge(s["v_ready"], i + 1)
                sp.dma_start(dst_v, vb[0:rows, p]).then_inc(s["store"][2][p], 16)
                sp.wait_ge(s["g_ready"], i + 1)
                sp.dma_start(dst_g, gb[0:rows, p]).then_inc(s["store"][3][p], 16)

            def prompt_stores(i, j, p):
                r = bass.ds(i * P, P)
                stores(i, j, p, P, io["q_s"][r, :], io["k_p"][r, :], io["v_p"][r, :], io["ga_s"][r, :])

            with sp.Fori(0, NP // 2 - 1) as j:
                for p in range(2):
                    i = j * 2 + p
                    sp.wait_ge(s["xT_ps"], 2 * (i + 1))
                    sp.dma_start(xt[:, p], io["x"][bass.ds((i + 2) * P, P), :]).then_inc(s["x_load"][p], 16)
                    prompt_stores(i, j, p)
            for i in (NP - 2, NP - 1):
                if i == NP - 2:
                    sp.wait_ge(s["xT_ps"], 2 * (i + 1))
                    sp.dma_start(xt[:, 0], io["x"][NP * P:NT * P, :]).then_inc(s["x_load"][0], 16)
                prompt_stores(i, i // 2, i % 2)
            r = slice(NP * P, NP * P + NS)
            stores(NP, NP // 2, 0, NS, io["q_s"][r, :], io["k_s"], io["v_s"], io["ga_s"][r, :])
            for n in range(4):
                sp.wait_ge(s["store"][n][0], 16 * (NP // 2 + 1))
                sp.wait_ge(s["store"][n][1], 16 * (NP // 2))

        @block.gpsimd
        def _(pool):
            pool.wait_ge(s["consts"], 48)

            def rotate(i, p):
                q = qk[:, p]
                pool.wait_ge(s["qk_norm"], 2 * i + 2)
                pool.tensor_tensor(q.rearrange("p (a h) d -> p a h d", a=2), q.rearrange("p (a h) d -> p a h d", a=2),
                                   qkg[:, :, None, :].broadcast_to([P, 2, 8, DQ]), ALU.mult).then_inc(s["qk_g"], 1)
                pool.wait_ge(s["qk_g"], i + 1)
                tile = rope[:, bass.ds(i, 1), :] if not isinstance(i, int) else rope[:, i:i + 1, :]
                cc = tile[:, :, 0:2 * HALF].broadcast_to([P, 16, 2 * HALF])
                lo = tile[:, :, 2 * HALF:3 * HALF].broadcast_to([P, 16, HALF])
                hi = tile[:, :, 3 * HALF:4 * HALF].broadcast_to([P, 16, HALF])
                pool.tensor_tensor(rot[:, 0], q[:, :, 0:2 * HALF], cc, ALU.mult).then_inc(s["qk_t1"], 1)
                pool.tensor_tensor(rot[:, 1, :, 0:HALF], q[:, :, HALF:2 * HALF], lo, ALU.mult).then_inc(s["qk_t2"], 1)
                pool.tensor_tensor(rot[:, 1, :, HALF:], q[:, :, 0:HALF], hi, ALU.mult).then_inc(s["qk_t2"], 1)
                pool.wait_ge(s["qk_t1"], i + 1)
                pool.wait_ge(s["qk_t2"], 2 * i + 2)
                pool.tensor_tensor(q[:, :, 0:2 * HALF], rot[:, 0], rot[:, 1], ALU.add).then_inc(s["qk_rot"], 1)

            with pool.Fori(0, NP // 2) as j:
                for p in range(2):
                    rotate(j * 2 + p, p)
            rotate(NP, 0)

        @block.scalar
        def _(act):
            def x_stats(i, p, load, seen):
                act.wait_ge(s["x_load"][p], load)
                after(act, s["qk_ss"], seen)
                act.activation(sq[:, :], xt[:, p], ACT.Square, accum_out=ssx[:, p:p + 1]).then_inc(s["x_ss"], 1)
                act.wait_ge(s["x_ss"], i + 1)
                act.activation(ssx[:, 2 + p:3 + p], ssx[:, p:p + 1], ACT.Sqrt, bias=eps[:, 0:1], scale=1.0 / D).then_inc(s["x_root"], 1)

            def hi_parts(i, p):
                for b in range(2):
                    act.wait_ge(s["xT_ps"], 2 * i + b + 1)
                    act.activation(xT_hi[p][:, 4 * b:4 * b + 4, :], xps[b][:, :, :], ACT.Copy).then_inc(s["xT_hi"], 1)

            def outputs(i, j, p, nxt):
                act.wait_ge(s["x_ss"], i + 1 + int(nxt))
                for g in range(2):
                    act.wait_ge(s["proj"][g], i + 1)
                    act.activation(sq[:, g * GW:(g + 1) * GW], proj[g][:, :], ACT.Square).then_inc(s["qk_sq"], 1)
                if nxt:
                    hi_parts(i + 1, 1 - p)
                act.wait_ge(s["qk_ss"], 2 * i + 2)
                act.activation(ss[:, 1], ss[:, 0], ACT.Sqrt, bias=eps[:, 0:1], scale=1.0 / DQ).then_inc(s["qk_root"], 1)
                act.wait_ge(s["proj"][2], i + 1)
                after(act, s["store"][2][p], 16 * j)
                act.activation(vb[:, p], proj[2][:, :], ACT.Copy).then_inc(s["v_ready"], 1)
                act.wait_ge(s["proj"][3], i + 1)
                after(act, s["store"][3][p], 16 * j)
                act.activation(gb[:, p], proj[3][:, :], ACT.Silu).then_inc(s["g_ready"], 1)

            act.wait_ge(s["eps"], 1)
            x_stats(0, 0, 16, 0)
            split_weights("act", act, 2, s, bufs)
            hi_parts(0, 0)
            split_rest = [2]
            for n in range(2, 8):
                g, b = n // 2, n % 2
                act.wait_ge(s["w_scaled"], n + 1)
                act.activation(w_hi[:, 4 * b:4 * b + 4, g * GW:(g + 1) * GW], stage[:, b], ACT.Copy).then_inc(s["w_hi"], 1)

            def step(i, j, p):
                x_stats(i + 1, 1 - p, j * 16 + 16 * (1 + p), 2 * i)
                outputs(i, j, p, True)

            over_tiles(act, step)
            outputs(NP, NP // 2, 0, False)

        @block.vector
        def _(dve):
            def x_norm(i, p):
                dve.wait_ge(s["x_root"], i + 1)
                col = slice(i, i + 1) if isinstance(i, int) else bass.ds(i, 1)
                dve.reciprocal(rstd[:, col], ssx[:, 2 + p:3 + p]).then_inc(s["x_rs"], 1)
                dve.wait_ge(s["x_rs"], i + 1)
                dve.tensor_scalar(xt[:, p], xt[:, p], rstd[:, col], None, ALU.mult).then_inc(s["x_norm"], 1)

            def lo_parts(i, p):
                for b in range(2):
                    dve.wait_ge(s["xT_hi"], 2 * i + b + 1)
                    dve.tensor_tensor(xT_lo[p][:, 4 * b:4 * b + 4, :], xps[b][:, :, :],
                                      f32(xT_hi[p][:, 4 * b:4 * b + 4, :]), ALU.subtract).then_inc(s["xT_lo"], 1)

            def outputs(i, j, p, nxt):
                for g in range(2):
                    dve.wait_ge(s["qk_sq"], 2 * i + g + 1)
                    dve.tensor_reduce(ss[:, 0, 8 * g:8 * g + 8], sq[:, g * GW:(g + 1) * GW].rearrange("p (a b) -> p a b", b=DQ),
                                      AX.X, ALU.add).then_inc(s["qk_ss"], 1)
                if nxt:
                    lo_parts(i + 1, 1 - p)
                dve.wait_ge(s["qk_root"], i + 1)
                dve.reciprocal(ss[:, 2], ss[:, 1]).then_inc(s["qk_rs"], 1)
                dve.wait_ge(s["qk_rs"], i + 1)
                after(dve, s["store"][0][p], 16 * j)
                after(dve, s["store"][1][p], 16 * j)
                for g in range(2):
                    dve.tensor_tensor(qk[:, p, 8 * g:8 * g + 8], proj[g][:, :].rearrange("p (a b) -> p a b", b=DQ),
                                      ss[:, 2, 8 * g:8 * g + 8, None].broadcast_to([P, 8, DQ]), ALU.mult).then_inc(s["qk_norm"], 1)

            dve.memset(eps[:, :], EPS).then_inc(s["eps"], 1)
            x_norm(0, 0)
            split_weights("dve", dve, 2, s, bufs)
            lo_parts(0, 0)
            for n in range(2, 8):
                g, b = n // 2, n % 2
                ks, cols = slice(4 * b, 4 * b + 4), slice(g * GW, (g + 1) * GW)
                dve.wait_ge(s["w_staged"][b], 16 * (g + 1))
                dve.tensor_tensor(stage[:, b], stage[:, b], wg[:, ks, None].broadcast_to([P, 4, GW]),
                                  ALU.mult).then_inc(s["w_scaled"], 1)
                dve.wait_ge(s["w_hi"], n + 1)
                dve.tensor_tensor(w_lo[:, ks, cols], stage[:, b], f32(w_hi[:, ks, cols]),
                                  ALU.subtract).then_inc(s["w_lo"], 1)

            def step(i, j, p):
                x_norm(i + 1, 1 - p)
                outputs(i, j, p, True)

            over_tiles(dve, step)
            outputs(NP, NP // 2, 0, False)

        @block.tensor
        def _(pe):
            def transposes(i, p):
                pe.wait_ge(s["x_norm"], i + 1)
                after(pe, s["xT_lo"], 2 * i)
                for b in range(2):
                    for k in range(4):
                        mm = pe.transpose(xps[b][:, k, :], xt[:, p, (4 * b + k) * P:(4 * b + k + 1) * P], ident[:, :])
                    mm.then_inc(s["xT_ps"], 1)

            def group(i, p, g, first):
                pe.wait_ge(s["xT_lo"], 2 * i + 2)
                if first:
                    pe.wait_ge(s["w_lo"], 2 * g + 2)
                if g < 2:
                    after(pe, s["qk_norm"], 2 * i)
                elif g == 2:
                    after(pe, s["v_ready"], i)
                else:
                    after(pe, s["g_ready"], i)
                product3(pe, proj[g][:, :], xT_hi[p], xT_lo[p], w_hi, w_lo,
                         slice(g * GW, (g + 1) * GW)).then_inc(s["proj"][g], 1)

            transposes(0, 0)

            def step(i, j, p):
                first = isinstance(i, int) and i == 0
                group(i, p, 0, first)
                group(i, p, 1, first)
                transposes(i + 1, 1 - p)
                group(i, p, 2, first)
                group(i, p, 3, first)

            over_tiles(pe, step)
            for g in range(4):
                group(NP, 0, g, False)


def make_identity(pool, ident, done):
    pool.memset(ident[:, :], 0.0).then_inc(done, 1)
    pool.wait_ge(done, 1)
    pool.affine_select(out=ident[:, :], in_=ident[:, :], compare_op=ALU.not_equal, fill=1.0, base=0,
                       pattern=[[-1, P]], channel_multiplier=1).then_inc(done, 1)


CH = P
BLOCKS = (128, 64, 32, 16, 8, 4)
NL = len(BLOCKS) + 1
LEAF_Q, LEAF_QE, LEAF_K, LEAF_KD = 6, 7, 8, 9
SLOTS = 10
F_MIN = 2.0 ** -62


def level_views(ap, width):
    v = ap.rearrange("p (n two w) -> p n two w", two=2, w=width // 2)
    n = v.shape[1]
    ref = v[:, :, 0, width // 2 - 1:width // 2].broadcast_to([P, n, width // 2])
    return v[:, :, 0, :], v[:, :, 1, :], ref


def decay_differences(dve, b, lv, blocks, last, n0=0):
    for slot, width in blocks:
        b_lo, b_up, ref = level_views(b, width)
        d_lo, d_up, _ = level_views(lv[:, slot - n0, :], width)
        dve.tensor_tensor(d_up, b_up, ref, ALU.subtract)
        dve.tensor_tensor(d_lo, ref, b_lo, ALU.subtract)
    pair = b.rearrange("p (n w) -> p n w", w=2)
    first = pair[:, :, 0:1].broadcast_to([P, pair.shape[1], 2])
    dve.tensor_tensor(lv[:, LEAF_Q - n0, :].rearrange("p (n w) -> p n w", w=2), pair, first, ALU.subtract)
    dve.tensor_tensor(lv[:, LEAF_K - n0, :].rearrange("p (n w) -> p n w", w=2), first, pair, ALU.subtract)
    dve.tensor_copy(lv[:, LEAF_QE - n0, :], b)
    run = b.rearrange("p (n w) -> p n w", w=last)
    end = run[:, :, last - 1:last].broadcast_to([P, run.shape[1], last])
    return dve.tensor_tensor(lv[:, LEAF_KD - n0, :].rearrange("p (n w) -> p n w", w=last), end, run, ALU.subtract)


def decay_products(pool, lv, q, k, blocks, n0=0):
    for slot, width in blocks:
        e_lo, e_up, _ = level_views(lv[:, slot - n0, :], width)
        _, q_up, _ = level_views(q, width)
        k_lo, _, _ = level_views(k, width)
        pool.tensor_tensor(e_up, e_up, q_up, ALU.mult)
        pool.tensor_tensor(e_lo, e_lo, k_lo, ALU.mult)
    n = q.shape[1]
    pool.tensor_tensor(lv[:, LEAF_Q - n0:LEAF_QE + 1 - n0, :], lv[:, LEAF_Q - n0:LEAF_QE + 1 - n0, :],
                       q[:, None, :].broadcast_to([P, 2, n]), ALU.mult)
    return pool.tensor_tensor(lv[:, LEAF_K - n0:LEAF_KD + 1 - n0, :], lv[:, LEAF_K - n0:LEAF_KD + 1 - n0, :],
                              k[:, None, :].broadcast_to([P, 2, n]), ALU.mult)


def pass_hgrn(nc, io, keep):
    with ExitStack() as ctx:
        def sb(name, shape, dt=F32):
            return ctx.enter_context(nc.sbuf_tensor("h_" + name, shape, dt))

        def sem(name):
            return ctx.enter_context(nc.semaphore("h_" + name))

        def ps(name, shape):
            return ctx.enter_context(nc.psum_tensor("h_" + name, shape, F32))

        ident, rstd = keep[:2]
        w_hi = sb("w_hi", [P, KD, 4 * GW], F32R)
        w_lo = sb("w_lo", [P, KD, 4 * GW], F32R)
        shared = sb("stage_or_levels", [P, 2, SLOTS * 2 * P])
        stage = shared[:, :, 0:4 * GW].rearrange("p b (k n) -> p b k n", k=4)
        lv = [shared[:, hf, :].rearrange("p (s n) -> p s n", s=SLOTS) for hf in range(2)]
        wg = sb("wg", [P, KD])
        xt = sb("xt", [P, D])
        xT_hi = [sb(f"xT_hi{p}", [P, KD, P], F32R) for p in range(2)]
        xT_lo = [sb(f"xT_lo{p}", [P, KD, P], F32R) for p in range(2)]
        q_tok, s_tok = sb("q_tok", [P, GW]), sb("s_tok", [P, GW])
        qT, kT, lfT, bT = (sb(n, [P, GW]) for n in ("qT", "kT", "lfT", "bT"))
        v_tok, gate = sb("v_tok", [P, 2, GW]), sb("gate", [P, 2, GW])
        mask = sb("mask", [P, NL, P], BF16)
        masked = sb("masked", [P, NL, P])
        att = sb("att", [P, 2, P])
        kd_tok = sb("kd_tok", [P, GW])
        state = sb("state", [P, H, DV])
        ebc = sb("ebc", [P, 2, H])
        o_out = sb("o_out", [P, GW])
        oss = sb("oss", [P, 3, H])
        ng = sb("ng", [P, DV])
        eps = sb("eps", [P, 1])
        lbt = sb("lbt", [P, 6, H])
        proj = [ps(f"proj{b}", [P, GW]) for b in range(2)]
        xps = [ps(f"xps{b}", [P, 4, P]) for b in range(2)]
        lps = ps("lps", [P, 8, P])
        tps = ps("tps", [P, 4, P])
        ops = ps("ops", [P, H, DV])
        s = {n: sem(n) for n in (
            "w_norm", "w_scaled", "w_hi", "w_lo", "consts", "lb_load", "mask_load", "mask", "eps", "lb", "lb_exp", "x_load",
            "x_norm", "xT_ps", "xT_hi", "xT_lo", "q_tok", "s_tok", "v_tok", "gate", "qT_ps", "sT_ps", "qT", "f",
            "f_clamped", "log_f", "cumsum", "diff", "decay", "ebc", "operands", "levels", "masked", "att", "av", "kdT_ps",
            "kd_tok", "gain_ps", "state", "o_sq", "o_ss", "o_root", "o_rs", "o_norm", "o_g", "o_out", "store", "tail")}
        s["w_staged"] = [sem(f"w_staged{b}") for b in range(2)]
        s["proj"] = [sem(f"proj{g}") for g in range(4)]
        bufs = (stage, wg, w_hi, w_lo)
        block = open_block(nc, ctx, s.values())
        all_levels = tuple(enumerate(BLOCKS))

        def half(ap, hf):
            return ap[:, hf * 2 * P:(hf + 1) * 2 * P]

        @block.sync
        def _(sp):
            sp.dma_start(wg[:, :], io["norm_g"]).then_inc(s["w_norm"], 16)
            sp.dma_start(xt[:, :], io["x"][0:P, :]).then_inc(s["x_load"], 16)
            sp.dma_start(lbt[:, 0:2, :], io["lb"]).then_inc(s["lb_load"], 16)
            sp.dma_start(masked[:, :, :], io["level_mask"]).then_inc(s["mask_load"], 16)
            sp.dma_start(ng[:, :], io["hgrn_norm_g"].partition_broadcast(P).rearrange("p a b -> p (a b)")).then_inc(s["consts"], 16)
            stage_weights(sp, io["w_in"], 4 * GW, 8, s, bufs)

            def load(i):
                sp.wait_ge(s["xT_ps"], 2 * i)
                sp.dma_start(xt[:, :], io["x"][bass.ds(i * P, P), :]).then_inc(s["x_load"], 16)

            def store(t):
                sp.wait_ge(s["o_out"], t + 1)
                sp.dma_start(io["mr_s"][bass.ds(t * P, P), :], o_out[:, :]).then_inc(s["store"], 16)

            load(1)
            load(2)
            with sp.Fori(3, NT) as i:
                load(i)
                store(i - 3)
            store(NP - 2)
            store(NP - 1)
            sp.wait_ge(s["state"], NP + 1)
            sp.dma_start(io["s_p"].rearrange("h d v -> d h v"), state[:, :, :]).then_inc(s["tail"], 16)
            sp.wait_ge(s["qT"], NT)
            sp.dma_start(io["hq_s"], qT[:, :]).then_inc(s["tail"], 16)
            sp.wait_ge(s["f_clamped"], NT)
            sp.dma_start(io["hk_s"], kT[:, :]).then_inc(s["tail"], 16)
            sp.wait_ge(s["log_f"], NT)
            sp.dma_start(io["hl_s"], lfT[:, :]).then_inc(s["tail"], 16)
            sp.wait_ge(s["v_tok"], NT)
            sp.dma_start(io["hv_s"], v_tok[:, 0]).then_inc(s["tail"], 16)
            sp.wait_ge(s["gate"], NT)
            sp.dma_start(io["hg_s"], gate[:, 0]).then_inc(s["tail"], 16)
            sp.wait_ge(s["tail"], 96)
            sp.wait_ge(s["store"], 16 * NP)

        @block.gpsimd
        def _(pool):
            pool.wait_ge(s["consts"], 16)

            def operands(i):
                for hf in range(2):
                    pool.wait_ge(s["decay"], 2 * i + hf + 1)
                    pool.wait_ge(s["qT"], i + 1)
                    pool.wait_ge(s["f_clamped"], i + 1)
                    decay_products(pool, lv[hf], half(qT, hf), half(kT, hf), all_levels).then_inc(s["operands"], 1)

            def gated(t, pt):
                pool.wait_ge(s["o_norm"], t + 1)
                o3 = o_out[:, :].rearrange("p (h v) -> p h v", h=H)
                pool.tensor_tensor(o3, o3, ng[:, None, :].broadcast_to([P, H, DV]), ALU.mult).then_inc(s["o_g"], 1)
                pool.wait_ge(s["o_g"], t + 1)
                pool.wait_ge(s["gate"], t + 1)
                pool.tensor_tensor(o_out[:, :], o_out[:, :], gate[:, pt], ALU.mult).then_inc(s["o_out"], 1)

            operands(0)
            with pool.Fori(0, NP // 2) as j:
                for pt in range(2):
                    t = j * 2 + pt
                    operands(t + 1)
                    gated(t, pt)

        @block.scalar
        def _(act):
            def hi_parts(i, p):
                for b in range(2):
                    act.wait_ge(s["xT_ps"], 2 * i + b + 1)
                    act.activation(xT_hi[p][:, 4 * b:4 * b + 4, :], xps[b][:, :, :], ACT.Copy).then_inc(s["xT_hi"], 1)

            def gate_input(i, p):
                after(act, s["proj"][3], i + 1)
                after(act, s["o_out"], i - 1)
                act.activation(gate[:, p], proj[1][:, :], ACT.Silu).then_inc(s["gate"], 1)

            def inputs_qf(i):
                act.wait_ge(s["proj"][0], i + 1)
                after(act, s["qT_ps"], i)
                act.activation(q_tok[:, :], proj[0][:, :], ACT.Silu).then_inc(s["q_tok"], 1)
                act.wait_ge(s["proj"][1], i + 1)
                after(act, s["sT_ps"], i)
                act.activation(s_tok[:, :], proj[1][:, :], ACT.Sigmoid).then_inc(s["s_tok"], 1)

            def q_columns(i):
                act.wait_ge(s["qT_ps"], i + 1)
                after(act, s["operands"], 2 * i)
                act.activation(qT[:, :], tps[:, :, :].rearrange("p h t -> p (h t)"), ACT.Copy).then_inc(s["qT"], 1)

            def value_input(i, p):
                act.wait_ge(s["proj"][2], i + 1)
                act.activation(v_tok[:, p], proj[0][:, :], ACT.Copy).then_inc(s["v_tok"], 1)

            def decays(i, p):
                act.wait_ge(s["f_clamped"], i + 1)
                act.activation(lfT[:, :], lfT[:, :], ACT.Ln).then_inc(s["log_f"], 1)

            def exps(i, hf):
                act.wait_ge(s["diff"], 2 * i + hf + 1)
                act.activation(lv[hf], lv[hf], ACT.Exp).then_inc(s["decay"], 1)

            def tile_decay(p):
                act.activation(ebc[:, p], bT[:, :].rearrange("p (h t) -> p h t", h=H)[:, :, P - 1], ACT.Exp).then_inc(s["ebc"], 1)

            def o_stats(t):
                act.wait_ge(s["av"], 4 * t + 4)
                after(act, s["store"], 16 * t)
                act.activation(o_out[:, :], ops[:, :, :].rearrange("p h v -> p (h v)"), ACT.Square).then_inc(s["o_sq"], 1)
                act.wait_ge(s["o_ss"], t + 1)
                act.activation(oss[:, 1], oss[:, 0], ACT.Sqrt, bias=eps[:, 0:1], scale=1.0 / DV).then_inc(s["o_root"], 1)

            def step(t, pt, more):
                i, p = t + 1, 1 - pt
                gate_input(t, pt)
                inputs_qf(i)
                act.wait_ge(s["kdT_ps"], t + 1)
                after(act, s["gain_ps"], t)
                act.activation(kd_tok[:, :], xps[1][:, :, :].rearrange("p h d -> p (h d)"), ACT.Copy).then_inc(s["kd_tok"], 1)
                q_columns(i)
                decays(i, p)
                exps(i, 0)
                value_input(i, p)
                if more:
                    hi_parts(i + 1, pt)
                exps(i, 1)
                tile_decay(p)
                o_stats(t)

            act.wait_ge(s["lb"], 2)
            act.activation(lbt[:, 3:5, :], lbt[:, 3:5, :], ACT.Exp).then_inc(s["lb_exp"], 1)
            split_weights("act", act, 8, s, bufs)
            hi_parts(0, 0)
            inputs_qf(0)
            q_columns(0)
            decays(0, 0)
            exps(0, 0)
            value_input(0, 0)
            hi_parts(1, 1)
            exps(0, 1)
            tile_decay(0)
            step(0, 0, True)
            step(1, 1, True)
            with act.Fori(0, NP // 2 - 2) as j:
                for pt in range(2):
                    step(2 * j + 2 + pt, pt, True)
            step(NP - 2, 0, True)
            step(NP - 1, 1, False)
            gate_input(NP, 0)

        @block.vector
        def _(dve):
            def x_norm(i):
                dve.wait_ge(s["x_load"], 16 * i + 16)
                col = slice(i, i + 1) if isinstance(i, int) else bass.ds(i, 1)
                dve.tensor_scalar(xt[:, :], xt[:, :], rstd[:, col], None, ALU.mult).then_inc(s["x_norm"], 1)

            def lo_parts(i, p):
                for b in range(2):
                    dve.wait_ge(s["xT_hi"], 2 * i + b + 1)
                    dve.tensor_tensor(xT_lo[p][:, 4 * b:4 * b + 4, :], xps[b][:, :, :],
                                      f32(xT_hi[p][:, 4 * b:4 * b + 4, :]), ALU.subtract).then_inc(s["xT_lo"], 1)

            def keep_pairs(t, h):
                n = 4 * t + h
                dve.wait_ge(s["levels"], n + 1)
                after(dve, s["att"], n)
                dve.tensor_tensor(masked[:, :, :], lps[:, 0:NL, :], mask[:, :, :], ALU.mult).then_inc(s["masked"], 1)
                dve.wait_ge(s["masked"], n + 1)
                if h >= 2:
                    dve.wait_ge(s["av"], n - 1)
                dve.tensor_reduce(att[:, h % 2], masked[:, :, :].rearrange("p l t -> p t l"), AX.X, ALU.add).then_inc(s["att"], 1)

            def forget(i):
                dve.wait_ge(s["sT_ps"], i + 1)
                after(dve, s["operands"], 2 * i)
                for h in range(H):
                    last = dve.tensor_scalar(lfT[:, h * P:(h + 1) * P], xps[0][:, h, :], lbt[:, 4, h:h + 1], lbt[:, 3, h:h + 1],
                                             ALU.mult, ALU.add)
                last.then_inc(s["f"], 1)
                dve.wait_ge(s["f"], i + 1)
                dve.tensor_scalar(kT[:, :], lfT[:, :], -1.0, 1.0, ALU.mult, ALU.add)
                dve.tensor_scalar(lfT[:, :], lfT[:, :], F_MIN, None, ALU.max).then_inc(s["f_clamped"], 1)

            def cumulate(i):
                dve.wait_ge(s["log_f"], i + 1)
                after(dve, s["ebc"], i)
                for h in range(H):
                    cols = slice(h * P, (h + 1) * P)
                    last = dve.tensor_tensor_scan(bT[:, cols], lfT[:, cols], lfT[:, cols], 0.0, ALU.add, ALU.bypass)
                last.then_inc(s["cumsum"], 1)
                dve.wait_ge(s["cumsum"], i + 1)

            def differences(i, t):
                for hf in range(2):
                    if t is not None:
                        dve.wait_ge(s["av"], 4 * t + 2 * hf + 2)
                        dve.wait_ge(s["kdT_ps"], t + 1)
                    decay_differences(dve, half(bT, hf), lv[hf], all_levels, P).then_inc(s["diff"], 1)

            def o_norm(t):
                o3 = o_out[:, :].rearrange("p (h v) -> p h v", h=H)
                dve.wait_ge(s["o_sq"], t + 1)
                dve.tensor_reduce(oss[:, 0], o3, AX.X, ALU.add).then_inc(s["o_ss"], 1)
                dve.wait_ge(s["o_root"], t + 1)
                dve.reciprocal(oss[:, 2], oss[:, 1]).then_inc(s["o_rs"], 1)
                dve.wait_ge(s["o_rs"], t + 1)
                dve.tensor_tensor(o3, ops[:, :, :], oss[:, 2, :, None].broadcast_to([P, H, DV]), ALU.mult).then_inc(s["o_norm"], 1)

            def carry(t, pt):
                dve.wait_ge(s["gain_ps"], t + 1)
                dve.wait_ge(s["ebc"], t + 1)
                for h in range(H):
                    last = dve.scalar_tensor_tensor(out=state[:, h], in0=state[:, h], scalar=ebc[:, pt, h:h + 1], in1=tps[:, h, :],
                                                    op0=ALU.mult, op1=ALU.add)
                last.then_inc(s["state"], 1)

            dve.memset(eps[:, :], EPS).then_inc(s["eps"], 1)
            dve.memset(state[:, :, :], 0.0).then_inc(s["state"], 1)
            dve.wait_ge(s["mask_load"], 16)
            dve.tensor_copy(mask[:, :, :], masked[:, :, :]).then_inc(s["mask"], 1)
            dve.wait_ge(s["mask"], 1)
            dve.wait_ge(s["lb_load"], 16)
            dve.tensor_tensor(lbt[:, 2], lbt[:, 0], lbt[:, 1], ALU.max).then_inc(s["lb"], 1)
            dve.wait_ge(s["lb"], 1)
            dve.tensor_tensor(lbt[:, 3:5], lbt[:, 0:2], lbt[:, 2, None, :].broadcast_to([P, 2, H]), ALU.subtract).then_inc(s["lb"], 1)
            dve.wait_ge(s["lb_exp"], 1)
            dve.tensor_tensor(lbt[:, 2], lbt[:, 3], lbt[:, 4], ALU.add).then_inc(s["lb"], 1)
            dve.wait_ge(s["lb"], 3)
            dve.reciprocal(lbt[:, 5], lbt[:, 2]).then_inc(s["lb"], 1)
            dve.wait_ge(s["lb"], 4)
            dve.tensor_tensor(lbt[:, 3:5], lbt[:, 3:5], lbt[:, 5, None, :].broadcast_to([P, 2, H]), ALU.mult).then_inc(s["lb"], 1)
            dve.wait_ge(s["lb"], 5)
            x_norm(0)
            split_weights("dve", dve, 8, s, bufs)
            lo_parts(0, 0)
            forget(0)
            cumulate(0)
            differences(0, None)
            x_norm(1)
            lo_parts(1, 1)

            def step(t, pt, more):
                i, p = t + 1, 1 - pt
                keep_pairs(t, 0)
                keep_pairs(t, 1)
                if more:
                    x_norm(i + 1)
                keep_pairs(t, 2)
                forget(i)
                keep_pairs(t, 3)
                cumulate(i)
                differences(i, t)
                if more:
                    lo_parts(i + 1, pt)
                o_norm(t)
                carry(t, pt)

            step(0, 0, True)
            step(1, 1, True)
            with dve.Fori(0, NP // 2 - 2) as j:
                for pt in range(2):
                    step(2 * j + 2 + pt, pt, True)
            step(NP - 2, 0, True)
            step(NP - 1, 1, False)

        @block.tensor
        def _(pe):
            def x_columns(i, p):
                pe.wait_ge(s["x_norm"], i + 1)
                after(pe, s["xT_lo"], 2 * i)
                after(pe, s["f"], i)
                after(pe, s["kd_tok"], i - 1)
                for b in range(2):
                    for k in range(4):
                        mm = pe.transpose(xps[b][:, k, :], xt[:, (4 * b + k) * P:(4 * b + k + 1) * P], ident[:, :])
                    mm.then_inc(s["xT_ps"], 1)

            def group(i, p, g, halves=(0, 1), first=False):
                if 0 in halves:
                    pe.wait_ge(s["xT_lo"], 2 * i + 2)
                    if first:
                        pe.wait_ge(s["w_lo"], 2 * g + 2)
                    after(pe, s[("v_tok", "gate", "q_tok", "s_tok")[g]], i if g < 2 else i + 1)
                mm = product3(pe, proj[g % 2][:, :], xT_hi[p], xT_lo[p], w_hi, w_lo,
                              slice(g * GW, (g + 1) * GW), halves)
                if 1 in halves:
                    mm.then_inc(s["proj"][g], 1)

            def head_columns(i, t):
                pe.wait_ge(s["q_tok"], i + 1)
                after(pe, s["state"], i)
                for h in range(H):
                    mm = pe.transpose(tps[:, h, :], q_tok[:, h * P:(h + 1) * P], ident[:, :])
                mm.then_inc(s["qT_ps"], 1)
                pe.wait_ge(s["s_tok"], i + 1)
                for h in range(H):
                    mm = pe.transpose(xps[0][:, h, :], s_tok[:, h * P:(h + 1) * P], ident[:, :])
                mm.then_inc(s["sT_ps"], 1)

            def levels(t, h):
                c = slice((h % 2) * P, (h % 2) * P + P)
                l = lv[h // 2]
                pe.wait_ge(s["operands"], 2 * t + h // 2 + 1)
                after(pe, s["masked"], 4 * t + h)
                for n in range(NL - 1):
                    pe.matmul(lps[:, n, :], l[:, n, c], l[:, n, c], start=True, stop=True)
                pe.matmul(lps[:, NL - 1, :], l[:, LEAF_K, c], l[:, LEAF_Q, c], start=True, stop=True).then_inc(s["levels"], 1)

            def out_rows(t, pt, h):
                c = slice((h % 2) * P, (h % 2) * P + P)
                pe.wait_ge(s["att"], 4 * t + h + 1)
                pe.wait_ge(s["state"], t + 1)
                after(pe, s["o_norm"], t)
                pe.wait_ge(s["v_tok"], t + 1)
                pe.matmul(ops[:, h, :], att[:, h % 2], v_tok[:, pt, h * DV:(h + 1) * DV], start=True, stop=False)
                pe.matmul(ops[:, h, :], lv[h // 2][:, LEAF_QE, c], state[:, h], start=False, stop=True).then_inc(s["av"], 1)

            def key_rows(t):
                pe.wait_ge(s["operands"], 2 * t + 2)
                for h in range(H):
                    c = slice((h % 2) * P, (h % 2) * P + P)
                    mm = pe.transpose(xps[1][:, h, :], lv[h // 2][:, LEAF_KD, c], ident[:, :])
                mm.then_inc(s["kdT_ps"], 1)

            def gains(t, pt):
                pe.wait_ge(s["kd_tok"], t + 1)
                pe.wait_ge(s["qT"], t + 2)
                for h in range(H):
                    mm = pe.matmul(tps[:, h, :], kd_tok[:, h * P:(h + 1) * P], v_tok[:, pt, h * DV:(h + 1) * DV],
                                   start=True, stop=True)
                mm.then_inc(s["gain_ps"], 1)

            def step(t, pt, more):
                i, p = t + 1, 1 - pt
                group(i, p, 0)
                levels(t, 0)
                group(i, p, 1, (0,))
                levels(t, 1)
                out_rows(t, pt, 0)
                group(i, p, 1, (1,))
                levels(t, 2)
                key_rows(t)
                out_rows(t, pt, 1)
                head_columns(i, t)
                levels(t, 3)
                out_rows(t, pt, 2)
                group(i, p, 2, (0,))
                out_rows(t, pt, 3)
                group(i, p, 2, (1,))
                if more:
                    x_columns(i + 1, pt)
                group(i, p, 3, (0,))
                gains(t, pt)
                group(i, p, 3, (1,))

            x_columns(0, 0)
            group(0, 0, 0, first=True)
            group(0, 0, 1, first=True)
            head_columns(0, None)
            group(0, 0, 2, first=True)
            x_columns(1, 1)
            group(0, 0, 3, first=True)
            step(0, 0, True)
            step(1, 1, True)
            with pe.Fori(0, NP // 2 - 2) as j:
                for pt in range(2):
                    step(2 * j + 2 + pt, pt, True)
            step(NP - 2, 0, True)
            step(NP - 1, 1, False)


NEG = -1e30


def pass_attention(nc, io, keep):
    with ExitStack() as ctx:
        def sb(name, shape, dt=F32):
            return ctx.enter_context(nc.sbuf_tensor("p_" + name, shape, dt))

        def sem(name):
            return ctx.enter_context(nc.semaphore("p_" + name))

        def ps(name, shape):
            return ctx.enter_context(nc.psum_tensor("p_" + name, shape, F32))

        ident, nlam = keep[0], keep[2]
        M = 2 * H
        KT = sb("KT", [P, M, SEQ], F32R)
        V = sb("V", [P, NP, H * DV])
        qk_in = sb("qk_in", [P, 2, 2, GW])
        k_hl = sb("k_hl", [P, M, 2, DQ], F32R)
        q_hl = sb("q_hl", [P, 2, M, 2, DQ], F32R)
        QS = [[sb(f"Q{part}{p}", [P, M, P], F32R) for part in "hl"] for p in range(2)]
        sc = [sb(f"scores{m}", [P, 3 - m, SEQ]) for m in range(2)]
        WT = sb("WT", [P, 2, 4, P])
        mask = sb("mask", [P, 4 * P])
        zero = sb("zero", [P, 4 * P])
        mx = sb("mx", [P, 2, 2, 4])
        nmx = sb("nmx", [P, 2, 2])
        ls = sb("ls", [P, 2, 2, H])
        rl = sb("rl", [P, 2, H])
        coef = sb("coef", [P, 2])
        r0 = sb("r0", [P, H])
        ob = sb("ob", [P, 2, H * DV])
        sps = [ps(f"sps{n}", [P, 512]) for n in range(4)]
        tps = [ps(f"tps{n}", [P, 4, P]) for n in range(2)]
        ops = [ps(f"ops{n}", [P, H, DV]) for n in range(2)]
        s = {n: sem(n) for n in ("v_load0", "v_load1", "v_load2", "v_load3", "mask_load", "zero", "q_hi", "k_hi", "q_lo", "k_lo",
                                 "sps_full", "sps_read", "neg_max", "exp", "recip", "coef",
                                 "weights", "wT_ps", "wT", "out_ps", "r0", "out")}
        s["qk_load"] = [sem(f"qk_load{p}") for p in range(2)]
        s["store"] = [sem(f"store{p}") for p in range(2)]
        block = open_block(nc, ctx, s.values())
        chunks = [[(c, min(512, (i + 1) * P - c)) for c in range(0, (i + 1) * P, 512)] for i in range(NP)]
        n_heads = NP * H
        tile_head = [(i, h) for i in range(NP) for h in range(H)]
        first_prep, first_sc, first_wt, n_use, n_wt = {0: 0}, {}, {}, 6, 0
        for i, h in tile_head:
            if h == 2 and i + 1 < NP:
                first_prep[i + 1] = n_use
                n_use += 6
            first_sc[i, h], first_wt[i, h] = n_use, n_wt
            n_use += 2 * len(chunks[i])
            n_wt += len(chunks[i])

        def twice(q):
            return q.rearrange("p (m d) -> p m d", d=DQ)[:, :, None, :].broadcast_to([P, M, 2, DQ])

        @block.sync
        def _(sp):
            def load(i):
                r = slice(i * P, (i + 1) * P)
                if i >= 2:
                    sp.wait_ge(s["q_lo"], i - 1)
                    sp.wait_ge(s["k_lo"], i - 1)
                sp.dma_start(qk_in[:, i % 2, 0], io["q_s"][r, :]).then_inc(s["qk_load"][i % 2], 16)
                sp.dma_start(qk_in[:, i % 2, 1], io["k_p"][r, :]).then_inc(s["qk_load"][i % 2], 16)

            load(0)
            sp.dma_start(mask[:, :], io["causal"]).then_inc(s["mask_load"], 16)
            load(1)
            for q in range(4):
                sp.dma_start(V[:, 4 * q:4 * q + 4, :], io["v_p"].rearrange("(b p) n -> p b n", p=P)[:, 4 * q:4 * q + 4, :])\
                  .then_inc(s[f"v_load{q}"], 16)
            for i in range(NP):
                if i + 2 < NP:
                    load(i + 2)
                sp.wait_ge(s["out"], i + 1)
                sp.dma_start(io["o_s"][i * P:(i + 1) * P, :], ob[:, i % 2]).then_inc(s["store"][i % 2], 16)
            for p in range(2):
                sp.wait_ge(s["store"][p], 16 * NP // 2)

        @block.gpsimd
        def _(pool):
            pool.memset(zero[:, :], 0.0).then_inc(s["zero"], 1)
            for i in range(NP):
                pool.wait_ge(s["k_hi"], i + 1)
                if i >= 1:
                    pool.wait_ge(s["sps_full"], first_prep[i - 1] + 6)
                pool.tensor_tensor(k_hl[:, :, 1], qk_in[:, i % 2, 1].rearrange("p (m d) -> p m d", d=DQ),
                                   f32(k_hl[:, :, 0]), ALU.subtract).then_inc(s["k_lo"], 1)
                pool.wait_ge(s["q_hi"], i + 1)
                pool.tensor_tensor(q_hl[:, 1], twice(qk_in[:, i % 2, 0]),
                                   f32(q_hl[:, 0]), ALU.subtract).then_inc(s["q_lo"], 1)

        @block.scalar
        def _(act):
            def split_hi(i):
                act.wait_ge(s["qk_load"][i % 2], 32 * (i // 2 + 1))
                if i >= 1:
                    act.wait_ge(s["sps_full"], first_prep[i - 1] + 6)
                act.activation(k_hl[:, :, 0], qk_in[:, i % 2, 1].rearrange("p (m d) -> p m d", d=DQ), ACT.Copy).then_inc(s["k_hi"], 1)
                act.activation(q_hl[:, 0], twice(qk_in[:, i % 2, 0]), ACT.Copy).then_inc(s["q_hi"], 1)

            def exp_row(n, m):
                i, h = tile_head[n]
                act.wait_ge(s["neg_max"], n + 1)
                w = (i + 1) * P
                row = sc[m][:, n % (3 - m), 0:w]
                act.activation(row, row, ACT.Exp, bias=nmx[:, n % 2, m:m + 1],
                               accum_out=ls[:, i % 2, m, h:h + 1]).then_inc(s["exp"], 1)

            def weights_out(n, c):
                i, h = tile_head[n]
                g = first_wt[i, h] + c
                act.wait_ge(s["wT_ps"], g + 1)
                if g >= 2:
                    act.wait_ge(s["out_ps"], g - 1)
                w = chunks[i][c][1]
                act.activation(WT[:, g % 2, 0:w // P, :], tps[g % 2][:, 0:w // P, :], ACT.Copy).then_inc(s["wT"], 1)

            split_hi(0)
            for n in range(n_heads + 2):
                n_c = len(chunks[tile_head[n - 2][0]]) if n >= 2 else 0
                if 1 <= n <= n_heads:
                    exp_row(n - 1, 0)
                if n_c:
                    weights_out(n - 2, 0)
                if 1 <= n <= n_heads:
                    exp_row(n - 1, 1)
                for c in range(1, n_c):
                    weights_out(n - 2, c)
                if n < n_heads and tile_head[n][1] == 0 and tile_head[n][0] + 1 < NP:
                    split_hi(tile_head[n][0] + 1)

        @block.vector
        def _(dve):
            def prep_out(i):
                if i >= 2:
                    dve.wait_ge(s["sps_full"], first_sc[i - 1, 0])
                for n in range(6):
                    k = first_prep[i] + n
                    dve.wait_ge(s["sps_full"], k + 1)
                    src = sps[k % 4][:, :].rearrange("p (m t) -> p m t", m=4)
                    dst = KT[:, 4 * n:4 * n + 4, i * P:(i + 1) * P] if n < 2 else QS[i % 2][(n - 2) // 2][:, 4 * (n % 2):4 * (n % 2) + 4, :]
                    dve.tensor_copy(dst, src).then_inc(s["sps_read"], 1)

            def rows(n):
                i, h = tile_head[n]
                last = len(chunks[i]) - 1
                if n >= 2:
                    dve.wait_ge(s["weights"], n - 1)
                if n >= 3:
                    dve.wait_ge(s["wT_ps"], first_wt[tile_head[n - 2]])
                for c, (c0, w) in enumerate(chunks[i]):
                    for m in range(2):
                        k = first_sc[i, h] + 2 * c + m
                        dve.wait_ge(s["sps_full"], k + 1)
                        add = mask[:, 4 * P - w:4 * P] if c == last else zero[:, 0:w]
                        red = dve.tensor_tensor_reduce(sc[m][:, n % (3 - m), c0:c0 + w], sps[k % 4][:, 0:w], add, SCALE, -3e38,
                                                       ALU.add, ALU.max, mx[:, n % 2, m, c:c + 1]).then_inc(s["sps_read"], 1)
                dve.wait_ge(s["sps_read"], first_sc[i, h] + 2 * len(chunks[i]))
                if n >= 2:
                    dve.wait_ge(s["exp"], 2 * n - 2)
                dve.tensor_reduce(nmx[:, n % 2, :], mx[:, n % 2, :, 0:last + 1], AX.X, ALU.max, negate=True).then_inc(s["neg_max"], 1)

            def combine(n):
                i, h = tile_head[n]
                dve.wait_ge(s["exp"], 2 * n + 2)
                dve.reciprocal(rl[:, 0, h:h + 1], ls[:, i % 2, 1, h:h + 1]).then_inc(s["recip"], 1)
                dve.wait_ge(s["recip"], n + 1)
                dve.scalar_tensor_tensor(out=coef[:, n % 2:n % 2 + 1], in0=ls[:, i % 2, 0, h:h + 1], scalar=nlam[:, 0:1],
                                         in1=rl[:, 0, h:h + 1], op0=ALU.mult, op1=ALU.mult).then_inc(s["coef"], 1)
                dve.wait_ge(s["coef"], n + 1)
                w = (i + 1) * P
                dve.scalar_tensor_tensor(out=sc[0][:, n % 3, 0:w], in0=sc[1][:, n % 2, 0:w], scalar=coef[:, n % 2:n % 2 + 1],
                                         in1=sc[0][:, n % 3, 0:w], op0=ALU.mult, op1=ALU.add).then_inc(s["weights"], 1)

            def out_rows(i):
                dve.reciprocal(r0[:, :], ls[:, i % 2, 0, :]).then_inc(s["r0"], 1)
                dve.wait_ge(s["r0"], i + 1)
                dve.wait_ge(s["out_ps"], first_wt[i, H - 1] + len(chunks[i]))
                if i >= 2:
                    dve.wait_ge(s["store"][i % 2], 16 * (i // 2))
                dve.tensor_tensor(ob[:, i % 2].rearrange("p (h v) -> p h v", h=H), ops[i % 2][:, :, :],
                                  r0[:, :, None].broadcast_to([P, H, DV]), ALU.mult).then_inc(s["out"], 1)

            dve.wait_ge(s["zero"], 1)
            dve.wait_ge(s["mask_load"], 16)
            prep_out(0)
            for n in range(n_heads + 3):
                if n < n_heads:
                    i, h = tile_head[n]
                    if h == 2 and i + 1 < NP:
                        prep_out(i + 1)
                    rows(n)
                if 1 <= n <= n_heads:
                    combine(n - 1)
                if n >= 3 and tile_head[n - 3][1] == H - 1:
                    out_rows(tile_head[n - 3][0])

        @block.tensor
        def _(pe):
            def prep(i):
                pe.wait_ge(s["k_lo"], i + 1)
                pe.wait_ge(s["q_lo"], i + 1)
                for n in range(6):
                    k = first_prep[i] + n
                    if k >= 4:
                        pe.wait_ge(s["sps_read"], k - 3)
                    for a in range(4):
                        m = 4 * (n % 2) + a
                        if n < 2:
                            src = f32(k_hl[:, m, :, :]).rearrange("p a b -> p (a b)")
                        else:
                            src = f32(q_hl[:, (n - 2) // 2, m]).rearrange("p a b -> p (a b)")
                        mm = pe.transpose(sps[k % 4][:, a * P:(a + 1) * P], src, ident[:, :])
                    mm.then_inc(s["sps_full"], 1)

            def scores(n, c):
                i, h = tile_head[n]
                c0, w = chunks[i][c]
                if c == 0:
                    pe.wait_ge(s["sps_read"], first_prep[i] + 6)
                for m in range(2):
                    k = first_sc[i, h] + 2 * c + m
                    pe.wait_ge(s["sps_read"], k - 3)
                    for part in range(2):
                        mm = pe.matmul(sps[k % 4][:, 0:w], QS[i % 2][part][:, 2 * h + m, :], KT[:, 2 * h + m, c0:c0 + w],
                                       start=(part == 0), stop=(part == 1))
                    mm.then_inc(s["sps_full"], 1)

            def weight_columns(n, c):
                i, h = tile_head[n]
                g = first_wt[i, h] + c
                if c == 0:
                    pe.wait_ge(s["weights"], n + 1)
                if g >= 2:
                    pe.wait_ge(s["wT"], g - 1)
                c0, w = chunks[i][c]
                for b in range(w // P):
                    mm = pe.transpose(tps[g % 2][:, b, :], sc[0][:, n % 3, c0 + b * P:c0 + (b + 1) * P], ident[:, :])
                mm.then_inc(s["wT_ps"], 1)

            def values(n, c):
                i, h = tile_head[n]
                g = first_wt[i, h] + c
                c0, w = chunks[i][c]
                pe.wait_ge(s["wT"], g + 1)
                pe.wait_ge(s[f"v_load{c}"], 16)
                if h == 0 and c == 0 and i >= 2:
                    pe.wait_ge(s["out"], i - 1)
                for b in range(w // P):
                    kb = c0 // P + b
                    mm = pe.matmul(ops[i % 2][:, h, :], WT[:, g % 2, b, :], V[:, kb, h * DV:(h + 1) * DV],
                                   start=(kb == 0), stop=(kb == i))
                mm.then_inc(s["out_ps"], 1)

            prep(0)
            for n in range(n_heads + 2):
                n_s = len(chunks[tile_head[n][0]]) if n < n_heads else 0
                n_v = len(chunks[tile_head[n - 2][0]]) if n >= 2 else 0
                if n_s and tile_head[n][1] == 2 and tile_head[n][0] + 1 < NP:
                    prep(tile_head[n][0] + 1)
                for c in range(max(n_s, n_v)):
                    if c < n_s:
                        scores(n, c)
                    if c < n_v:
                        weight_columns(n - 2, c)
                    if 1 <= c <= n_v:
                        values(n - 2, c - 1)
                if n_v and max(n_s, n_v) == n_v:
                    values(n - 2, n_v - 1)


def pass_lambda(nc, io, keep):
    ident, nlam = keep[0], keep[2]
    with ExitStack() as ctx:
        lam = ctx.enter_context(nc.sbuf_tensor("l_lam", [P, 4, DQ], F32))
        prod = ctx.enter_context(nc.sbuf_tensor("l_prod", [P, 2, DQ], F32))
        red = ctx.enter_context(nc.sbuf_tensor("l_sum", [P, 4], F32))
        load, step, idr = (ctx.enter_context(nc.semaphore("l_" + n)) for n in ("load", "step", "ident"))
        block = open_block(nc, ctx, (load, step, idr))

        @block.gpsimd
        def _(pool):
            make_identity(pool, ident, idr)
            pool.wait_ge(idr, 2)

        @block.sync
        def _(sp):
            for n, name in enumerate(("lambda_q1", "lambda_q2", "lambda_k1", "lambda_k2")):
                sp.dma_start(lam[:, n], io[name].partition_broadcast(P).rearrange("p a b -> p (a b)")).then_inc(load, 16)

        @block.vector
        def _(dve):
            dve.wait_ge(load, 64)
            dve.tensor_tensor(prod[:, :], lam[:, 0:2], lam[:, 2:4], ALU.mult).then_inc(step, 1)
            dve.wait_ge(step, 1)
            dve.tensor_reduce(red[:, 0:2], prod[:, :, :], AX.X, ALU.add).then_inc(step, 1)
            dve.wait_ge(step, 3)
            dve.tensor_tensor(red[:, 2:3], red[:, 1:2], red[:, 0:1], ALU.subtract).then_inc(step, 1)
            dve.wait_ge(step, 4)
            dve.tensor_scalar(nlam[:, 0:1], red[:, 2:3], LAM_INIT, None, ALU.subtract).then_inc(step, 1)
            dve.wait_ge(step, 5)

        @block.scalar
        def _(act):
            act.wait_ge(step, 2)
            act.activation(red[:, 0:2], red[:, 0:2], ACT.Exp).then_inc(step, 1)


def pass_sample_attention(nc, io, keep):
    with ExitStack() as ctx:
        def sb(name, shape, dt=F32):
            return ctx.enter_context(nc.sbuf_tensor("s_" + name, shape, dt))

        def sem(name):
            return ctx.enter_context(nc.semaphore("s_" + name))

        def ps(name, shape):
            return ctx.enter_context(nc.psum_tensor("s_" + name, shape, F32))

        ident, nlam = keep[0], keep[2]
        NK = PAST + DEC_T
        pages = sb("pages", [1, DEC_B * NPG], I32)
        kc = sb("kc", [P, 2, NPG, GW])
        vc = sb("vc", [P, 2, NPG, GW])
        v_new = sb("v_new", [DEC_T, DEC_B, GW])
        qk_new = sb("qk_new", [NS, 2, GW])
        Q = sb("Q", [P, DEC_B, H, 32])
        K_new = sb("K_new", [P, H, NS])
        KT = sb("KT", [P, 2, H, PAST])
        sc = sb("sc", [P, 2, NK])
        PT = sb("PT", [P, 2, NPG + 1, P])
        mask = sb("mask", [P, DEC_T])
        zero = sb("zero", [P, PAST])
        is_map = sb("is_map", [P, 2])
        sign = sb("sign", [P, 1])
        mx = sb("mx", [P, 2, 2])
        nmx = sb("nmx", [P, 2])
        l = sb("l", [P, 2])
        rl = sb("rl", [P, 2])
        coef = sb("coef", [P, 2])
        part = sb("part", [P, 2, DV])
        maps = sb("maps", [NS, 2, H, DV])
        rows = sb("rows", [NS, H * DV])
        tps = [ps(f"tps{n}", [P, 4, P]) for n in range(2)]
        sps = [ps(f"sps{n}", [P, PAST]) for n in range(2)]
        nps = ps("nps", [P, 2, 256])
        pps = [ps(f"pps{n}", [P, 4, P]) for n in range(2)]
        ops = ps("ops", [P, 2, 256])
        s = {n: sem(n) for n in ("pages", "new", "consts", "zero", "sign", "new_ps", "Q", "K_new", "kT_ps", "kT", "scores", "row_max",
                                 "neg_max", "exp", "recip", "coef", "pT_ps", "pT", "outs", "part", "maps", "sum", "store")}
        s["kc"] = [sem(f"kc{p}") for p in range(2)]
        s["vc"] = [sem(f"vc{p}") for p in range(2)]
        s["part_store"] = [sem(f"part_store{p}") for p in range(2)]
        block = open_block(nc, ctx, s.values())

        @block.sync
        def _(sp):
            sp.dma_start(pages[:, :], io["page_table"]).then_inc(s["pages"], 16)
            sp.dma_start(qk_new[:, 0], io["q_s"][NP * P:NP * P + NS, :]).then_inc(s["new"], 16)
            sp.dma_start(qk_new[:, 1], io["k_s"]).then_inc(s["new"], 16)
            sp.dma_start(v_new[:, :, :], io["v_s"].rearrange("(b t) n -> t b n", t=DEC_T)).then_inc(s["new"], 16)
            sp.dma_start(mask[:, :], io["new_mask"]).then_inc(s["consts"], 16)
            sp.dma_start(is_map[:, :], io["is_map"]).then_inc(s["consts"], 16)
            sp.wait_ge(s["pages"], 16)

            def store_part(j):
                sp.wait_ge(s["part"], j + 1)
                sp.dma_start(io["part_s"][j], part[:, j % 2]).then_inc(s["part_store"][j % 2], 16)

            for j in range(DEC_B):
                if j >= 2:
                    store_part(j - 2)
                    sp.wait_ge(s["kT_ps"], 4 * (j - 1))
                    sp.wait_ge(s["outs"], j - 1)
                for g in range(NPG):
                    page = sp.value_load(pages[0:1, j * NPG + g:j * NPG + g + 1], min_val=0, max_val=N_POOL - 1)
                    sp.dma_start(kc[:, j % 2, g], io["cache_k"][bass.ds(page * PAGE, PAGE), :]).then_inc(s["kc"][j % 2], 16)
                    sp.dma_start(vc[:, j % 2, g], io["cache_v"][bass.ds(page * PAGE, PAGE), :]).then_inc(s["vc"][j % 2], 16)
            store_part(DEC_B - 2)
            store_part(DEC_B - 1)
            for p in range(2):
                sp.wait_ge(s["part_store"][p], 16 * DEC_B // 2)
            for j in range(DEC_B):
                for m in range(2):
                    src = io["part_s"][j].rearrange("(h x) v -> x h v", h=H)[m * DEC_T:(m + 1) * DEC_T]
                    sp.dma_start(maps[j * DEC_T:(j + 1) * DEC_T, m], src).then_inc(s["maps"], 16)
            sp.wait_ge(s["sum"], 1)
            sp.dma_start(io["o_s"][NP * P:NP * P + NS, :], rows[:, :]).then_inc(s["store"], 16)
            sp.wait_ge(s["store"], 16)

        @block.gpsimd
        def _(pool):
            pool.memset(Q[:, :, :, :], 0.0).then_inc(s["zero"], 1)
            pool.memset(zero[:, :], 0.0).then_inc(s["zero"], 1)
            pool.wait_ge(s["zero"], 2)

        @block.scalar
        def _(act):
            def keys_out(j):
                for g in range(NPG):
                    act.wait_ge(s["kT_ps"], 4 * j + g + 1)
                    if j >= 2:
                        act.wait_ge(s["scores"], 2 * (j - 1))
                    act.activation(KT[:, j % 2, :, g * PAGE:(g + 1) * PAGE], tps[g % 2][:, :, :], ACT.Copy).then_inc(s["kT"], 1)

            keys_out(0)
            for j in range(DEC_B):
                if j + 1 < DEC_B:
                    keys_out(j + 1)
                act.wait_ge(s["neg_max"], j + 1)
                act.activation(sc[:, j % 2, :], sc[:, j % 2, :], ACT.Exp, bias=nmx[:, j % 2:j % 2 + 1],
                               accum_out=l[:, j % 2:j % 2 + 1]).then_inc(s["exp"], 1)

        @block.vector
        def _(dve):
            dve.wait_ge(s["consts"], 32)
            dve.wait_ge(s["zero"], 2)
            dve.scalar_tensor_tensor(out=sign[:, :], in0=is_map[:, 1:2], scalar=nlam[:, 0:1], in1=is_map[:, 0:1],
                                     op0=ALU.mult, op1=ALU.add).then_inc(s["sign"], 1)
            dve.wait_ge(s["new_ps"], 1)
            for m in range(2):
                r = slice(m * DQ, (m + 1) * DQ)
                for h in range(H):
                    last = dve.tensor_copy(Q[r, :, h, m * DEC_T:(m + 1) * DEC_T],
                                           pps[0][r, h, 0:NS].rearrange("p (b t) -> p b t", b=DEC_B))
            last.then_inc(s["Q"], 1)
            dve.wait_ge(s["new_ps"], 2)
            dve.tensor_copy(K_new[:, :, :], pps[1][:, :, 0:NS]).then_inc(s["K_new"], 1)
            dve.wait_ge(s["sign"], 1)

            def weights_out(j):
                for a in range(2):
                    dve.wait_ge(s["pT_ps"], 2 * j + a + 1)
                    if j >= 2:
                        dve.wait_ge(s["outs"], j - 1)
                    if a == 0:
                        dve.tensor_copy(PT[:, j % 2, 0:NPG], pps[0][:, :, :]).then_inc(s["pT"], 1)
                    else:
                        dve.tensor_copy(PT[0:DEC_T, j % 2, NPG], pps[1][0:DEC_T, 0, :]).then_inc(s["pT"], 1)

            def out_part(j):
                b = j % 2
                dve.wait_ge(s["exp"], j + 1)
                dve.reciprocal(rl[:, b:b + 1], l[:, b:b + 1]).then_inc(s["recip"], 1)
                dve.wait_ge(s["recip"], j + 1)
                dve.tensor_tensor(coef[:, b:b + 1], rl[:, b:b + 1], sign[:, :], ALU.mult).then_inc(s["coef"], 1)
                dve.wait_ge(s["coef"], j + 1)
                dve.wait_ge(s["outs"], j + 1)
                if j >= 2:
                    dve.wait_ge(s["part_store"][b], 16 * (j // 2))
                dve.tensor_scalar(part[:, b], ops[:, b, 0:DV], coef[:, b:b + 1], None, ALU.mult).then_inc(s["part"], 1)

            for j in range(DEC_B + 1):
                if j < DEC_B:
                    b = j % 2
                    dve.wait_ge(s["scores"], 2 * j + 1)
                    if j >= 2:
                        dve.wait_ge(s["pT_ps"], 2 * j - 2)
                    dve.tensor_tensor_reduce(sc[:, b, 0:PAST], sps[b][:, :], zero[:, :], SCALE, -3e38, ALU.add, ALU.max,
                                             mx[:, b, 0:1]).then_inc(s["row_max"], 1)
                    dve.wait_ge(s["scores"], 2 * j + 2)
                    dve.tensor_tensor_reduce(sc[:, b, PAST:NK], nps[:, b, 0:DEC_T], mask[:, :], SCALE, -3e38, ALU.add, ALU.max,
                                             mx[:, b, 1:2]).then_inc(s["row_max"], 1)
                    dve.wait_ge(s["row_max"], 2 * j + 2)
                    if j >= 2:
                        dve.wait_ge(s["exp"], j - 1)
                    dve.tensor_reduce(nmx[:, b:b + 1], mx[:, b, :], AX.X, ALU.max, negate=True).then_inc(s["neg_max"], 1)
                if j >= 1:
                    weights_out(j - 1)
                    out_part(j - 1)
            dve.wait_ge(s["maps"], 16 * 2 * DEC_B)
            dve.tensor_tensor(rows[:, :].rearrange("p (h v) -> p h v", h=H), maps[:, 0], maps[:, 1], ALU.add).then_inc(s["sum"], 1)

        @block.tensor
        def _(pe):
            pe.wait_ge(s["new"], 48)
            for n in range(2):
                for h in range(H):
                    mm = pe.transpose(pps[n][:, h, 0:NS], qk_new[:, n, h * P:(h + 1) * P], ident[0:NS, 0:NS])
                mm.then_inc(s["new_ps"], 1)

            def key_columns(j):
                pe.wait_ge(s["kc"][j % 2], 64 * (j // 2 + 1))
                for g in range(NPG):
                    n = 4 * j + g
                    if n >= 2:
                        pe.wait_ge(s["kT"], n - 1)
                    for h in range(H):
                        mm = pe.transpose(tps[g % 2][:, h, :], kc[:, j % 2, g, h * P:(h + 1) * P], ident[:, :])
                    mm.then_inc(s["kT_ps"], 1)

            def scores(j):
                b = j % 2
                pe.wait_ge(s["kT"], 4 * j + 4)
                if j >= 2:
                    pe.wait_ge(s["row_max"], 2 * j - 2)
                for h in range(H):
                    mm = pe.matmul(sps[b][32 * h:32 * h + 32, :], Q[:, j, h, :], KT[:, b, h, :], start=True, stop=True)
                mm.then_inc(s["scores"], 1)
                if j >= 1:
                    pe.wait_ge(s["row_max"], 2 * j)
                for h in range(H):
                    mm = pe.matmul(nps[32 * h:32 * h + 32, b, 0:DEC_T], Q[:, j, h, :], K_new[:, h, j * DEC_T:(j + 1) * DEC_T],
                                   start=True, stop=True)
                mm.then_inc(s["scores"], 1)

            def weight_columns(j):
                pe.wait_ge(s["exp"], j + 1)
                if j >= 1:
                    pe.wait_ge(s["pT"], 2 * j)
                for g in range(NPG):
                    mm = pe.transpose(pps[0][:, g, :], sc[:, j % 2, g * PAGE:(g + 1) * PAGE], ident[:, :])
                mm.then_inc(s["pT_ps"], 1)
                pe.transpose(pps[1][0:DEC_T, 0, :], sc[:, j % 2, PAST:NK], ident[:, :]).then_inc(s["pT_ps"], 1)

            def values(j):
                b = j % 2
                pe.wait_ge(s["pT"], 2 * j + 2)
                pe.wait_ge(s["vc"][b], 64 * (j // 2 + 1))
                if j >= 1:
                    pe.wait_ge(s["part"], j)
                for h in range(H):
                    out = ops[32 * h:32 * h + 32, b, 0:DV]
                    for g in range(NPG):
                        pe.matmul(out, PT[:, b, g, 32 * h:32 * h + 32], vc[:, b, g, h * DV:(h + 1) * DV], start=(g == 0), stop=False)
                    mm = pe.matmul(out, PT[0:DEC_T, b, NPG, 32 * h:32 * h + 32], v_new[:, j, h * DV:(h + 1) * DV],
                                   start=False, stop=True)
                mm.then_inc(s["outs"], 1)

            key_columns(0)
            pe.wait_ge(s["Q"], 1)
            pe.wait_ge(s["K_new"], 1)
            for j in range(DEC_B + 1):
                if j < DEC_B:
                    scores(j)
                if j >= 1:
                    weight_columns(j - 1)
                    values(j - 1)
                if j + 1 < DEC_B:
                    key_columns(j + 1)


def pass_sample_hgrn(nc, io, keep):
    with ExitStack() as ctx:
        def sb(name, shape, dt=F32):
            return ctx.enter_context(nc.sbuf_tensor("r_" + name, shape, dt))

        def sem(name):
            return ctx.enter_context(nc.semaphore("r_" + name))

        def ps(name, shape):
            return ctx.enter_context(nc.psum_tensor("r_" + name, shape, F32))

        ident = keep[0]
        levels = tuple((n, w) for n, w in enumerate(BLOCKS) if w <= DEC_T)
        n0 = levels[0][0]
        qT, kT, lfT, bT = (sb(n, [P, GW]) for n in ("qT", "kT", "lfT", "bT"))
        v_tok, gate = sb("v_tok", [P, GW]), sb("gate", [P, GW])
        go = sb("go", [P, P])
        lv = sb("lv", [P, SLOTS - n0, GW])
        runs = sb("runs", [P, DEC_B])
        own = sb("own", [P, DEC_B, P])
        S0 = sb("S0", [P, DEC_B, H, DV])
        S1 = sb("S1", [P, DEC_B, H, DV])
        qe = sb("qe", [P, 2, DEC_B, P])
        v_own = sb("v_own", [P, 2, DEC_B, DV])
        ebc = sb("ebc", [P, H, DEC_B])
        mask = sb("mask", [P, NL, P])
        masked = sb("masked", [P, 3, P])
        att = sb("att", [P, H, P])
        kd_tok = sb("kd_tok", [P, GW])
        rows = sb("rows", [P, GW])
        sq = sb("sq", [P, GW])
        oss = sb("oss", [P, 3, H])
        ng = sb("ng", [P, DV])
        eps = sb("eps", [P, 1])
        lps = ps("lps", [P, 4, P])
        tps = ps("tps", [P, 4, P])
        ops = ps("ops", [P, H, DV])
        ups = [[ps(f"ups{a}{b}", [P, 4, DV]) for b in range(2)] for a in range(2)]
        s = {n: sem(n) for n in ("load", "state_load", "eps", "cumsum", "diff", "decay", "ebc", "operands", "levels", "masked", "att",
                                 "kdT_ps", "kd_tok", "qe", "v_own", "av", "gain_ps", "scaled", "state", "o_sq", "o_ss", "o_root",
                                 "o_rs", "o_norm", "o_g", "o_out", "store")}
        block = open_block(nc, ctx, s.values())

        @block.sync
        def _(sp):
            loads = ((lfT[:, :], io["hl_s"]), (go[:, :], io["run_go"]), (qT[:, :], io["hq_s"]), (kT[:, :], io["hk_s"]),
                     (v_tok[:, :], io["hv_s"]), (gate[:, :], io["hg_s"]), (mask[:, :, :], io["level_mask"]),
                     (runs[:, :], io["runs"]), (own[:, :, :], io["own"]),
                     (ng[:, :], io["hgrn_norm_g"].partition_broadcast(P).rearrange("p a b -> p (a b)")))
            for dst, src in loads:
                sp.dma_start(dst, src).then_inc(s["load"], 16)
            sp.dma_start(S0[:, :, :, :].rearrange("p b h v -> p (b h) v"), io["state"].rearrange("b h d v -> d (b h) v")).then_inc(s["state_load"], 16)
            sp.wait_ge(s["state"], H)
            sp.dma_start(io["s_s"].rearrange("b h d v -> d (b h) v"), S1[:, :, :, :].rearrange("p b h v -> p (b h) v")).then_inc(s["store"], 16)
            sp.wait_ge(s["o_out"], 1)
            sp.dma_start(io["mr_s"][NP * P:NP * P + NS, :], rows[0:NS, :]).then_inc(s["store"], 16)
            sp.wait_ge(s["store"], 32)

        @block.gpsimd
        def _(pool):
            pool.wait_ge(s["decay"], 1)
            decay_products(pool, lv, qT[:, :], kT[:, :], levels, n0).then_inc(s["operands"], 1)
            for h in range(H):
                if h >= 2:
                    pool.wait_ge(s["gain_ps"], h - 1)
                pool.tensor_tensor(v_own[:, h % 2], v_tok[:, None, h * DV:(h + 1) * DV].broadcast_to([P, DEC_B, DV]),
                                   runs[:, :, None].broadcast_to([P, DEC_B, DV]), ALU.mult).then_inc(s["v_own"], 1)
            pool.wait_ge(s["o_norm"], 1)
            r3 = rows[:, :].rearrange("p (h v) -> p h v", h=H)
            pool.tensor_tensor(r3, r3, ng[:, None, :].broadcast_to([P, H, DV]), ALU.mult).then_inc(s["o_g"], 1)
            pool.wait_ge(s["o_g"], 1)
            pool.tensor_tensor(rows[:, :], rows[:, :], gate[:, :], ALU.mult).then_inc(s["o_out"], 1)

        @block.scalar
        def _(act):
            act.wait_ge(s["diff"], 1)
            act.activation(lv[:, :, :], lv[:, :, :], ACT.Exp).then_inc(s["decay"], 1)
            act.activation(ebc[:, :, :], bT[:, :].rearrange("p (h b t) -> p h b t", h=H, t=DEC_T)[:, :, 0:DEC_B, DEC_T - 1],
                           ACT.Exp).then_inc(s["ebc"], 1)
            act.wait_ge(s["kdT_ps"], 1)
            act.activation(kd_tok[:, :], tps[:, :, :].rearrange("p h d -> p (h d)"), ACT.Copy).then_inc(s["kd_tok"], 1)
            act.wait_ge(s["av"], H)
            act.wait_ge(s["eps"], 1)
            act.activation(sq[:, :], ops[:, :, :].rearrange("p h v -> p (h v)"), ACT.Square).then_inc(s["o_sq"], 1)
            act.wait_ge(s["o_ss"], 1)
            act.activation(oss[:, 1], oss[:, 0], ACT.Sqrt, bias=eps[:, 0:1], scale=1.0 / DV).then_inc(s["o_root"], 1)

        @block.vector
        def _(dve):
            dve.memset(eps[:, :], EPS).then_inc(s["eps"], 1)
            dve.wait_ge(s["load"], 160)
            for h in range(H):
                cols = slice(h * P, (h + 1) * P)
                last = dve.tensor_tensor_scan(bT[:, cols], go[:, :], lfT[:, cols], 0.0, ALU.mult, ALU.add)
            last.then_inc(s["cumsum"], 1)
            dve.wait_ge(s["cumsum"], 1)
            decay_differences(dve, bT[:, :], lv, levels, DEC_T, n0).then_inc(s["diff"], 1)
            dve.wait_ge(s["operands"], 1)
            for h in range(H):
                dve.wait_ge(s["levels"], h + 1)
                dve.wait_ge(s["att"], h)
                dve.tensor_tensor(masked[:, :, :], lps[:, 0:3, :], mask[:, n0:, :], ALU.mult).then_inc(s["masked"], 1)
                dve.wait_ge(s["masked"], h + 1)
                dve.tensor_reduce(att[:, h], masked[:, :, :].rearrange("p l t -> p t l"), AX.X, ALU.add).then_inc(s["att"], 1)
                if h >= 2:
                    dve.wait_ge(s["av"], h - 1)
                dve.tensor_tensor(qe[:, h % 2], lv[:, LEAF_QE - n0, None, h * P:(h + 1) * P].broadcast_to([P, DEC_B, P]), own[:, :, :],
                                  ALU.mult).then_inc(s["qe"], 1)
            dve.wait_ge(s["state_load"], 16)
            dve.wait_ge(s["ebc"], 1)
            for h in range(H):
                dve.tensor_tensor(S1[:, :, h], S0[:, :, h], ebc[:, h, :, None].broadcast_to([P, DEC_B, DV]), ALU.mult).then_inc(s["scaled"], 1)
                dve.wait_ge(s["scaled"], h + 1)
                dve.wait_ge(s["gain_ps"], h + 1)
                for b in range(2):
                    last = dve.tensor_tensor(S1[:, 4 * b:4 * b + 4, h], S1[:, 4 * b:4 * b + 4, h], ups[h % 2][b][:, :, :], ALU.add)
                last.then_inc(s["state"], 1)
            r3 = rows[:, :].rearrange("p (h v) -> p h v", h=H)
            dve.wait_ge(s["o_sq"], 1)
            dve.tensor_reduce(oss[:, 0], sq[:, :].rearrange("p (h v) -> p h v", h=H), AX.X, ALU.add).then_inc(s["o_ss"], 1)
            dve.wait_ge(s["o_root"], 1)
            dve.reciprocal(oss[:, 2], oss[:, 1]).then_inc(s["o_rs"], 1)
            dve.wait_ge(s["o_rs"], 1)
            dve.tensor_tensor(r3, ops[:, :, :], oss[:, 2, :, None].broadcast_to([P, H, DV]), ALU.mult).then_inc(s["o_norm"], 1)

        @block.tensor
        def _(pe):
            pe.wait_ge(s["operands"], 1)
            for h in range(H):
                mm = pe.transpose(tps[:, h, :], lv[:, LEAF_KD - n0, h * P:(h + 1) * P], ident[:, :])
            mm.then_inc(s["kdT_ps"], 1)

            def products(h):
                c = slice(h * P, (h + 1) * P)
                if h >= 1:
                    pe.wait_ge(s["masked"], h)
                for a, (n, _) in enumerate(levels):
                    pe.matmul(lps[:, a, :], lv[:, n - n0, c], lv[:, n - n0, c], start=True, stop=True)
                pe.matmul(lps[:, 2, :], lv[:, LEAF_K - n0, c], lv[:, LEAF_Q - n0, c], start=True, stop=True).then_inc(s["levels"], 1)

            products(0)
            for h in range(H):
                if h + 1 < H:
                    products(h + 1)
                pe.wait_ge(s["att"], h + 1)
                pe.wait_ge(s["qe"], h + 1)
                pe.wait_ge(s["state_load"], 16)
                pe.matmul(ops[:, h, :], att[:, h, :], v_tok[:, h * DV:(h + 1) * DV], start=True, stop=False)
                for b in range(DEC_B):
                    mm = pe.matmul(ops[:, h, :], qe[:, h % 2, b, :], S0[:, b, h, :], start=False, stop=(b == DEC_B - 1))
                mm.then_inc(s["av"], 1)
            pe.wait_ge(s["kd_tok"], 1)
            for h in range(H):
                pe.wait_ge(s["v_own"], h + 1)
                if h >= 2:
                    pe.wait_ge(s["state"], h - 1)
                for b in range(2):
                    mm = pe.matmul(ups[h % 2][b][:, :, :].rearrange("p b v -> p (b v)"), kd_tok[:, h * P:(h + 1) * P],
                                   v_own[:, h % 2, 4 * b:4 * b + 4, :].rearrange("p b v -> p (b v)"), start=True, stop=True)
                mm.then_inc(s["gain_ps"], 1)


def pass_output(nc, io, keep):
    with ExitStack() as ctx:
        def sb(name, shape, dt=F32):
            return ctx.enter_context(nc.sbuf_tensor("y_" + name, shape, dt))

        def sem(name):
            return ctx.enter_context(nc.semaphore("y_" + name))

        def ps(name, shape):
            return ctx.enter_context(nc.psum_tensor("y_" + name, shape, F32))

        ident = keep[0]
        w_hi, w_lo = sb("w_hi", [P, KD, D], F32R), sb("w_lo", [P, KD, D], F32R)
        stage = sb("stage", [P, 2, KD, GW])
        o_in, ga, mr = (sb(n, [P, 2, GW]) for n in ("o_in", "ga", "mr"))
        xt = sb("xt", [P, 2, D])
        yt = sb("yt", [P, 2, D])
        sq = sb("sq", [P, GW])
        oss = sb("oss", [P, 3, H])
        ng = sb("ng", [P, 2, DV])
        eps = sb("eps", [P, 1])
        mT_hi = [sb(f"mT_hi{p}", [P, KD, P], F32R) for p in range(2)]
        mT_lo = [sb(f"mT_lo{p}", [P, KD, P], F32R) for p in range(2)]
        yps = [[ps(f"yps{p}{g}", [P, GW]) for g in range(2)] for p in range(2)]
        tps = [ps(f"tps{b}", [P, 4, P]) for b in range(2)]
        s = {n: sem(n) for n in ("w_hi", "w_lo", "ng", "ng_scaled", "eps", "o_sq", "o_ss", "o_root", "o_rs", "o_norm",
                                 "o_g", "gated", "mT_ps", "mT_hi", "mT_lo", "y_ps", "y")}
        for n in ("w_load", "o_load", "ga_load", "mr_load", "x_load", "store"):
            s[n] = [sem(f"{n}{p}") for p in range(2)]
        block = open_block(nc, ctx, s.values())

        def over_tiles(eng, step):
            step(0, 0, 0, True)
            step(1, 1, 0, True)
            with eng.Fori(1, NP // 2) as j:
                for p in range(2):
                    step(j * 2 + p, p, j, True)
            step(NP, 0, NP // 2, False)

        @block.sync
        def _(sp):
            def load(i, p, rows=P):
                r = bass.ds(i * P, rows)
                sp.dma_start(o_in[0:rows, p], io["o_s"][r, :]).then_inc(s["o_load"][p], 16)
                sp.dma_start(ga[0:rows, p], io["ga_s"][r, :]).then_inc(s["ga_load"][p], 16)
                sp.dma_start(mr[0:rows, p], io["mr_s"][r, :]).then_inc(s["mr_load"][p], 16)

            def load_x(i, p, rows=P):
                sp.dma_start(xt[0:rows, p], io["x"][bass.ds(i * P, rows), :]).then_inc(s["x_load"][p], 16)

            sp.dma_start(ng[:, 0], io["subln_g"].partition_broadcast(P).rearrange("p a b -> p (a b)")).then_inc(s["ng"], 16)
            load(0, 0)
            for g in range(2):
                sp.dma_start(stage[:, g], io["w_out"].rearrange("(k p) n -> p k n", p=P)[:, :, g * GW:(g + 1) * GW]).then_inc(s["w_load"][g], 16)
            load(1, 1)
            load_x(0, 0)
            load_x(1, 1)

            def store(i, p, rows, dst):
                sp.wait_ge(s["y"], 2 * i + 2)
                sp.dma_start(dst, yt[0:rows, p]).then_inc(s["store"][p], 16)

            with sp.Fori(0, NP // 2 - 1) as j:
                for p in range(2):
                    i = j * 2 + p
                    sp.wait_ge(s["mT_ps"], 2 * i + 2)
                    load(i + 2, p)
                    store(i, p, P, io["y_p"][bass.ds(i * P, P), :])
                    load_x(i + 2, p)
            sp.wait_ge(s["mT_ps"], 2 * NP - 2)
            load(NP, 0, NS)
            store(NP - 2, 0, P, io["y_p"][(NP - 2) * P:(NP - 1) * P, :])
            load_x(NP, 0, NS)
            store(NP - 1, 1, P, io["y_p"][(NP - 1) * P:NP * P, :])
            store(NP, 0, NS, io["y_s"])
            sp.wait_ge(s["store"][0], 16 * (NP // 2 + 1))
            sp.wait_ge(s["store"][1], 16 * (NP // 2))

        @block.gpsimd
        def _(pool):
            def gates(i, p, j):
                o3 = o_in[:, p].rearrange("p (h v) -> p h v", h=H)
                pool.wait_ge(s["o_norm"], i + 1)
                pool.tensor_tensor(o3, o3, ng[:, 1, None, :].broadcast_to([P, H, DV]), ALU.mult).then_inc(s["o_g"], 1)
                pool.wait_ge(s["o_g"], i + 1)
                pool.wait_ge(s["ga_load"][p], j * 16 + 16)
                pool.tensor_tensor(o_in[:, p], o_in[:, p], ga[:, p], ALU.mult).then_inc(s["gated"], 1)

            pool.wait_ge(s["ng_scaled"], 1)
            over_tiles(pool, lambda i, p, j, more: gates(i, p, j))

        @block.scalar
        def _(act):
            def squares(i, p, load):
                act.wait_ge(s["o_load"][p], load)
                after(act, s["o_ss"], i)
                act.activation(sq[:, :], o_in[:, p], ACT.Square).then_inc(s["o_sq"], 1)
                act.wait_ge(s["o_ss"], i + 1)
                act.activation(oss[:, 1], oss[:, 0], ACT.Sqrt, bias=eps[:, 0:1], scale=1.0 / DV).then_inc(s["o_root"], 1)

            def hi_parts(i, p):
                for b in range(2):
                    act.wait_ge(s["mT_ps"], 2 * i + b + 1)
                    act.activation(mT_hi[p][:, 4 * b:4 * b + 4, :], tps[b][:, :, :], ACT.Copy).then_inc(s["mT_hi"], 1)

            def step(i, p, j, more):
                if more:
                    squares(i + 1, 1 - p, (j + p) * 16 + 16)
                    hi_parts(i + 1, 1 - p)

            act.wait_ge(s["eps"], 1)
            squares(0, 0, 16)
            for g in range(2):
                act.wait_ge(s["w_load"][g], 16)
                act.activation(w_hi[:, :, g * GW:(g + 1) * GW], stage[:, g], ACT.Copy).then_inc(s["w_hi"], 1)
                if g == 0:
                    hi_parts(0, 0)
            over_tiles(act, step)

        @block.vector
        def _(dve):
            def norm(i, p):
                o3 = o_in[:, p].rearrange("p (h v) -> p h v", h=H)
                dve.wait_ge(s["o_sq"], i + 1)
                dve.tensor_reduce(oss[:, 0], sq[:, :].rearrange("p (h v) -> p h v", h=H), AX.X, ALU.add).then_inc(s["o_ss"], 1)
                dve.wait_ge(s["o_root"], i + 1)
                dve.reciprocal(oss[:, 2], oss[:, 1]).then_inc(s["o_rs"], 1)
                dve.wait_ge(s["o_rs"], i + 1)
                dve.tensor_tensor(o3, o3, oss[:, 2, :, None].broadcast_to([P, H, DV]), ALU.mult).then_inc(s["o_norm"], 1)

            def lo_parts(i, p):
                for b in range(2):
                    dve.wait_ge(s["mT_hi"], 2 * i + b + 1)
                    dve.tensor_tensor(mT_lo[p][:, 4 * b:4 * b + 4, :], tps[b][:, :, :],
                                      f32(mT_hi[p][:, 4 * b:4 * b + 4, :]), ALU.subtract).then_inc(s["mT_lo"], 1)

            def step(i, p, j, more):
                if more:
                    norm(i + 1, 1 - p)
                    lo_parts(i + 1, 1 - p)
                dve.wait_ge(s["x_load"][p], j * 16 + 16)
                after(dve, s["store"][p], j * 16)
                for g in range(2):
                    dve.wait_ge(s["y_ps"], 2 * i + g + 1)
                    dve.tensor_tensor(yt[:, p, g * GW:(g + 1) * GW], yps[p][g][:, :], xt[:, p, g * GW:(g + 1) * GW],
                                      ALU.add).then_inc(s["y"], 1)

            dve.memset(eps[:, :], EPS).then_inc(s["eps"], 1)
            dve.wait_ge(s["ng"], 16)
            dve.tensor_scalar(ng[:, 1], ng[:, 0], 1.0 - LAM_INIT, None, ALU.mult).then_inc(s["ng_scaled"], 1)
            norm(0, 0)
            for g in range(2):
                dve.wait_ge(s["w_hi"], g + 1)
                cols = slice(g * GW, (g + 1) * GW)
                dve.tensor_tensor(w_lo[:, :, cols], stage[:, g], f32(w_hi[:, :, cols]), ALU.subtract).then_inc(s["w_lo"], 1)
                if g == 0:
                    lo_parts(0, 0)
            over_tiles(dve, step)

        @block.tensor
        def _(pe):
            def columns(i, p, load):
                after(pe, s["mT_lo"], 2 * i)
                pe.wait_ge(s["mr_load"][p], load)
                for b, src in ((0, o_in), (1, mr)):
                    if b == 0:
                        pe.wait_ge(s["gated"], i + 1)
                    for k in range(4):
                        mm = pe.transpose(tps[b][:, k, :], src[:, p, k * P:(k + 1) * P], ident[:, :])
                    mm.then_inc(s["mT_ps"], 1)

            def step(i, p, j, more):
                pe.wait_ge(s["mT_lo"], 2 * i + 2)
                for g in range(2):
                    if isinstance(i, int) and i == 0:
                        pe.wait_ge(s["w_lo"], g + 1)
                    after(pe, s["y"], 4 * j)
                    product3(pe, yps[p][g][:, :], mT_hi[p], mT_lo[p], w_hi, w_lo, slice(g * GW, (g + 1) * GW)).then_inc(s["y_ps"], 1)
                    if g == 0 and more:
                        columns(i + 1, 1 - p, (j + p) * 16 + 16)

            columns(0, 0, 16)
            over_tiles(pe, step)


def build_program(nc, io):
    with ExitStack() as ctx:
        ident = ctx.enter_context(nc.sbuf_tensor("ident", [P, P], F32))
        rstd = ctx.enter_context(nc.sbuf_tensor("rstd", [P, 32], F32))
        nlam = ctx.enter_context(nc.sbuf_tensor("nlam", [P, 16], F32))
        keep = (ident, rstd, nlam)
        pass_lambda(nc, io, keep)
        pass_attention_inputs(nc, io, keep)
        pass_hgrn(nc, io, keep)
        pass_sample_hgrn(nc, io, keep)
        pass_attention(nc, io, keep)
        pass_sample_attention(nc, io, keep)
        pass_output(nc, io, keep)


def rotary_table():
    inv = (np.float32(500000.0) ** (-np.arange(0, 2 * HALF, 2, dtype=np.float32) / np.float32(2 * HALF))).astype(np.float32)
    pos = np.concatenate([np.arange(SEQ), PAST + np.tile(np.arange(DEC_T), DEC_B), np.zeros(P - NS)]).astype(np.float32)
    ang = (pos[:, None] * inv[None, :]).astype(np.float32)
    c, n = np.cos(ang), np.sin(ang)
    table = np.concatenate([c, c, -n, n], axis=1).astype(np.float32)
    return np.ascontiguousarray(table.reshape(NT, P, 4 * HALF).transpose(1, 0, 2))


def shape_constants():
    t = np.arange(P)
    level = np.zeros((P, NL, P), np.float32)
    for n, w in enumerate(BLOCKS):
        same = (t[:, None] // w) == (t[None] // w)
        level[:, n] = same & (t[:, None] % w < w // 2) & (t[None] % w >= w // 2)
    level[:, NL - 1] = (t[:, None] // 2 == t[None] // 2) & (t[:, None] <= t[None])
    causal = np.zeros((P, 4 * P), np.float32)
    causal[:, 3 * P:] = np.where(t[None] > t[:, None], NEG, 0.0)
    new_mask = np.where(np.arange(DEC_T)[None] > (t % DEC_T)[:, None], NEG, 0.0).astype(np.float32)
    is_map = np.stack([(t % 32) // DEC_T == 0, (t % 32) // DEC_T == 1], 1).astype(np.float32)
    return {
        "rope": rotary_table(), "level_mask": level, "causal": causal, "new_mask": new_mask, "is_map": is_map,
        "run_go": np.tile((t % DEC_T != 0).astype(np.float32)[None], (P, 1)),
        "runs": (t[:, None] // DEC_T == np.arange(DEC_B)[None]).astype(np.float32),
        "own": np.tile((t[None] // DEC_T == np.arange(DEC_B)[:, None]).astype(np.float32)[None], (P, 1, 1)),
    }


_OUTS = {"y_p": (SEQ, D), "y_s": (NS, D), "k_p": (SEQ, GW), "v_p": (SEQ, GW), "s_p": (H, P, DV),
         "k_s": (NS, GW), "v_s": (NS, GW), "s_s": (DEC_B, H, P, DV)}
_SCRATCH = {"q_s": (NT * P, GW), "ga_s": (NT * P, GW), "o_s": (NT * P, GW), "mr_s": (NT * P, GW), "part_s": (DEC_B, P, DV),
            "hq_s": (P, GW), "hk_s": (P, GW), "hl_s": (P, GW), "hv_s": (P, GW), "hg_s": (P, GW)}


def kernel(**inputs):
    import concourse.bacc as _bacc
    from concourse.bass_utils import run_bass_kernel_spmd as _run

    a = {k: np.asarray(v) for k, v in inputs.items()}
    arrays = {
        "x": np.concatenate([a["x_prompt"].reshape(SEQ, D), a["x_sample"].reshape(NS, D), np.zeros((P - NS, D), np.float32)]),
        "cache_k": a["cache_k"].reshape(N_POOL * PAGE, GW),
        "cache_v": a["cache_v"].reshape(N_POOL * PAGE, GW),
        "state": a["state_hgrn"].reshape(DEC_B, H, P, DV),
        "page_table": a["page_table"].reshape(1, DEC_B * NPG),
        "norm_g": a["norm_g"].reshape(KD, P).T,
        "w_in": a["w_in"].reshape(D, NG * GW),
        "lb": a["hgrn_lb_logits"].reshape(2, H, P).transpose(2, 0, 1),
        "w_out": a["w_out"].reshape(D, D),
    }
    for name in ("q_norm_g", "k_norm_g", "lambda_q1", "lambda_k1", "lambda_q2", "lambda_k2", "subln_g", "hgrn_norm_g"):
        arrays[name] = a[name]
    arrays.update(shape_constants())
    nc = _bacc.Bacc("TRN2", target_bir_lowering=False, num_devices=1)
    io, fed = {}, {}
    for name, v in arrays.items():
        v = np.ascontiguousarray(v)
        fed[f"in_{name}"] = v
        io[name] = nc.dram_tensor(f"in_{name}", v.shape, mybir.dt.from_np(v.dtype), kind="ExternalInput").ap()
    for name, shape in _OUTS.items():
        io[name] = nc.dram_tensor(f"out_{name}", shape, F32, kind="ExternalOutput").ap()
    for name, shape in _SCRATCH.items():
        io[name] = nc.dram_tensor(f"tmp_{name}", shape, F32, kind="Internal").ap()
    build_program(nc, io)
    r = _run(nc, [fed], core_ids=[0]).results[0]
    o = {name: r[f"out_{name}"] for name in _OUTS}
    return (o["y_p"].reshape(1, SEQ, D), o["y_s"].reshape(DEC_B, DEC_T, D),
            o["k_p"].reshape(1, 1, SEQ, H, P), o["v_p"].reshape(1, 1, SEQ, H, DV), o["s_p"].reshape(1, 1, H, P, DV),
            o["k_s"].reshape(1, DEC_B, DEC_T, H, P), o["v_s"].reshape(1, DEC_B, DEC_T, H, DV),
            o["s_s"].reshape(1, DEC_B, H, P, DV))
```

```python
from contextlib import ExitStack

import numpy as np

import concourse.bass as bass
from concourse import mybir

ALU = mybir.AluOpType
ACT = mybir.ActivationFunctionType
AX = mybir.AxisListType
F32 = mybir.dt.float32
F32R = mybir.dt.float32r
BF16 = mybir.dt.bfloat16
I32 = mybir.dt.int32

P = 128
D = 1024
KD = D // P
SEQ, DEC_B, DEC_T = 2048, 8, 8
NS = DEC_B * DEC_T
NP = SEQ // P
NT = NP + 1
GW = 512
NG = 8
H = 4
DQ = 64
DV = 128
HALF = 8
PAST, PAGE = 512, 128
NPG = PAST // PAGE
N_POOL = 40
EPS = 1e-6
LAM_INIT = 0.2
SCALE = DQ ** -0.5


def f32(ap):
    return ap.bitcast(F32)


def handles(sems):
    for x in sems:
        if isinstance(x, (list, tuple)):
            yield from handles(x)
        else:
            yield x


def clear_semaphores(nc, sems):
    nums = sorted(x.num for x in handles(sems))
    while nums:
        n = 1
        while n < len(nums) and nums[n] == nums[0] + n:
            n += 1
        nc.all_engine_barrier(sems_to_clear=range(nums[0], nums[0] + n))
        nums = nums[n:]


def open_block(nc, ctx, sems):
    ctx.callback(clear_semaphores, nc, sems)
    return ctx.enter_context(nc.Block())


PIECES = 4
PB = KD // PIECES


def split_weights(kind, eng, pieces, s, bufs):
    stage, wg, w_hi, w_lo = bufs

    for n in pieces:
        b = n % PIECES
        ks, cols = slice(b * PB, b * PB + PB), slice(n // PIECES * GW, n // PIECES * GW + GW)
        if kind == "pool":
            if n == 0:
                eng.wait_ge(s["w_norm"], 16)
            eng.wait_ge(s["w_staged"][b], 16 * (n // PIECES + 1))
            eng.tensor_tensor(stage[b], stage[b], wg[:, ks, None].broadcast_to([P, PB, GW]), ALU.mult).then_inc(s["w_scaled"], 1)
        elif kind == "act":
            eng.wait_ge(s["w_scaled"], n + 1)
            eng.activation(w_hi[:, ks, cols], stage[b], ACT.Copy).then_inc(s["w_hi"], 1)
        else:
            eng.wait_ge(s["w_scaled"], n + 1)
            eng.wait_ge(s["w_hi"], n + 1)
            eng.tensor_tensor(w_lo[:, ks, cols], stage[b], f32(w_hi[:, ks, cols]), ALU.subtract).then_inc(s["w_lo"], 1)


def stage_weights(eng, w_dram, first_col, s, bufs):
    stage = bufs[0]
    for n in range(4 * PIECES):
        if n >= PIECES:
            eng.wait_ge(s["w_lo"], n - PIECES + 1)
        b, col = n % PIECES, first_col + n // PIECES * GW
        src = w_dram.rearrange("(k p) n -> p k n", p=P)[:, PB * b:PB * b + PB, col:col + GW]
        eng.dma_start(stage[b], src).then_inc(s["w_staged"][b], 16)


def after(eng, sem, count):
    if not isinstance(count, int) or count > 0:
        eng.wait_ge(sem, count)


def product3(eng, out, x_hi, x_lo, w_hi, w_lo, cols, halves=(0, 1)):
    for k in range(KD // 2 * halves[0], KD // 2 * (halves[-1] + 1)):
        for a, b in ((x_hi, w_hi), (x_hi, w_lo), (x_lo, w_hi)):
            mm = eng.matmul(out, a[:, k, :], b[:, k, cols], start=(k == 0 and a is x_hi and b is w_hi),
                            stop=(k == KD - 1 and a is x_lo))
    return mm


def make_identity(pool, ident, done):
    pool.memset(ident[:, :], 0.0).then_inc(done, 1)
    pool.wait_ge(done, 1)
    pool.affine_select(out=ident[:, :], in_=ident[:, :], compare_op=ALU.not_equal, fill=1.0, base=0,
                       pattern=[[-1, P]], channel_multiplier=1).then_inc(done, 1)


def pass_attention_inputs(nc, io, keep):
    with ExitStack() as ctx:
        def sb(name, shape, dt=F32):
            return ctx.enter_context(nc.sbuf_tensor("a_" + name, shape, dt))

        def sem(name):
            return ctx.enter_context(nc.semaphore("a_" + name))

        w_hi = sb("w_hi", [P, KD, 4 * GW], F32R)
        w_lo = sb("w_lo", [P, KD, 4 * GW], F32R)
        stage_all = sb("stage", [P, PIECES, PB, GW])
        stage = [stage_all[:, b] for b in range(PIECES)]
        wg = sb("wg", [P, KD])
        xt = sb("xt", [P, 2, D])
        xT_hi = [sb(f"xT_hi{p}", [P, KD, P], F32R) for p in range(2)]
        xT_lo = [sb(f"xT_lo{p}", [P, KD, P], F32R) for p in range(2)]
        lam, lam_prod, lam_sum = sb("lam", [P, 4, DQ]), sb("lam_prod", [P, 2, DQ]), sb("lam_sum", [P, 4])
        ident, rstd, nlam = keep
        rope = sb("rope", [P, NT, 4 * HALF])
        qkg = sb("qkg", [P, 2, DQ])
        eps = sb("eps", [P, 1])
        ssx = sb("ssx", [P, 4])
        sq = sb("sq", [P, 2 * GW])
        ss = sb("ss", [P, 3, 16])
        qk = sb("qk", [P, 2, 16, DQ])
        rot = sb("rot", [P, 2, 16, 2 * HALF])
        vb = sb("vb", [P, 2, GW])
        gb = sb("gb", [P, 2, GW])
        proj = [ctx.enter_context(nc.psum_tensor(f"a_proj{g}", [P, GW], F32)) for g in range(4)]
        xps = [ctx.enter_context(nc.psum_tensor(f"a_xps{b}", [P, 4, P], F32)) for b in range(2)]

        s = {n: sem(n) for n in ("w_norm", "w_scaled", "w_hi", "w_lo", "consts", "eps", "x_ss", "x_root",
                                 "x_rs", "x_norm", "xT_ps", "xT_hi", "xT_lo", "qk_sq", "qk_ss", "qk_root", "qk_rs",
                                 "qk_norm", "qk_g", "qk_t1", "qk_t2", "qk_rot", "v_ready", "g_ready",
                                 "ident", "lam_load", "lam")}
        s["w_staged"] = [sem(f"w_staged{b}") for b in range(PIECES)]
        s["x_load"] = [sem(f"x_load{p}") for p in range(2)]
        s["proj"] = [sem(f"proj{g}") for g in range(4)]
        s["store"] = [[sem(f"store{n}{p}") for p in range(2)] for n in range(4)]
        bufs = (stage, wg, w_hi, w_lo)
        block = open_block(nc, ctx, s.values())

        def over_tiles(eng, step):
            step(0, 0, 0)
            step(1, 0, 1)
            with eng.Fori(1, NP // 2) as j:
                for p in range(2):
                    step(j * 2 + p, j, p)

        @block.sync
        def _(sp):
            sp.dma_start(wg[:, :], io["norm_g"]).then_inc(s["w_norm"], 16)
            for p in range(2):
                sp.dma_start(xt[:, p], io["x"][p * P:(p + 1) * P, :]).then_inc(s["x_load"][p], 16)
            stage_weights(sp, io["w_in"], 0, s, bufs)
            sp.dma_start(rope[:, :, :], io["rope"]).then_inc(s["consts"], 16)
            for n, name in enumerate(("q_norm_g", "k_norm_g")):
                sp.dma_start(qkg[:, n], io[name].partition_broadcast(P).rearrange("p a b -> p (a b)")).then_inc(s["consts"], 16)

            for n, name in enumerate(("lambda_q1", "lambda_q2", "lambda_k1", "lambda_k2")):
                sp.dma_start(lam[:, n], io[name].partition_broadcast(P).rearrange("p a b -> p (a b)")).then_inc(s["lam_load"], 16)

            def stores(i, j, p, rows, dst_q, dst_k, dst_v, dst_g):
                sp.wait_ge(s["qk_rot"], i + 1)
                sp.dma_start(dst_q, qk[0:rows, p, 0:8].rearrange("p a b -> p (a b)")).then_inc(s["store"][0][p], 16)
                sp.dma_start(dst_k, qk[0:rows, p, 8:16].rearrange("p a b -> p (a b)")).then_inc(s["store"][1][p], 16)
                sp.wait_ge(s["v_ready"], i + 1)
                sp.dma_start(dst_v, vb[0:rows, p]).then_inc(s["store"][2][p], 16)
                sp.wait_ge(s["g_ready"], i + 1)
                sp.dma_start(dst_g, gb[0:rows, p]).then_inc(s["store"][3][p], 16)

            def prompt_stores(i, j, p):
                r = bass.ds(i * P, P)
                stores(i, j, p, P, io["q_s"][r, :], io["k_p"][r, :], io["v_p"][r, :], io["ga_s"][r, :])

            with sp.Fori(0, NP // 2 - 1) as j:
                for p in range(2):
                    i = j * 2 + p
                    sp.wait_ge(s["xT_ps"], 2 * (i + 1))
                    sp.dma_start(xt[:, p], io["x"][bass.ds((i + 2) * P, P), :]).then_inc(s["x_load"][p], 16)
                    prompt_stores(i, j, p)
            for i in (NP - 2, NP - 1):
                if i == NP - 2:
                    sp.wait_ge(s["xT_ps"], 2 * (i + 1))
                    sp.dma_start(xt[:, 0], io["x"][NP * P:NT * P, :]).then_inc(s["x_load"][0], 16)
                prompt_stores(i, i // 2, i % 2)
            r = slice(NP * P, NP * P + NS)
            stores(NP, NP // 2, 0, NS, io["q_s"][r, :], io["k_s"], io["v_s"], io["ga_s"][r, :])
            for n in range(4):
                sp.wait_ge(s["store"][n][0], 16 * (NP // 2 + 1))
                sp.wait_ge(s["store"][n][1], 16 * (NP // 2))

        @block.gpsimd
        def _(pool):
            make_identity(pool, ident, s["ident"])
            split_weights("pool", pool, range(4 * PIECES), s, bufs)
            pool.wait_ge(s["consts"], 48)

            def rotate(i, p):
                q = qk[:, p]
                pool.wait_ge(s["qk_norm"], 2 * i + 2)
                pool.tensor_tensor(q.rearrange("p (a h) d -> p a h d", a=2), q.rearrange("p (a h) d -> p a h d", a=2),
                                   qkg[:, :, None, :].broadcast_to([P, 2, 8, DQ]), ALU.mult).then_inc(s["qk_g"], 1)
                pool.wait_ge(s["qk_g"], i + 1)
                tile = rope[:, bass.ds(i, 1), :] if not isinstance(i, int) else rope[:, i:i + 1, :]
                cc = tile[:, :, 0:2 * HALF].broadcast_to([P, 16, 2 * HALF])
                lo = tile[:, :, 2 * HALF:3 * HALF].broadcast_to([P, 16, HALF])
                hi = tile[:, :, 3 * HALF:4 * HALF].broadcast_to([P, 16, HALF])
                pool.tensor_tensor(rot[:, 0], q[:, :, 0:2 * HALF], cc, ALU.mult).then_inc(s["qk_t1"], 1)
                pool.tensor_tensor(rot[:, 1, :, 0:HALF], q[:, :, HALF:2 * HALF], lo, ALU.mult).then_inc(s["qk_t2"], 1)
                pool.tensor_tensor(rot[:, 1, :, HALF:], q[:, :, 0:HALF], hi, ALU.mult).then_inc(s["qk_t2"], 1)
                pool.wait_ge(s["qk_t1"], i + 1)
                pool.wait_ge(s["qk_t2"], 2 * i + 2)
                pool.tensor_tensor(q[:, :, 0:2 * HALF], rot[:, 0], rot[:, 1], ALU.add).then_inc(s["qk_rot"], 1)

            with pool.Fori(0, NP // 2) as j:
                for p in range(2):
                    rotate(j * 2 + p, p)
            rotate(NP, 0)

        @block.scalar
        def _(act):
            def x_stats(i, p, load, seen):
                act.wait_ge(s["x_load"][p], load)
                after(act, s["qk_ss"], seen)
                act.activation(sq[:, :], xt[:, p], ACT.Square, accum_out=ssx[:, p:p + 1]).then_inc(s["x_ss"], 1)
                act.wait_ge(s["x_ss"], i + 1)
                act.activation(ssx[:, 2 + p:3 + p], ssx[:, p:p + 1], ACT.Sqrt, bias=eps[:, 0:1], scale=1.0 / D).then_inc(s["x_root"], 1)

            def hi_parts(i, p):
                for b in range(2):
                    act.wait_ge(s["xT_ps"], 2 * i + b + 1)
                    act.activation(xT_hi[p][:, 4 * b:4 * b + 4, :], xps[b][:, :, :], ACT.Copy).then_inc(s["xT_hi"], 1)

            def outputs(i, j, p, nxt):
                act.wait_ge(s["x_ss"], i + 1 + int(nxt))
                for g in range(2):
                    act.wait_ge(s["proj"][g], i + 1)
                    act.activation(sq[:, g * GW:(g + 1) * GW], proj[g][:, :], ACT.Square).then_inc(s["qk_sq"], 1)
                if nxt:
                    hi_parts(i + 1, 1 - p)
                act.wait_ge(s["qk_ss"], 2 * i + 2)
                act.activation(ss[:, 1], ss[:, 0], ACT.Sqrt, bias=eps[:, 0:1], scale=1.0 / DQ).then_inc(s["qk_root"], 1)
                act.wait_ge(s["proj"][2], i + 1)
                after(act, s["store"][2][p], 16 * j)
                act.activation(vb[:, p], proj[2][:, :], ACT.Copy).then_inc(s["v_ready"], 1)
                act.wait_ge(s["proj"][3], i + 1)
                after(act, s["store"][3][p], 16 * j)
                act.activation(gb[:, p], proj[3][:, :], ACT.Silu).then_inc(s["g_ready"], 1)

            act.wait_ge(s["eps"], 1)
            x_stats(0, 0, 16, 0)
            split_weights("act", act, range(0, PIECES), s, bufs)
            hi_parts(0, 0)
            split_weights("act", act, range(PIECES, 4 * PIECES), s, bufs)

            def step(i, j, p):
                x_stats(i + 1, 1 - p, j * 16 + 16 * (1 + p), 2 * i)
                outputs(i, j, p, True)

            over_tiles(act, step)
            outputs(NP, NP // 2, 0, False)
            act.wait_ge(s["lam"], 2)
            act.activation(lam_sum[:, 0:2], lam_sum[:, 0:2], ACT.Exp).then_inc(s["lam"], 1)

        @block.vector
        def _(dve):
            def x_norm(i, p):
                dve.wait_ge(s["x_root"], i + 1)
                col = slice(i, i + 1) if isinstance(i, int) else bass.ds(i, 1)
                dve.reciprocal(rstd[:, col], ssx[:, 2 + p:3 + p]).then_inc(s["x_rs"], 1)
                dve.wait_ge(s["x_rs"], i + 1)
                dve.tensor_scalar(xt[:, p], xt[:, p], rstd[:, col], None, ALU.mult).then_inc(s["x_norm"], 1)

            def lo_parts(i, p):
                for b in range(2):
                    dve.wait_ge(s["xT_hi"], 2 * i + b + 1)
                    dve.tensor_tensor(xT_lo[p][:, 4 * b:4 * b + 4, :], xps[b][:, :, :],
                                      f32(xT_hi[p][:, 4 * b:4 * b + 4, :]), ALU.subtract).then_inc(s["xT_lo"], 1)

            def outputs(i, j, p, nxt):
                for g in range(2):
                    dve.wait_ge(s["qk_sq"], 2 * i + g + 1)
                    dve.tensor_reduce(ss[:, 0, 8 * g:8 * g + 8], sq[:, g * GW:(g + 1) * GW].rearrange("p (a b) -> p a b", b=DQ),
                                      AX.X, ALU.add).then_inc(s["qk_ss"], 1)
                if nxt:
                    lo_parts(i + 1, 1 - p)
                dve.wait_ge(s["qk_root"], i + 1)
                dve.reciprocal(ss[:, 2], ss[:, 1]).then_inc(s["qk_rs"], 1)
                dve.wait_ge(s["qk_rs"], i + 1)
                after(dve, s["store"][0][p], 16 * j)
                after(dve, s["store"][1][p], 16 * j)
                for g in range(2):
                    dve.tensor_tensor(qk[:, p, 8 * g:8 * g + 8], proj[g][:, :].rearrange("p (a b) -> p a b", b=DQ),
                                      ss[:, 2, 8 * g:8 * g + 8, None].broadcast_to([P, 8, DQ]), ALU.mult).then_inc(s["qk_norm"], 1)

            dve.memset(eps[:, :], EPS).then_inc(s["eps"], 1)
            x_norm(0, 0)
            split_weights("dve", dve, range(0, PIECES), s, bufs)
            lo_parts(0, 0)
            split_weights("dve", dve, range(PIECES, 4 * PIECES), s, bufs)

            def step(i, j, p):
                x_norm(i + 1, 1 - p)
                outputs(i, j, p, True)

            over_tiles(dve, step)
            outputs(NP, NP // 2, 0, False)
            dve.wait_ge(s["lam_load"], 64)
            dve.tensor_tensor(lam_prod[:, :], lam[:, 0:2], lam[:, 2:4], ALU.mult).then_inc(s["lam"], 1)
            dve.wait_ge(s["lam"], 1)
            dve.tensor_reduce(lam_sum[:, 0:2], lam_prod[:, :, :], AX.X, ALU.add).then_inc(s["lam"], 1)
            dve.wait_ge(s["lam"], 3)
            dve.tensor_tensor(lam_sum[:, 2:3], lam_sum[:, 1:2], lam_sum[:, 0:1], ALU.subtract).then_inc(s["lam"], 1)
            dve.wait_ge(s["lam"], 4)
            dve.tensor_scalar(nlam[:, 0:1], lam_sum[:, 2:3], LAM_INIT, None, ALU.subtract).then_inc(s["lam"], 1)

        @block.tensor
        def _(pe):
            def transposes(i, p):
                pe.wait_ge(s["x_norm"], i + 1)
                after(pe, s["xT_lo"], 2 * i)
                for b in range(2):
                    for k in range(4):
                        mm = pe.transpose(xps[b][:, k, :], xt[:, p, (4 * b + k) * P:(4 * b + k + 1) * P], ident[:, :])
                    mm.then_inc(s["xT_ps"], 1)

            def group(i, p, g, first):
                pe.wait_ge(s["xT_lo"], 2 * i + 2)
                if first:
                    pe.wait_ge(s["w_lo"], PIECES * (g + 1))
                if g < 2:
                    after(pe, s["qk_norm"], 2 * i)
                elif g == 2:
                    after(pe, s["v_ready"], i)
                else:
                    after(pe, s["g_ready"], i)
                product3(pe, proj[g][:, :], xT_hi[p], xT_lo[p], w_hi, w_lo,
                         slice(g * GW, (g + 1) * GW)).then_inc(s["proj"][g], 1)

            pe.wait_ge(s["ident"], 2)
            transposes(0, 0)

            def step(i, j, p):
                first = isinstance(i, int) and i == 0
                group(i, p, 0, first)
                group(i, p, 1, first)
                transposes(i + 1, 1 - p)
                group(i, p, 2, first)
                group(i, p, 3, first)

            over_tiles(pe, step)
            for g in range(4):
                group(NP, 0, g, False)


CH = P
BLOCKS = (128, 64, 32, 16, 8, 4)
NL = len(BLOCKS) + 1
LEAF_Q, LEAF_QE, LEAF_K, LEAF_KD = 6, 7, 8, 9
SLOTS = 10
F_MIN = 2.0 ** -62


def level_views(ap, width):
    v = ap.rearrange("p (n two w) -> p n two w", two=2, w=width // 2)
    n = v.shape[1]
    ref = v[:, :, 0, width // 2 - 1:width // 2].broadcast_to([P, n, width // 2])
    return v[:, :, 0, :], v[:, :, 1, :], ref


def decay_differences(dve, b, lv, blocks, last, n0=0):
    for slot, width in blocks:
        b_lo, b_up, ref = level_views(b, width)
        d_lo, d_up, _ = level_views(lv[:, slot - n0, :], width)
        dve.tensor_tensor(d_up, b_up, ref, ALU.subtract)
        dve.tensor_tensor(d_lo, ref, b_lo, ALU.subtract)
    pair = b.rearrange("p (n w) -> p n w", w=2)
    first = pair[:, :, 0:1].broadcast_to([P, pair.shape[1], 2])
    dve.tensor_tensor(lv[:, LEAF_Q - n0, :].rearrange("p (n w) -> p n w", w=2), pair, first, ALU.subtract)
    dve.tensor_tensor(lv[:, LEAF_K - n0, :].rearrange("p (n w) -> p n w", w=2), first, pair, ALU.subtract)
    dve.tensor_copy(lv[:, LEAF_QE - n0, :], b)
    run = b.rearrange("p (n w) -> p n w", w=last)
    end = run[:, :, last - 1:last].broadcast_to([P, run.shape[1], last])
    return dve.tensor_tensor(lv[:, LEAF_KD - n0, :].rearrange("p (n w) -> p n w", w=last), end, run, ALU.subtract)


def decay_products(pool, lv, q, k, blocks, n0=0):
    for slot, width in blocks:
        e_lo, e_up, _ = level_views(lv[:, slot - n0, :], width)
        _, q_up, _ = level_views(q, width)
        k_lo, _, _ = level_views(k, width)
        pool.tensor_tensor(e_up, e_up, q_up, ALU.mult)
        pool.tensor_tensor(e_lo, e_lo, k_lo, ALU.mult)
    n = q.shape[1]
    pool.tensor_tensor(lv[:, LEAF_Q - n0:LEAF_QE + 1 - n0, :], lv[:, LEAF_Q - n0:LEAF_QE + 1 - n0, :],
                       q[:, None, :].broadcast_to([P, 2, n]), ALU.mult)
    return pool.tensor_tensor(lv[:, LEAF_K - n0:LEAF_KD + 1 - n0, :], lv[:, LEAF_K - n0:LEAF_KD + 1 - n0, :],
                              k[:, None, :].broadcast_to([P, 2, n]), ALU.mult)


def pass_hgrn(nc, io, keep):
    with ExitStack() as ctx:
        def sb(name, shape, dt=F32):
            return ctx.enter_context(nc.sbuf_tensor("h_" + name, shape, dt))

        def sem(name):
            return ctx.enter_context(nc.semaphore("h_" + name))

        def ps(name, shape):
            return ctx.enter_context(nc.psum_tensor("h_" + name, shape, F32))

        ident, rstd = keep[:2]
        w_hi = sb("w_hi", [P, KD, 4 * GW], F32R)
        w_lo = sb("w_lo", [P, KD, 4 * GW], F32R)
        shared = sb("stage_or_levels", [P, 2, SLOTS * 2 * P])
        stage = [shared[:, b // 2, b % 2 * PB * GW:(b % 2 + 1) * PB * GW].rearrange("p (k n) -> p k n", k=PB)
                 for b in range(PIECES)]
        lv = [shared[:, hf, :].rearrange("p (s n) -> p s n", s=SLOTS) for hf in range(2)]
        wg = sb("wg", [P, KD])
        xt = sb("xt", [P, D])
        xT_hi = [sb(f"xT_hi{p}", [P, KD, P], F32R) for p in range(2)]
        xT_lo = [sb(f"xT_lo{p}", [P, KD, P], F32R) for p in range(2)]
        q_tok, s_tok = sb("q_tok", [P, GW]), sb("s_tok", [P, GW])
        qT, kT, lfT, bT = (sb(n, [P, GW]) for n in ("qT", "kT", "lfT", "bT"))
        v_tok, gate = sb("v_tok", [P, 2, GW]), sb("gate", [P, 2, GW])
        mask = sb("mask", [P, NL, P], BF16)
        masked = sb("masked", [P, NL, P])
        att = sb("att", [P, 2, P])
        kd_tok = sb("kd_tok", [P, GW])
        state = sb("state", [P, H, DV])
        ebc = sb("ebc", [P, 2, H])
        o_out = sb("o_out", [P, GW])
        oss = sb("oss", [P, 3, H])
        ng = sb("ng", [P, DV])
        eps = sb("eps", [P, 1])
        lbt = sb("lbt", [P, 6, H])
        proj = [ps(f"proj{b}", [P, GW]) for b in range(2)]
        xps = [ps(f"xps{b}", [P, 4, P]) for b in range(2)]
        lps = ps("lps", [P, 8, P])
        tps = ps("tps", [P, 4, P])
        ops = ps("ops", [P, H, DV])
        s = {n: sem(n) for n in (
            "w_norm", "w_scaled", "w_hi", "w_lo", "consts", "lb_load", "mask_load", "mask", "eps", "lb", "lb_exp", "x_load",
            "x_norm", "xT_ps", "xT_hi", "xT_lo", "q_tok", "s_tok", "v_tok", "gate", "qT_ps", "sT_ps", "qT", "f",
            "f_clamped", "log_f", "cumsum", "diff", "decay", "ebc", "operands", "levels", "masked", "att", "av", "kdT_ps",
            "kd_tok", "gain_ps", "state", "o_sq", "o_ss", "o_root", "o_rs", "o_norm", "o_g", "o_out", "store", "tail")}
        s["w_staged"] = [sem(f"w_staged{b}") for b in range(PIECES)]
        s["proj"] = [sem(f"proj{g}") for g in range(4)]
        bufs = (stage, wg, w_hi, w_lo)
        block = open_block(nc, ctx, s.values())
        all_levels = tuple(enumerate(BLOCKS))

        def half(ap, hf):
            return ap[:, hf * 2 * P:(hf + 1) * 2 * P]

        @block.sync
        def _(sp):
            sp.dma_start(wg[:, :], io["norm_g"]).then_inc(s["w_norm"], 16)
            sp.dma_start(xt[:, :], io["x"][0:P, :]).then_inc(s["x_load"], 16)
            sp.dma_start(lbt[:, 0:2, :], io["lb"]).then_inc(s["lb_load"], 16)
            sp.dma_start(masked[:, :, :], io["level_mask"]).then_inc(s["mask_load"], 16)
            sp.dma_start(ng[:, :], io["hgrn_norm_g"].partition_broadcast(P).rearrange("p a b -> p (a b)")).then_inc(s["consts"], 16)
            stage_weights(sp, io["w_in"], 4 * GW, s, bufs)

            def load(i):
                sp.wait_ge(s["xT_ps"], 2 * i)
                sp.dma_start(xt[:, :], io["x"][bass.ds(i * P, P), :]).then_inc(s["x_load"], 16)

            def store(t):
                sp.wait_ge(s["o_out"], t + 1)
                sp.dma_start(io["mr_s"][bass.ds(t * P, P), :], o_out[:, :]).then_inc(s["store"], 16)

            load(1)
            load(2)
            with sp.Fori(3, NT) as i:
                load(i)
                store(i - 3)
            store(NP - 2)
            store(NP - 1)
            sp.wait_ge(s["state"], NP + 1)
            sp.dma_start(io["s_p"].rearrange("h d v -> d h v"), state[:, :, :]).then_inc(s["tail"], 16)
            sp.wait_ge(s["qT"], NT)
            sp.dma_start(io["hq_s"], qT[:, :]).then_inc(s["tail"], 16)
            sp.wait_ge(s["f_clamped"], NT)
            sp.dma_start(io["hk_s"], kT[:, :]).then_inc(s["tail"], 16)
            sp.wait_ge(s["log_f"], NT)
            sp.dma_start(io["hl_s"], lfT[:, :]).then_inc(s["tail"], 16)
            sp.wait_ge(s["v_tok"], NT)
            sp.dma_start(io["hv_s"], v_tok[:, 0]).then_inc(s["tail"], 16)
            sp.wait_ge(s["gate"], NT)
            sp.dma_start(io["hg_s"], gate[:, 0]).then_inc(s["tail"], 16)
            sp.wait_ge(s["tail"], 96)
            sp.wait_ge(s["store"], 16 * NP)

        @block.gpsimd
        def _(pool):
            split_weights("pool", pool, range(4 * PIECES), s, bufs)
            pool.wait_ge(s["consts"], 16)

            def operands(i):
                for hf in range(2):
                    pool.wait_ge(s["decay"], 2 * i + hf + 1)
                    pool.wait_ge(s["qT"], i + 1)
                    pool.wait_ge(s["f_clamped"], i + 1)
                    decay_products(pool, lv[hf], half(qT, hf), half(kT, hf), all_levels).then_inc(s["operands"], 1)

            def gated(t, pt):
                pool.wait_ge(s["o_norm"], t + 1)
                o3 = o_out[:, :].rearrange("p (h v) -> p h v", h=H)
                pool.tensor_tensor(o3, o3, ng[:, None, :].broadcast_to([P, H, DV]), ALU.mult).then_inc(s["o_g"], 1)
                pool.wait_ge(s["o_g"], t + 1)
                pool.wait_ge(s["gate"], t + 1)
                pool.tensor_tensor(o_out[:, :], o_out[:, :], gate[:, pt], ALU.mult).then_inc(s["o_out"], 1)

            operands(0)
            with pool.Fori(0, NP // 2 - 1) as j:
                for pt in range(2):
                    t = j * 2 + pt
                    operands(t + 1)
                    gated(t, pt)
            operands(NP - 1)
            gated(NP - 2, 0)
            gated(NP - 1, 1)

        @block.scalar
        def _(act):
            def hi_parts(i, p):
                for b in range(2):
                    act.wait_ge(s["xT_ps"], 2 * i + b + 1)
                    act.activation(xT_hi[p][:, 4 * b:4 * b + 4, :], xps[b][:, :, :], ACT.Copy).then_inc(s["xT_hi"], 1)

            def gate_input(i, p):
                after(act, s["proj"][3], i + 1)
                after(act, s["o_out"], i - 1)
                act.activation(gate[:, p], proj[1][:, :], ACT.Silu).then_inc(s["gate"], 1)

            def inputs_qf(i):
                act.wait_ge(s["proj"][0], i + 1)
                after(act, s["qT_ps"], i)
                act.activation(q_tok[:, :], proj[0][:, :], ACT.Silu).then_inc(s["q_tok"], 1)
                act.wait_ge(s["proj"][1], i + 1)
                after(act, s["sT_ps"], i)
                act.activation(s_tok[:, :], proj[1][:, :], ACT.Sigmoid).then_inc(s["s_tok"], 1)

            def q_columns(i):
                act.wait_ge(s["qT_ps"], i + 1)
                after(act, s["operands"], 2 * i)
                act.activation(qT[:, :], tps[:, :, :].rearrange("p h t -> p (h t)"), ACT.Copy).then_inc(s["qT"], 1)

            def value_input(i, p):
                act.wait_ge(s["proj"][2], i + 1)
                act.activation(v_tok[:, p], proj[0][:, :], ACT.Copy).then_inc(s["v_tok"], 1)

            def decays(i, p):
                act.wait_ge(s["f_clamped"], i + 1)
                act.activation(lfT[:, :], lfT[:, :], ACT.Ln).then_inc(s["log_f"], 1)

            def exps(i, hf):
                act.wait_ge(s["diff"], 2 * i + hf + 1)
                act.activation(lv[hf], lv[hf], ACT.Exp).then_inc(s["decay"], 1)

            def tile_decay(p):
                act.activation(ebc[:, p], bT[:, :].rearrange("p (h t) -> p h t", h=H)[:, :, P - 1], ACT.Exp).then_inc(s["ebc"], 1)

            def o_stats(t):
                act.wait_ge(s["av"], 4 * t + 4)
                after(act, s["store"], 16 * t)
                act.activation(o_out[:, :], ops[:, :, :].rearrange("p h v -> p (h v)"), ACT.Square).then_inc(s["o_sq"], 1)
                act.wait_ge(s["o_ss"], t + 1)
                act.activation(oss[:, 1], oss[:, 0], ACT.Sqrt, bias=eps[:, 0:1], scale=1.0 / DV).then_inc(s["o_root"], 1)

            def step(t, pt, more):
                i, p = t + 1, 1 - pt
                gate_input(t, pt)
                inputs_qf(i)
                act.wait_ge(s["kdT_ps"], t + 1)
                after(act, s["gain_ps"], t)
                act.activation(kd_tok[:, :], xps[1][:, :, :].rearrange("p h d -> p (h d)"), ACT.Copy).then_inc(s["kd_tok"], 1)
                q_columns(i)
                decays(i, p)
                if more:
                    exps(i, 0)
                value_input(i, p)
                if more:
                    hi_parts(i + 1, pt)
                    exps(i, 1)
                    tile_decay(p)
                o_stats(t)

            act.wait_ge(s["lb"], 2)
            act.activation(lbt[:, 3:5, :], lbt[:, 3:5, :], ACT.Exp).then_inc(s["lb_exp"], 1)
            split_weights("act", act, range(0, PIECES), s, bufs)
            hi_parts(0, 0)
            split_weights("act", act, range(PIECES, 3 * PIECES), s, bufs)
            inputs_qf(0)
            split_weights("act", act, range(3 * PIECES, 4 * PIECES), s, bufs)
            q_columns(0)
            decays(0, 0)
            exps(0, 0)
            value_input(0, 0)
            hi_parts(1, 1)
            exps(0, 1)
            tile_decay(0)
            step(0, 0, True)
            step(1, 1, True)
            with act.Fori(0, NP // 2 - 2) as j:
                for pt in range(2):
                    step(2 * j + 2 + pt, pt, True)
            step(NP - 2, 0, True)
            step(NP - 1, 1, False)
            gate_input(NP, 0)

        @block.vector
        def _(dve):
            def x_norm(i):
                dve.wait_ge(s["x_load"], 16 * i + 16)
                col = slice(i, i + 1) if isinstance(i, int) else bass.ds(i, 1)
                dve.tensor_scalar(xt[:, :], xt[:, :], rstd[:, col], None, ALU.mult).then_inc(s["x_norm"], 1)

            def lo_parts(i, p):
                for b in range(2):
                    dve.wait_ge(s["xT_hi"], 2 * i + b + 1)
                    dve.tensor_tensor(xT_lo[p][:, 4 * b:4 * b + 4, :], xps[b][:, :, :],
                                      f32(xT_hi[p][:, 4 * b:4 * b + 4, :]), ALU.subtract).then_inc(s["xT_lo"], 1)

            def keep_pairs(t, h):
                n = 4 * t + h
                dve.wait_ge(s["levels"], n + 1)
                after(dve, s["att"], n)
                dve.tensor_tensor(masked[:, :, :], lps[:, 0:NL, :], mask[:, :, :], ALU.mult).then_inc(s["masked"], 1)
                dve.wait_ge(s["masked"], n + 1)
                if h >= 2:
                    dve.wait_ge(s["av"], n - 1)
                dve.tensor_reduce(att[:, h % 2], masked[:, :, :].rearrange("p l t -> p t l"), AX.X, ALU.add).then_inc(s["att"], 1)

            def forget(i):
                dve.wait_ge(s["sT_ps"], i + 1)
                after(dve, s["operands"], 2 * i)
                for h in range(H):
                    last = dve.tensor_scalar(lfT[:, h * P:(h + 1) * P], xps[0][:, h, :], lbt[:, 4, h:h + 1], lbt[:, 3, h:h + 1],
                                             ALU.mult, ALU.add)
                last.then_inc(s["f"], 1)
                dve.wait_ge(s["f"], i + 1)
                dve.tensor_scalar(kT[:, :], lfT[:, :], -1.0, 1.0, ALU.mult, ALU.add)
                dve.tensor_scalar(lfT[:, :], lfT[:, :], F_MIN, None, ALU.max).then_inc(s["f_clamped"], 1)

            def cumulate(i):
                dve.wait_ge(s["log_f"], i + 1)
                after(dve, s["ebc"], i)
                for h in range(H):
                    cols = slice(h * P, (h + 1) * P)
                    last = dve.tensor_tensor_scan(bT[:, cols], lfT[:, cols], lfT[:, cols], 0.0, ALU.add, ALU.bypass)
                last.then_inc(s["cumsum"], 1)
                dve.wait_ge(s["cumsum"], i + 1)

            def differences(i, t):
                for hf in range(2):
                    if t is not None:
                        dve.wait_ge(s["av"], 4 * t + 2 * hf + 2)
                        dve.wait_ge(s["kdT_ps"], t + 1)
                    decay_differences(dve, half(bT, hf), lv[hf], all_levels, P).then_inc(s["diff"], 1)

            def o_norm(t):
                o3 = o_out[:, :].rearrange("p (h v) -> p h v", h=H)
                dve.wait_ge(s["o_sq"], t + 1)
                dve.tensor_reduce(oss[:, 0], o3, AX.X, ALU.add).then_inc(s["o_ss"], 1)
                dve.wait_ge(s["o_root"], t + 1)
                dve.reciprocal(oss[:, 2], oss[:, 1]).then_inc(s["o_rs"], 1)
                dve.wait_ge(s["o_rs"], t + 1)
                dve.tensor_tensor(o3, ops[:, :, :], oss[:, 2, :, None].broadcast_to([P, H, DV]), ALU.mult).then_inc(s["o_norm"], 1)

            def carry(t, pt):
                dve.wait_ge(s["gain_ps"], t + 1)
                dve.wait_ge(s["ebc"], t + 1)
                for h in range(H):
                    last = dve.scalar_tensor_tensor(out=state[:, h], in0=state[:, h], scalar=ebc[:, pt, h:h + 1], in1=tps[:, h, :],
                                                    op0=ALU.mult, op1=ALU.add)
                last.then_inc(s["state"], 1)

            dve.memset(eps[:, :], EPS).then_inc(s["eps"], 1)
            dve.memset(state[:, :, :], 0.0).then_inc(s["state"], 1)
            dve.wait_ge(s["mask_load"], 16)
            dve.tensor_copy(mask[:, :, :], masked[:, :, :]).then_inc(s["mask"], 1)
            dve.wait_ge(s["mask"], 1)
            dve.wait_ge(s["lb_load"], 16)
            dve.tensor_tensor(lbt[:, 2], lbt[:, 0], lbt[:, 1], ALU.max).then_inc(s["lb"], 1)
            dve.wait_ge(s["lb"], 1)
            dve.tensor_tensor(lbt[:, 3:5], lbt[:, 0:2], lbt[:, 2, None, :].broadcast_to([P, 2, H]), ALU.subtract).then_inc(s["lb"], 1)
            dve.wait_ge(s["lb_exp"], 1)
            dve.tensor_tensor(lbt[:, 2], lbt[:, 3], lbt[:, 4], ALU.add).then_inc(s["lb"], 1)
            dve.wait_ge(s["lb"], 3)
            dve.reciprocal(lbt[:, 5], lbt[:, 2]).then_inc(s["lb"], 1)
            dve.wait_ge(s["lb"], 4)
            dve.tensor_tensor(lbt[:, 3:5], lbt[:, 3:5], lbt[:, 5, None, :].broadcast_to([P, 2, H]), ALU.mult).then_inc(s["lb"], 1)
            dve.wait_ge(s["lb"], 5)
            x_norm(0)
            split_weights("dve", dve, range(0, PIECES), s, bufs)
            lo_parts(0, 0)
            split_weights("dve", dve, range(PIECES, 4 * PIECES), s, bufs)
            forget(0)
            cumulate(0)
            differences(0, None)
            x_norm(1)
            lo_parts(1, 1)

            def step(t, pt, more):
                i, p = t + 1, 1 - pt
                keep_pairs(t, 0)
                keep_pairs(t, 1)
                if more:
                    x_norm(i + 1)
                keep_pairs(t, 2)
                forget(i)
                keep_pairs(t, 3)
                if more:
                    cumulate(i)
                    differences(i, t)
                    lo_parts(i + 1, pt)
                o_norm(t)
                carry(t, pt)

            step(0, 0, True)
            step(1, 1, True)
            with dve.Fori(0, NP // 2 - 2) as j:
                for pt in range(2):
                    step(2 * j + 2 + pt, pt, True)
            step(NP - 2, 0, True)
            step(NP - 1, 1, False)

        @block.tensor
        def _(pe):
            def x_columns(i, p):
                pe.wait_ge(s["x_norm"], i + 1)
                after(pe, s["xT_lo"], 2 * i)
                after(pe, s["f"], i)
                after(pe, s["kd_tok"], i - 1)
                for b in range(2):
                    for k in range(4):
                        mm = pe.transpose(xps[b][:, k, :], xt[:, (4 * b + k) * P:(4 * b + k + 1) * P], ident[:, :])
                    mm.then_inc(s["xT_ps"], 1)

            def group(i, p, g, halves=(0, 1), first=False):
                if 0 in halves:
                    pe.wait_ge(s["xT_lo"], 2 * i + 2)
                    if first:
                        pe.wait_ge(s["w_lo"], PIECES * (g + 1))
                    after(pe, s[("v_tok", "gate", "q_tok", "s_tok")[g]], i if g < 2 else i + 1)
                mm = product3(pe, proj[g % 2][:, :], xT_hi[p], xT_lo[p], w_hi, w_lo,
                              slice(g * GW, (g + 1) * GW), halves)
                if 1 in halves:
                    mm.then_inc(s["proj"][g], 1)

            def head_columns(i, t):
                pe.wait_ge(s["q_tok"], i + 1)
                after(pe, s["state"], i)
                for h in range(H):
                    mm = pe.transpose(tps[:, h, :], q_tok[:, h * P:(h + 1) * P], ident[:, :])
                mm.then_inc(s["qT_ps"], 1)
                pe.wait_ge(s["s_tok"], i + 1)
                for h in range(H):
                    mm = pe.transpose(xps[0][:, h, :], s_tok[:, h * P:(h + 1) * P], ident[:, :])
                mm.then_inc(s["sT_ps"], 1)

            def levels(t, h):
                c = slice((h % 2) * P, (h % 2) * P + P)
                l = lv[h // 2]
                pe.wait_ge(s["operands"], 2 * t + h // 2 + 1)
                after(pe, s["masked"], 4 * t + h)
                for n in range(NL - 1):
                    pe.matmul(lps[:, n, :], l[:, n, c], l[:, n, c], start=True, stop=True)
                pe.matmul(lps[:, NL - 1, :], l[:, LEAF_K, c], l[:, LEAF_Q, c], start=True, stop=True).then_inc(s["levels"], 1)

            def out_rows(t, pt, h):
                c = slice((h % 2) * P, (h % 2) * P + P)
                pe.wait_ge(s["att"], 4 * t + h + 1)
                pe.wait_ge(s["state"], t + 1)
                after(pe, s["o_norm"], t)
                pe.wait_ge(s["v_tok"], t + 1)
                pe.matmul(ops[:, h, :], att[:, h % 2], v_tok[:, pt, h * DV:(h + 1) * DV], start=True, stop=False)
                pe.matmul(ops[:, h, :], lv[h // 2][:, LEAF_QE, c], state[:, h], start=False, stop=True).then_inc(s["av"], 1)

            def key_rows(t):
                pe.wait_ge(s["operands"], 2 * t + 2)
                for h in range(H):
                    c = slice((h % 2) * P, (h % 2) * P + P)
                    mm = pe.transpose(xps[1][:, h, :], lv[h // 2][:, LEAF_KD, c], ident[:, :])
                mm.then_inc(s["kdT_ps"], 1)

            def gains(t, pt):
                pe.wait_ge(s["kd_tok"], t + 1)
                pe.wait_ge(s["qT"], t + 2)
                for h in range(H):
                    mm = pe.matmul(tps[:, h, :], kd_tok[:, h * P:(h + 1) * P], v_tok[:, pt, h * DV:(h + 1) * DV],
                                   start=True, stop=True)
                mm.then_inc(s["gain_ps"], 1)

            def step(t, pt, more):
                i, p = t + 1, 1 - pt
                group(i, p, 0)
                levels(t, 0)
                group(i, p, 1, (0,))
                levels(t, 1)
                out_rows(t, pt, 0)
                group(i, p, 1, (1,))
                levels(t, 2)
                key_rows(t)
                out_rows(t, pt, 1)
                head_columns(i, t)
                levels(t, 3)
                out_rows(t, pt, 2)
                group(i, p, 2, (0,))
                out_rows(t, pt, 3)
                group(i, p, 2, (1,))
                if more:
                    x_columns(i + 1, pt)
                group(i, p, 3, (0,))
                gains(t, pt)
                group(i, p, 3, (1,))

            x_columns(0, 0)
            group(0, 0, 0, first=True)
            group(0, 0, 1, first=True)
            head_columns(0, None)
            group(0, 0, 2, first=True)
            x_columns(1, 1)
            group(0, 0, 3, first=True)
            step(0, 0, True)
            step(1, 1, True)
            with pe.Fori(0, NP // 2 - 2) as j:
                for pt in range(2):
                    step(2 * j + 2 + pt, pt, True)
            step(NP - 2, 0, True)
            step(NP - 1, 1, False)


NEG = -1e30


def pass_attention(nc, io, keep):
    with ExitStack() as ctx:
        def sb(name, shape, dt=F32):
            return ctx.enter_context(nc.sbuf_tensor("p_" + name, shape, dt))

        def sem(name):
            return ctx.enter_context(nc.semaphore("p_" + name))

        def ps(name, shape):
            return ctx.enter_context(nc.psum_tensor("p_" + name, shape, F32))

        ident, nlam = keep[0], keep[2]
        M = 2 * H
        KT = sb("KT", [P, M, SEQ], F32R)
        V = sb("V", [P, NP, H * DV])
        qk_in = sb("qk_in", [P, 2, 2, GW])
        k_hl = sb("k_hl", [P, M, 2, DQ], F32R)
        q_hl = sb("q_hl", [P, 2, M, 2, DQ], F32R)
        QS = [[sb(f"Q{part}{p}", [P, M, P], F32R) for part in "hl"] for p in range(2)]
        sc = [sb(f"scores{m}", [P, 3 - m, SEQ]) for m in range(2)]
        WT = sb("WT", [P, 2, 4, P])
        mask = sb("mask", [P, 4 * P])
        zero = sb("zero", [P, 4 * P])
        mx = sb("mx", [P, 2, 2, 4])
        nmx = sb("nmx", [P, 2, 2])
        ls = sb("ls", [P, 2, 2, H])
        rl = sb("rl", [P, H])
        coef = sb("coef", [P, 2])
        r0 = sb("r0", [P, H])
        ob = sb("ob", [P, 2, H * DV])
        sps = [ps(f"sps{n}", [P, 512]) for n in range(4)]
        tps = [ps(f"tps{n}", [P, 4, P]) for n in range(2)]
        ops = [ps(f"ops{n}", [P, H, DV]) for n in range(2)]
        s = {n: sem(n) for n in ("v_load0", "v_load1", "v_load2", "v_load3", "mask_load", "zero", "q_hi", "k_hi", "q_lo", "k_lo",
                                 "sps_full", "sps_read", "neg_max", "exp", "recip", "coef",
                                 "weights", "wT_ps", "wT", "out_ps", "r0", "out")}
        s["qk_load"] = [sem(f"qk_load{p}") for p in range(2)]
        s["store"] = [sem(f"store{p}") for p in range(2)]
        block = open_block(nc, ctx, s.values())
        chunks = [[(c, min(512, (i + 1) * P - c)) for c in range(0, (i + 1) * P, 512)] for i in range(NP)]
        n_heads = NP * H
        tile_head = [(i, h) for i in range(NP) for h in range(H)]
        first_prep, first_sc, first_wt, n_use, n_wt = {0: 0}, {}, {}, 6, 0
        for i, h in tile_head:
            if h == 2 and i + 1 < NP:
                first_prep[i + 1] = n_use
                n_use += 6
            first_sc[i, h], first_wt[i, h] = n_use, n_wt
            n_use += 2 * len(chunks[i])
            n_wt += len(chunks[i])

        def twice(q):
            return q.rearrange("p (m d) -> p m d", d=DQ)[:, :, None, :].broadcast_to([P, M, 2, DQ])

        @block.sync
        def _(sp):
            def load(i):
                r = slice(i * P, (i + 1) * P)
                if i >= 2:
                    sp.wait_ge(s["q_lo"], i - 1)
                    sp.wait_ge(s["k_lo"], i - 1)
                sp.dma_start(qk_in[:, i % 2, 0], io["q_s"][r, :]).then_inc(s["qk_load"][i % 2], 16)
                sp.dma_start(qk_in[:, i % 2, 1], io["k_p"][r, :]).then_inc(s["qk_load"][i % 2], 16)

            load(0)
            sp.dma_start(mask[:, :], io["causal"]).then_inc(s["mask_load"], 16)
            load(1)
            for q in range(4):
                sp.dma_start(V[:, 4 * q:4 * q + 4, :], io["v_p"].rearrange("(b p) n -> p b n", p=P)[:, 4 * q:4 * q + 4, :])\
                  .then_inc(s[f"v_load{q}"], 16)
            for i in range(NP + 1):
                if i + 2 < NP:
                    load(i + 2)
                if i >= 1:
                    sp.wait_ge(s["out"], i)
                    sp.dma_start(io["o_s"][(i - 1) * P:i * P, :], ob[:, (i - 1) % 2]).then_inc(s["store"][(i - 1) % 2], 16)
            for p in range(2):
                sp.wait_ge(s["store"][p], 16 * NP // 2)

        @block.gpsimd
        def _(pool):
            pool.memset(zero[:, :], 0.0).then_inc(s["zero"], 1)
            for i in range(NP):
                pool.wait_ge(s["k_hi"], i + 1)
                if i >= 1:
                    pool.wait_ge(s["sps_full"], first_prep[i - 1] + 6)
                pool.tensor_tensor(k_hl[:, :, 1], qk_in[:, i % 2, 1].rearrange("p (m d) -> p m d", d=DQ),
                                   f32(k_hl[:, :, 0]), ALU.subtract).then_inc(s["k_lo"], 1)
                pool.wait_ge(s["q_hi"], i + 1)
                pool.tensor_tensor(q_hl[:, 1], twice(qk_in[:, i % 2, 0]),
                                   f32(q_hl[:, 0]), ALU.subtract).then_inc(s["q_lo"], 1)

        @block.scalar
        def _(act):
            def split_hi(i):
                act.wait_ge(s["qk_load"][i % 2], 32 * (i // 2 + 1))
                if i >= 1:
                    act.wait_ge(s["sps_full"], first_prep[i - 1] + 6)
                act.activation(k_hl[:, :, 0], qk_in[:, i % 2, 1].rearrange("p (m d) -> p m d", d=DQ), ACT.Copy).then_inc(s["k_hi"], 1)
                act.activation(q_hl[:, 0], twice(qk_in[:, i % 2, 0]), ACT.Copy).then_inc(s["q_hi"], 1)

            def exp_row(n, m):
                i, h = tile_head[n]
                act.wait_ge(s["neg_max"], n + 1)
                w = (i + 1) * P
                row = sc[m][:, n % (3 - m), 0:w]
                act.activation(row, row, ACT.Exp, bias=nmx[:, n % 2, m:m + 1],
                               accum_out=ls[:, i % 2, m, h:h + 1]).then_inc(s["exp"], 1)

            def weights_out(n, c):
                i, h = tile_head[n]
                g = first_wt[i, h] + c
                act.wait_ge(s["wT_ps"], g + 1)
                if g >= 2:
                    act.wait_ge(s["out_ps"], g - 1)
                w = chunks[i][c][1]
                act.activation(WT[:, g % 2, 0:w // P, :], tps[g % 2][:, 0:w // P, :], ACT.Copy).then_inc(s["wT"], 1)

            split_hi(0)
            for n in range(n_heads + 2):
                n_c = len(chunks[tile_head[n - 2][0]]) if n >= 2 else 0
                if 1 <= n <= n_heads:
                    exp_row(n - 1, 0)
                if n_c:
                    weights_out(n - 2, 0)
                if 1 <= n <= n_heads:
                    exp_row(n - 1, 1)
                for c in range(1, n_c):
                    weights_out(n - 2, c)
                if n < n_heads and tile_head[n][1] == 0 and tile_head[n][0] + 1 < NP:
                    split_hi(tile_head[n][0] + 1)

        @block.vector
        def _(dve):
            def prep_out(i):
                if i >= 2:
                    dve.wait_ge(s["sps_full"], first_sc[i - 1, 0])
                for n in range(6):
                    k = first_prep[i] + n
                    dve.wait_ge(s["sps_full"], k + 1)
                    src = sps[k % 4][:, :].rearrange("p (m t) -> p m t", m=4)
                    dst = KT[:, 4 * n:4 * n + 4, i * P:(i + 1) * P] if n < 2 else QS[i % 2][(n - 2) // 2][:, 4 * (n % 2):4 * (n % 2) + 4, :]
                    dve.tensor_copy(dst, src).then_inc(s["sps_read"], 1)

            def rows(n):
                i, h = tile_head[n]
                last = len(chunks[i]) - 1
                if n >= 2:
                    dve.wait_ge(s["weights"], n - 1)
                if n >= 3:
                    dve.wait_ge(s["wT_ps"], first_wt[tile_head[n - 2]])
                for c, (c0, w) in enumerate(chunks[i]):
                    for m in range(2):
                        k = first_sc[i, h] + 2 * c + m
                        dve.wait_ge(s["sps_full"], k + 1)
                        add = mask[:, 4 * P - w:4 * P] if c == last else zero[:, 0:w]
                        red = dve.tensor_tensor_reduce(sc[m][:, n % (3 - m), c0:c0 + w], sps[k % 4][:, 0:w], add, SCALE, -3e38,
                                                       ALU.add, ALU.max, mx[:, n % 2, m, c:c + 1]).then_inc(s["sps_read"], 1)
                dve.wait_ge(s["sps_read"], first_sc[i, h] + 2 * len(chunks[i]))
                if n >= 2:
                    dve.wait_ge(s["exp"], 2 * n - 2)
                dve.tensor_reduce(nmx[:, n % 2, :], mx[:, n % 2, :, 0:last + 1], AX.X, ALU.max, negate=True).then_inc(s["neg_max"], 1)

            def combine(n):
                i, h = tile_head[n]
                dve.wait_ge(s["exp"], 2 * n + 2)
                dve.reciprocal(rl[:, h:h + 1], ls[:, i % 2, 1, h:h + 1]).then_inc(s["recip"], 1)
                dve.wait_ge(s["recip"], n + 1)
                dve.scalar_tensor_tensor(out=coef[:, n % 2:n % 2 + 1], in0=ls[:, i % 2, 0, h:h + 1], scalar=nlam[:, 0:1],
                                         in1=rl[:, h:h + 1], op0=ALU.mult, op1=ALU.mult).then_inc(s["coef"], 1)
                dve.wait_ge(s["coef"], n + 1)
                w = (i + 1) * P
                dve.scalar_tensor_tensor(out=sc[0][:, n % 3, 0:w], in0=sc[1][:, n % 2, 0:w], scalar=coef[:, n % 2:n % 2 + 1],
                                         in1=sc[0][:, n % 3, 0:w], op0=ALU.mult, op1=ALU.add).then_inc(s["weights"], 1)

            def out_rows(i):
                dve.reciprocal(r0[:, :], ls[:, i % 2, 0, :]).then_inc(s["r0"], 1)
                dve.wait_ge(s["r0"], i + 1)
                dve.wait_ge(s["out_ps"], first_wt[i, H - 1] + len(chunks[i]))
                if i >= 2:
                    dve.wait_ge(s["store"][i % 2], 16 * (i // 2))
                dve.tensor_tensor(ob[:, i % 2].rearrange("p (h v) -> p h v", h=H), ops[i % 2][:, :, :],
                                  r0[:, :, None].broadcast_to([P, H, DV]), ALU.mult).then_inc(s["out"], 1)

            dve.wait_ge(s["zero"], 1)
            dve.wait_ge(s["mask_load"], 16)
            prep_out(0)
            for n in range(n_heads + 3):
                if n < n_heads:
                    i, h = tile_head[n]
                    if h == 2 and i + 1 < NP:
                        prep_out(i + 1)
                    rows(n)
                if 1 <= n <= n_heads:
                    combine(n - 1)
                if n >= 3 and tile_head[n - 3][1] == H - 1:
                    out_rows(tile_head[n - 3][0])

        @block.tensor
        def _(pe):
            def prep(i):
                pe.wait_ge(s["k_lo"], i + 1)
                pe.wait_ge(s["q_lo"], i + 1)
                for n in range(6):
                    k = first_prep[i] + n
                    if k >= 4:
                        pe.wait_ge(s["sps_read"], k - 3)
                    for a in range(4):
                        m = 4 * (n % 2) + a
                        if n < 2:
                            src = f32(k_hl[:, m, :, :]).rearrange("p a b -> p (a b)")
                        else:
                            src = f32(q_hl[:, (n - 2) // 2, m]).rearrange("p a b -> p (a b)")
                        mm = pe.transpose(sps[k % 4][:, a * P:(a + 1) * P], src, ident[:, :])
                    mm.then_inc(s["sps_full"], 1)

            def scores(n, c):
                i, h = tile_head[n]
                c0, w = chunks[i][c]
                if c == 0:
                    pe.wait_ge(s["sps_read"], first_prep[i] + 6)
                for m in range(2):
                    k = first_sc[i, h] + 2 * c + m
                    pe.wait_ge(s["sps_read"], k - 3)
                    for part in range(2):
                        mm = pe.matmul(sps[k % 4][:, 0:w], QS[i % 2][part][:, 2 * h + m, :], KT[:, 2 * h + m, c0:c0 + w],
                                       start=(part == 0), stop=(part == 1))
                    mm.then_inc(s["sps_full"], 1)

            def weight_columns(n, c):
                i, h = tile_head[n]
                g = first_wt[i, h] + c
                if c == 0:
                    pe.wait_ge(s["weights"], n + 1)
                if g >= 2:
                    pe.wait_ge(s["wT"], g - 1)
                c0, w = chunks[i][c]
                for b in range(w // P):
                    mm = pe.transpose(tps[g % 2][:, b, :], sc[0][:, n % 3, c0 + b * P:c0 + (b + 1) * P], ident[:, :])
                mm.then_inc(s["wT_ps"], 1)

            def values(n, c):
                i, h = tile_head[n]
                g = first_wt[i, h] + c
                c0, w = chunks[i][c]
                pe.wait_ge(s["wT"], g + 1)
                pe.wait_ge(s[f"v_load{c}"], 16)
                if h == 0 and c == 0 and i >= 2:
                    pe.wait_ge(s["out"], i - 1)
                for b in range(w // P):
                    kb = c0 // P + b
                    mm = pe.matmul(ops[i % 2][:, h, :], WT[:, g % 2, b, :], V[:, kb, h * DV:(h + 1) * DV],
                                   start=(kb == 0), stop=(kb == i))
                mm.then_inc(s["out_ps"], 1)

            prep(0)
            for n in range(n_heads + 2):
                n_s = len(chunks[tile_head[n][0]]) if n < n_heads else 0
                n_v = len(chunks[tile_head[n - 2][0]]) if n >= 2 else 0
                if n_s and tile_head[n][1] == 2 and tile_head[n][0] + 1 < NP:
                    prep(tile_head[n][0] + 1)
                for c in range(max(n_s, n_v)):
                    if c < n_s:
                        scores(n, c)
                    if c < n_v:
                        weight_columns(n - 2, c)
                    if 1 <= c <= n_v:
                        values(n - 2, c - 1)
                if n_v and max(n_s, n_v) == n_v:
                    values(n - 2, n_v - 1)


def pass_samples(nc, io, keep):
    with ExitStack() as ctx:
        def sb(name, shape, dt=F32):
            return ctx.enter_context(nc.sbuf_tensor("s_" + name, shape, dt))

        def sem(name):
            return ctx.enter_context(nc.semaphore("s_" + name))

        def ps(name, shape):
            return ctx.enter_context(nc.psum_tensor("s_" + name, shape, F32))

        ident, nlam, w_out = keep[0], keep[2], keep[3]
        NK = PAST + DEC_T
        AHEAD = 3
        pages = sb("pages", [1, DEC_B * NPG], I32)
        kc = sb("kc", [P, AHEAD, NPG, GW])
        vc = sb("vc", [P, AHEAD, NPG, GW])
        v_new = sb("v_new", [DEC_T, AHEAD, GW])
        qk_new = sb("qk_new", [NS, 2, GW])
        Q = sb("Q", [P, DEC_B, H, 32])
        K_new = sb("K_new", [P, H, NS])
        KT = sb("KT", [P, 2, H, PAST])
        sc = sb("sc", [P, 2, NK])
        PT = sb("PT", [P, 2, NPG + 1, P])
        mask = sb("mask", [P, DEC_T])
        zero = sb("zero", [P, PAST])
        is_map = sb("is_map", [P, 2])
        sign = sb("sign", [P, 1])
        mx = sb("mx", [P, 2, 2])
        nmx = sb("nmx", [P, 2])
        l = sb("l", [P, 2])
        rl = sb("rl", [P, 2])
        coef = sb("coef", [P, 2])
        part = sb("part", [P, 2, DV])
        tps = [ps(f"tps{n}", [P, 4, P]) for n in range(2)]
        sps = [ps(f"sps{n}", [P, PAST]) for n in range(2)]
        nps = ps("nps", [P, 2, 256])
        pps = [ps(f"pps{n}", [P, 4, P]) for n in range(2)]
        ops = ps("ops", [P, 2, 256])
        levels = tuple((n, w) for n, w in enumerate(BLOCKS) if w <= DEC_T)
        n0 = levels[0][0]
        qT, kT, lfT, bT = (sb(n, [P, GW]) for n in ("qT", "kT", "lfT", "bT"))
        v_tok, gate = sb("v_tok", [P, GW]), sb("gate", [P, GW])
        go = sb("go", [P, P])
        lv = sb("lv", [P, SLOTS - n0, GW])
        runs = sb("runs", [P, DEC_B])
        own = sb("own", [P, DEC_B, P])
        S = sb("S", [P, DEC_B, H, DV])
        qe = sb("qe", [P, 2, DEC_B, P])
        v_own = sb("v_own", [P, 2, DEC_B, DV])
        ebc = sb("ebc", [P, H, DEC_B])
        level = sb("level", [P, NL, P])
        masked = sb("masked", [P, 3, P])
        att = sb("att", [P, H, P])
        kd_tok = sb("kd_tok", [P, GW])
        o_rows = sb("o_rows", [P, GW])
        sq = sb("sq", [P, GW])
        oss = sb("oss", [P, 3, H])
        ng = sb("ng", [P, DV])
        eps = sb("eps", [P, 1])
        lps, kps = pps
        rps = ops[:, :, :].rearrange("p a (b v) -> p (a b) v", v=DV)
        ups = [tps, [sps[b][:, :].rearrange("p (b v) -> p b v", v=DV) for b in range(2)]]
        s = {n: sem(n) for n in ("pages", "new", "consts", "zero", "sign", "new_ps", "Q", "K_new", "kT_ps", "kT", "scores", "row_max",
                                 "neg_max", "exp", "recip", "coef", "pT_ps", "pT", "outs", "part", "w_load",
                                 "load", "state_load", "eps", "cumsum", "diff", "decay", "ebc", "operands", "levels", "masked", "att",
                                 "kdT_ps", "kd_tok", "qe", "v_own", "av", "gain_ps", "scaled", "state", "o_sq", "o_ss", "o_root",
                                 "o_rs", "o_norm", "o_g", "o_out", "r_store")}
        s["kc"] = [sem(f"kc{p}") for p in range(AHEAD)]
        s["vc"] = [sem(f"vc{p}") for p in range(AHEAD)]
        s["part_store"] = [sem(f"part_store{p}") for p in range(2)]
        block = open_block(nc, ctx, s.values())

        @block.sync
        def _(sp):
            loads = ((lfT[:, :], io["hl_s"]), (go[:, :], io["run_go"]), (qT[:, :], io["hq_s"]), (kT[:, :], io["hk_s"]),
                     (v_tok[:, :], io["hv_s"]), (gate[:, :], io["hg_s"]), (level[:, :, :], io["level_mask"]),
                     (runs[:, :], io["runs"]), (own[:, :, :], io["own"]),
                     (ng[:, :], io["hgrn_norm_g"].partition_broadcast(P).rearrange("p a b -> p (a b)")))
            for dst, src in loads:
                sp.dma_start(dst, src).then_inc(s["load"], 16)
            sp.dma_start(S[:, :, :, :].rearrange("p b h v -> p (b h) v"), io["state"].rearrange("b h d v -> d (b h) v")).then_inc(s["state_load"], 16)
            sp.dma_start(pages[:, :], io["page_table"]).then_inc(s["pages"], 16)
            sp.dma_start(qk_new[:, 0], io["q_s"][NP * P:NP * P + NS, :]).then_inc(s["new"], 16)
            sp.dma_start(qk_new[:, 1], io["k_s"]).then_inc(s["new"], 16)
            sp.dma_start(mask[:, :], io["new_mask"]).then_inc(s["consts"], 16)
            sp.dma_start(is_map[:, :], io["is_map"]).then_inc(s["consts"], 16)
            sp.wait_ge(s["pages"], 16)

            def store_part(j):
                sp.wait_ge(s["part"], j + 1)
                sp.dma_start(io["part_s"][j], part[:, j % 2]).then_inc(s["part_store"][j % 2], 16)

            for j in range(DEC_B):
                if j == AHEAD:
                    for g in range(2):
                        sp.dma_start(w_out[:, g], io["w_out"].rearrange("(k p) n -> p k n", p=P)[:, :, g * GW:(g + 1) * GW])\
                          .then_inc(s["w_load"], 16)
                    sp.wait_ge(s["state"], H)
                    sp.dma_start(io["s_s"].rearrange("b h d v -> d (b h) v"), S[:, :, :, :].rearrange("p b h v -> p (b h) v")).then_inc(s["r_store"], 16)
                    sp.wait_ge(s["o_out"], 1)
                    sp.dma_start(io["mr_s"][NP * P:NP * P + NS, :], o_rows[0:NS, :]).then_inc(s["r_store"], 16)
                if j >= AHEAD:
                    sp.wait_ge(s["kT_ps"], 4 * (j - AHEAD + 1))
                    sp.wait_ge(s["outs"], j - AHEAD + 1)
                b = j % AHEAD
                for g in range(NPG):
                    page = sp.value_load(pages[0:1, j * NPG + g:j * NPG + g + 1], min_val=0, max_val=N_POOL - 1)
                    sp.dma_start(kc[:, b, g], io["cache_k"][bass.ds(page * PAGE, PAGE), :]).then_inc(s["kc"][b], 16)
                    sp.dma_start(vc[:, b, g], io["cache_v"][bass.ds(page * PAGE, PAGE), :]).then_inc(s["vc"][b], 16)
                sp.dma_start(v_new[:, b], io["v_s"][j * DEC_T:(j + 1) * DEC_T, :]).then_inc(s["vc"][b], 16)
                if j >= AHEAD:
                    store_part(j - AHEAD)
            for j in range(DEC_B - AHEAD, DEC_B):
                store_part(j)
            sp.wait_ge(s["w_load"], 32)
            sp.wait_ge(s["r_store"], 32)
            for p in range(2):
                sp.wait_ge(s["part_store"][p], 16 * DEC_B // 2)

        @block.gpsimd
        def _(pool):
            pool.memset(Q[:, :, :, :], 0.0).then_inc(s["zero"], 1)
            pool.memset(zero[:, :], 0.0).then_inc(s["zero"], 1)
            pool.wait_ge(s["zero"], 2)
            pool.wait_ge(s["decay"], 1)
            decay_products(pool, lv, qT[:, :], kT[:, :], levels, n0).then_inc(s["operands"], 1)
            for h in range(H):
                if h >= 2:
                    pool.wait_ge(s["gain_ps"], h - 1)
                pool.tensor_tensor(v_own[:, h % 2], v_tok[:, None, h * DV:(h + 1) * DV].broadcast_to([P, DEC_B, DV]),
                                   runs[:, :, None].broadcast_to([P, DEC_B, DV]), ALU.mult).then_inc(s["v_own"], 1)
            pool.wait_ge(s["o_norm"], 1)
            r3 = o_rows[:, :].rearrange("p (h v) -> p h v", h=H)
            pool.tensor_tensor(r3, r3, ng[:, None, :].broadcast_to([P, H, DV]), ALU.mult).then_inc(s["o_g"], 1)
            pool.wait_ge(s["o_g"], 1)
            pool.tensor_tensor(o_rows[:, :], o_rows[:, :], gate[:, :], ALU.mult).then_inc(s["o_out"], 1)

        @block.scalar
        def _(act):
            act.wait_ge(s["diff"], 1)
            act.activation(lv[:, :, :], lv[:, :, :], ACT.Exp).then_inc(s["decay"], 1)
            act.activation(ebc[:, :, :], bT[:, :].rearrange("p (h b t) -> p h b t", h=H, t=DEC_T)[:, :, 0:DEC_B, DEC_T - 1],
                           ACT.Exp).then_inc(s["ebc"], 1)
            act.wait_ge(s["kdT_ps"], 1)
            act.activation(kd_tok[:, :], kps[:, :, :].rearrange("p h d -> p (h d)"), ACT.Copy).then_inc(s["kd_tok"], 1)
            act.wait_ge(s["av"], H)
            act.wait_ge(s["eps"], 1)
            act.activation(sq[:, :], rps[:, :, :].rearrange("p h v -> p (h v)"), ACT.Square).then_inc(s["o_sq"], 1)
            act.wait_ge(s["o_ss"], 1)
            act.activation(oss[:, 1], oss[:, 0], ACT.Sqrt, bias=eps[:, 0:1], scale=1.0 / DV).then_inc(s["o_root"], 1)
            def keys_out(j):
                for g in range(NPG):
                    act.wait_ge(s["kT_ps"], 4 * j + g + 1)
                    if j >= 2:
                        act.wait_ge(s["scores"], 2 * (j - 1))
                    act.activation(KT[:, j % 2, :, g * PAGE:(g + 1) * PAGE], tps[g % 2][:, :, :], ACT.Copy).then_inc(s["kT"], 1)

            keys_out(0)
            for j in range(DEC_B):
                if j + 1 < DEC_B:
                    keys_out(j + 1)
                act.wait_ge(s["neg_max"], j + 1)
                act.activation(sc[:, j % 2, :], sc[:, j % 2, :], ACT.Exp, bias=nmx[:, j % 2:j % 2 + 1],
                               accum_out=l[:, j % 2:j % 2 + 1]).then_inc(s["exp"], 1)

        @block.vector
        def _(dve):
            dve.memset(eps[:, :], EPS).then_inc(s["eps"], 1)
            dve.wait_ge(s["load"], 160)
            for h in range(H):
                cols = slice(h * P, (h + 1) * P)
                last = dve.tensor_tensor_scan(bT[:, cols], go[:, :], lfT[:, cols], 0.0, ALU.mult, ALU.add)
            last.then_inc(s["cumsum"], 1)
            dve.wait_ge(s["cumsum"], 1)
            decay_differences(dve, bT[:, :], lv, levels, DEC_T, n0).then_inc(s["diff"], 1)
            dve.wait_ge(s["operands"], 1)
            for h in range(H):
                dve.wait_ge(s["levels"], h + 1)
                dve.wait_ge(s["att"], h)
                dve.tensor_tensor(masked[:, :, :], lps[:, 0:3, :], level[:, n0:, :], ALU.mult).then_inc(s["masked"], 1)
                dve.wait_ge(s["masked"], h + 1)
                dve.tensor_reduce(att[:, h], masked[:, :, :].rearrange("p l t -> p t l"), AX.X, ALU.add).then_inc(s["att"], 1)
                if h >= 2:
                    dve.wait_ge(s["av"], h - 1)
                dve.tensor_tensor(qe[:, h % 2], lv[:, LEAF_QE - n0, None, h * P:(h + 1) * P].broadcast_to([P, DEC_B, P]), own[:, :, :],
                                  ALU.mult).then_inc(s["qe"], 1)
            dve.wait_ge(s["state_load"], 16)
            dve.wait_ge(s["ebc"], 1)
            for h in range(H):
                dve.wait_ge(s["av"], h + 1)
                dve.tensor_tensor(S[:, :, h], S[:, :, h], ebc[:, h, :, None].broadcast_to([P, DEC_B, DV]), ALU.mult).then_inc(s["scaled"], 1)
                dve.wait_ge(s["scaled"], h + 1)
                dve.wait_ge(s["gain_ps"], h + 1)
                for b in range(2):
                    last = dve.tensor_tensor(S[:, 4 * b:4 * b + 4, h], S[:, 4 * b:4 * b + 4, h], ups[h % 2][b][:, :, :], ALU.add)
                last.then_inc(s["state"], 1)
            r3 = o_rows[:, :].rearrange("p (h v) -> p h v", h=H)
            dve.wait_ge(s["o_sq"], 1)
            dve.tensor_reduce(oss[:, 0], sq[:, :].rearrange("p (h v) -> p h v", h=H), AX.X, ALU.add).then_inc(s["o_ss"], 1)
            dve.wait_ge(s["o_root"], 1)
            dve.reciprocal(oss[:, 2], oss[:, 1]).then_inc(s["o_rs"], 1)
            dve.wait_ge(s["o_rs"], 1)
            dve.tensor_tensor(r3, rps[:, :, :], oss[:, 2, :, None].broadcast_to([P, H, DV]), ALU.mult).then_inc(s["o_norm"], 1)
            dve.wait_ge(s["consts"], 32)
            dve.wait_ge(s["zero"], 2)
            dve.scalar_tensor_tensor(out=sign[:, :], in0=is_map[:, 1:2], scalar=nlam[:, 0:1], in1=is_map[:, 0:1],
                                     op0=ALU.mult, op1=ALU.add).then_inc(s["sign"], 1)
            dve.wait_ge(s["new_ps"], 1)
            for m in range(2):
                r = slice(m * DQ, (m + 1) * DQ)
                for h in range(H):
                    last = dve.tensor_copy(Q[r, :, h, m * DEC_T:(m + 1) * DEC_T],
                                           pps[0][r, h, 0:NS].rearrange("p (b t) -> p b t", b=DEC_B))
            last.then_inc(s["Q"], 1)
            dve.wait_ge(s["new_ps"], 2)
            dve.tensor_copy(K_new[:, :, :], pps[1][:, :, 0:NS]).then_inc(s["K_new"], 1)
            dve.wait_ge(s["sign"], 1)

            def weights_out(j):
                for a in range(2):
                    dve.wait_ge(s["pT_ps"], 2 * j + a + 1)
                    if j >= 2:
                        dve.wait_ge(s["outs"], j - 1)
                    if a == 0:
                        dve.tensor_copy(PT[:, j % 2, 0:NPG], pps[0][:, :, :]).then_inc(s["pT"], 1)
                    else:
                        dve.tensor_copy(PT[0:DEC_T, j % 2, NPG], pps[1][0:DEC_T, 0, :]).then_inc(s["pT"], 1)

            def out_part(j):
                b = j % 2
                dve.wait_ge(s["exp"], j + 1)
                dve.reciprocal(rl[:, b:b + 1], l[:, b:b + 1]).then_inc(s["recip"], 1)
                dve.wait_ge(s["recip"], j + 1)
                dve.tensor_tensor(coef[:, b:b + 1], rl[:, b:b + 1], sign[:, :], ALU.mult).then_inc(s["coef"], 1)
                dve.wait_ge(s["coef"], j + 1)
                dve.wait_ge(s["outs"], j + 1)
                if j >= 2:
                    dve.wait_ge(s["part_store"][b], 16 * (j // 2))
                dve.tensor_scalar(part[:, b], ops[:, b, 0:DV], coef[:, b:b + 1], None, ALU.mult).then_inc(s["part"], 1)

            for j in range(DEC_B + 1):
                if j < DEC_B:
                    b = j % 2
                    dve.wait_ge(s["scores"], 2 * j + 1)
                    if j >= 2:
                        dve.wait_ge(s["pT_ps"], 2 * j - 2)
                    dve.tensor_tensor_reduce(sc[:, b, 0:PAST], sps[b][:, :], zero[:, :], SCALE, -3e38, ALU.add, ALU.max,
                                             mx[:, b, 0:1]).then_inc(s["row_max"], 1)
                    dve.wait_ge(s["scores"], 2 * j + 2)
                    dve.tensor_tensor_reduce(sc[:, b, PAST:NK], nps[:, b, 0:DEC_T], mask[:, :], SCALE, -3e38, ALU.add, ALU.max,
                                             mx[:, b, 1:2]).then_inc(s["row_max"], 1)
                    dve.wait_ge(s["row_max"], 2 * j + 2)
                    if j >= 2:
                        dve.wait_ge(s["exp"], j - 1)
                    dve.tensor_reduce(nmx[:, b:b + 1], mx[:, b, :], AX.X, ALU.max, negate=True).then_inc(s["neg_max"], 1)
                if j >= 1:
                    weights_out(j - 1)
                    out_part(j - 1)

        @block.tensor
        def _(pe):
            pe.wait_ge(s["operands"], 1)
            for h in range(H):
                mm = pe.transpose(kps[:, h, :], lv[:, LEAF_KD - n0, h * P:(h + 1) * P], ident[:, :])
            mm.then_inc(s["kdT_ps"], 1)

            def products(h):
                c = slice(h * P, (h + 1) * P)
                if h >= 1:
                    pe.wait_ge(s["masked"], h)
                for a, (n, _) in enumerate(levels):
                    pe.matmul(lps[:, a, :], lv[:, n - n0, c], lv[:, n - n0, c], start=True, stop=True)
                pe.matmul(lps[:, 2, :], lv[:, LEAF_K - n0, c], lv[:, LEAF_Q - n0, c], start=True, stop=True).then_inc(s["levels"], 1)

            products(0)
            for h in range(H):
                if h + 1 < H:
                    products(h + 1)
                pe.wait_ge(s["att"], h + 1)
                pe.wait_ge(s["qe"], h + 1)
                pe.wait_ge(s["state_load"], 16)
                pe.matmul(rps[:, h, :], att[:, h, :], v_tok[:, h * DV:(h + 1) * DV], start=True, stop=False)
                for b in range(DEC_B):
                    mm = pe.matmul(rps[:, h, :], qe[:, h % 2, b, :], S[:, b, h, :], start=False, stop=(b == DEC_B - 1))
                mm.then_inc(s["av"], 1)
            pe.wait_ge(s["kd_tok"], 1)
            for h in range(H):
                pe.wait_ge(s["v_own"], h + 1)
                if h >= 2:
                    pe.wait_ge(s["state"], h - 1)
                for b in range(2):
                    mm = pe.matmul(ups[h % 2][b][:, :, :].rearrange("p b v -> p (b v)"), kd_tok[:, h * P:(h + 1) * P],
                                   v_own[:, h % 2, 4 * b:4 * b + 4, :].rearrange("p b v -> p (b v)"), start=True, stop=True)
                mm.then_inc(s["gain_ps"], 1)
            pe.wait_ge(s["masked"], H)
            pe.wait_ge(s["kd_tok"], 1)
            pe.wait_ge(s["state"], H)
            pe.wait_ge(s["o_norm"], 1)
            pe.wait_ge(s["new"], 32)
            for n in range(2):
                for h in range(H):
                    mm = pe.transpose(pps[n][:, h, 0:NS], qk_new[:, n, h * P:(h + 1) * P], ident[0:NS, 0:NS])
                mm.then_inc(s["new_ps"], 1)

            def key_columns(j):
                pe.wait_ge(s["kc"][j % AHEAD], 64 * (j // AHEAD + 1))
                for g in range(NPG):
                    n = 4 * j + g
                    if n >= 2:
                        pe.wait_ge(s["kT"], n - 1)
                    for h in range(H):
                        mm = pe.transpose(tps[g % 2][:, h, :], kc[:, j % AHEAD, g, h * P:(h + 1) * P], ident[:, :])
                    mm.then_inc(s["kT_ps"], 1)

            def scores(j):
                b = j % 2
                pe.wait_ge(s["kT"], 4 * j + 4)
                if j >= 2:
                    pe.wait_ge(s["row_max"], 2 * j - 2)
                for h in range(H):
                    mm = pe.matmul(sps[b][32 * h:32 * h + 32, :], Q[:, j, h, :], KT[:, b, h, :], start=True, stop=True)
                mm.then_inc(s["scores"], 1)
                if j >= 1:
                    pe.wait_ge(s["row_max"], 2 * j)
                for h in range(H):
                    mm = pe.matmul(nps[32 * h:32 * h + 32, b, 0:DEC_T], Q[:, j, h, :], K_new[:, h, j * DEC_T:(j + 1) * DEC_T],
                                   start=True, stop=True)
                mm.then_inc(s["scores"], 1)

            def weight_columns(j):
                pe.wait_ge(s["exp"], j + 1)
                if j >= 1:
                    pe.wait_ge(s["pT"], 2 * j)
                for g in range(NPG):
                    mm = pe.transpose(pps[0][:, g, :], sc[:, j % 2, g * PAGE:(g + 1) * PAGE], ident[:, :])
                mm.then_inc(s["pT_ps"], 1)
                pe.transpose(pps[1][0:DEC_T, 0, :], sc[:, j % 2, PAST:NK], ident[:, :]).then_inc(s["pT_ps"], 1)

            def values(j):
                b = j % 2
                pe.wait_ge(s["pT"], 2 * j + 2)
                pe.wait_ge(s["vc"][j % AHEAD], 16 * (NPG + 1) * (j // AHEAD + 1))
                if j >= 1:
                    pe.wait_ge(s["part"], j)
                for h in range(H):
                    out = ops[32 * h:32 * h + 32, b, 0:DV]
                    for g in range(NPG):
                        pe.matmul(out, PT[:, b, g, 32 * h:32 * h + 32], vc[:, j % AHEAD, g, h * DV:(h + 1) * DV], start=(g == 0), stop=False)
                    mm = pe.matmul(out, PT[0:DEC_T, b, NPG, 32 * h:32 * h + 32], v_new[:, j % AHEAD, h * DV:(h + 1) * DV],
                                   start=False, stop=True)
                mm.then_inc(s["outs"], 1)

            key_columns(0)
            pe.wait_ge(s["Q"], 1)
            pe.wait_ge(s["K_new"], 1)
            for j in range(DEC_B + 1):
                if j < DEC_B:
                    scores(j)
                if j >= 1:
                    weight_columns(j - 1)
                    values(j - 1)
                if j + 1 < DEC_B:
                    key_columns(j + 1)


def pass_output(nc, io, keep):
    with ExitStack() as ctx:
        def sb(name, shape, dt=F32):
            return ctx.enter_context(nc.sbuf_tensor("y_" + name, shape, dt))

        def sem(name):
            return ctx.enter_context(nc.semaphore("y_" + name))

        def ps(name, shape):
            return ctx.enter_context(nc.psum_tensor("y_" + name, shape, F32))

        ident, stage = keep[0], keep[3]
        w_hi, w_lo = sb("w_hi", [P, KD, D], F32R), sb("w_lo", [P, KD, D], F32R)
        o_in, ga, mr = (sb(n, [P, 2, GW]) for n in ("o_in", "ga", "mr"))
        xt = sb("xt", [P, 2, D])
        yt = sb("yt", [P, 2, D])
        maps = sb("maps", [NS, 2, H, DV])
        sq = sb("sq", [P, GW])
        oss = sb("oss", [P, 3, H])
        ng = sb("ng", [P, 2, DV])
        eps = sb("eps", [P, 1])
        mT_hi = [sb(f"mT_hi{p}", [P, KD, P], F32R) for p in range(2)]
        mT_lo = [sb(f"mT_lo{p}", [P, KD, P], F32R) for p in range(2)]
        yps = [[ps(f"yps{p}{g}", [P, GW]) for g in range(2)] for p in range(2)]
        tps = [ps(f"tps{b}", [P, 4, P]) for b in range(2)]
        s = {n: sem(n) for n in ("w_hi", "w_lo", "ng", "ng_scaled", "eps", "o_sq", "o_ss", "o_root", "o_rs", "o_norm",
                                 "o_g", "gated", "mT_ps", "mT_hi", "mT_lo", "y_ps", "y",
                                 "maps", "sum", "sum_store")}
        for n in ("o_load", "ga_load", "mr_load", "x_load", "store"):
            s[n] = [sem(f"{n}{p}") for p in range(2)]
        block = open_block(nc, ctx, s.values())

        def over_tiles(eng, step):
            step(0, 0, 0, True)
            step(1, 1, 0, True)
            with eng.Fori(1, NP // 2) as j:
                for p in range(2):
                    step(j * 2 + p, p, j, True)
            step(NP, 0, NP // 2, False)

        @block.sync
        def _(sp):
            def load(i, p, rows=P):
                r = bass.ds(i * P, rows)
                sp.dma_start(o_in[0:rows, p], io["o_s"][r, :]).then_inc(s["o_load"][p], 16)
                sp.dma_start(ga[0:rows, p], io["ga_s"][r, :]).then_inc(s["ga_load"][p], 16)
                sp.dma_start(mr[0:rows, p], io["mr_s"][r, :]).then_inc(s["mr_load"][p], 16)

            def load_x(i, p, rows=P):
                sp.dma_start(xt[0:rows, p], io["x"][bass.ds(i * P, rows), :]).then_inc(s["x_load"][p], 16)

            sp.dma_start(ng[:, 0], io["subln_g"].partition_broadcast(P).rearrange("p a b -> p (a b)")).then_inc(s["ng"], 16)
            load(0, 0)
            load(1, 1)
            load_x(0, 0)
            load_x(1, 1)
            for j in range(DEC_B):
                for m in range(2):
                    src = io["part_s"][j].rearrange("(h x) v -> x h v", h=H)[m * DEC_T:(m + 1) * DEC_T]
                    sp.dma_start(maps[j * DEC_T:(j + 1) * DEC_T, m], src).then_inc(s["maps"], 16)

            def store(i, p, rows, dst):
                sp.wait_ge(s["y"], 2 * i + 2)
                sp.dma_start(dst, yt[0:rows, p]).then_inc(s["store"][p], 16)

            with sp.Fori(0, NP // 2 - 1) as j:
                for p in range(2):
                    i = j * 2 + p
                    sp.wait_ge(s["mT_ps"], 2 * i + 2)
                    load(i + 2, p)
                    store(i, p, P, io["y_p"][bass.ds(i * P, P), :])
                    load_x(i + 2, p)
            sp.wait_ge(s["sum"], 1)
            sp.dma_start(io["o_s"][NP * P:NP * P + NS, :], maps[:, 0].rearrange("p h v -> p (h v)")).then_inc(s["sum_store"], 16)
            sp.wait_ge(s["mT_ps"], 2 * NP - 2)
            sp.wait_ge(s["sum_store"], 16)
            load(NP, 0, NS)
            store(NP - 2, 0, P, io["y_p"][(NP - 2) * P:(NP - 1) * P, :])
            load_x(NP, 0, NS)
            store(NP - 1, 1, P, io["y_p"][(NP - 1) * P:NP * P, :])
            store(NP, 0, NS, io["y_s"])
            sp.wait_ge(s["store"][0], 16 * (NP // 2 + 1))
            sp.wait_ge(s["store"][1], 16 * (NP // 2))

        @block.gpsimd
        def _(pool):
            def gates(i, p, j):
                o3 = o_in[:, p].rearrange("p (h v) -> p h v", h=H)
                pool.wait_ge(s["o_norm"], i + 1)
                pool.tensor_tensor(o3, o3, ng[:, 1, None, :].broadcast_to([P, H, DV]), ALU.mult).then_inc(s["o_g"], 1)
                pool.wait_ge(s["o_g"], i + 1)
                pool.wait_ge(s["ga_load"][p], j * 16 + 16)
                pool.tensor_tensor(o_in[:, p], o_in[:, p], ga[:, p], ALU.mult).then_inc(s["gated"], 1)

            pool.wait_ge(s["ng_scaled"], 1)
            over_tiles(pool, lambda i, p, j, more: gates(i, p, j))

        @block.scalar
        def _(act):
            def squares(i, p, load):
                act.wait_ge(s["o_load"][p], load)
                after(act, s["o_ss"], i)
                act.activation(sq[:, :], o_in[:, p], ACT.Square).then_inc(s["o_sq"], 1)
                act.wait_ge(s["o_ss"], i + 1)
                act.activation(oss[:, 1], oss[:, 0], ACT.Sqrt, bias=eps[:, 0:1], scale=1.0 / DV).then_inc(s["o_root"], 1)

            def hi_parts(i, p):
                for b in range(2):
                    act.wait_ge(s["mT_ps"], 2 * i + b + 1)
                    act.activation(mT_hi[p][:, 4 * b:4 * b + 4, :], tps[b][:, :, :], ACT.Copy).then_inc(s["mT_hi"], 1)

            def step(i, p, j, more):
                if more:
                    squares(i + 1, 1 - p, (j + p) * 16 + 16)
                    hi_parts(i + 1, 1 - p)

            act.wait_ge(s["eps"], 1)
            squares(0, 0, 16)
            for n in range(4):
                ks, cols = slice(n % 2 * 4, n % 2 * 4 + 4), slice(n // 2 * GW, n // 2 * GW + GW)
                act.activation(w_hi[:, ks, cols], stage[:, n // 2, ks], ACT.Copy).then_inc(s["w_hi"], 1)
                if n == 1:
                    hi_parts(0, 0)
            over_tiles(act, step)

        @block.vector
        def _(dve):
            def norm(i, p):
                o3 = o_in[:, p].rearrange("p (h v) -> p h v", h=H)
                dve.wait_ge(s["o_sq"], i + 1)
                dve.tensor_reduce(oss[:, 0], sq[:, :].rearrange("p (h v) -> p h v", h=H), AX.X, ALU.add).then_inc(s["o_ss"], 1)
                dve.wait_ge(s["o_root"], i + 1)
                dve.reciprocal(oss[:, 2], oss[:, 1]).then_inc(s["o_rs"], 1)
                dve.wait_ge(s["o_rs"], i + 1)
                dve.tensor_tensor(o3, o3, oss[:, 2, :, None].broadcast_to([P, H, DV]), ALU.mult).then_inc(s["o_norm"], 1)

            def lo_parts(i, p):
                for b in range(2):
                    dve.wait_ge(s["mT_hi"], 2 * i + b + 1)
                    dve.tensor_tensor(mT_lo[p][:, 4 * b:4 * b + 4, :], tps[b][:, :, :],
                                      f32(mT_hi[p][:, 4 * b:4 * b + 4, :]), ALU.subtract).then_inc(s["mT_lo"], 1)

            def step(i, p, j, more):
                if more:
                    norm(i + 1, 1 - p)
                    lo_parts(i + 1, 1 - p)
                dve.wait_ge(s["x_load"][p], j * 16 + 16)
                after(dve, s["store"][p], j * 16)
                for g in range(2):
                    dve.wait_ge(s["y_ps"], 2 * i + g + 1)
                    dve.tensor_tensor(yt[:, p, g * GW:(g + 1) * GW], yps[p][g][:, :], xt[:, p, g * GW:(g + 1) * GW],
                                      ALU.add).then_inc(s["y"], 1)
                if isinstance(i, int) and i == 0:
                    dve.wait_ge(s["maps"], 16 * 2 * DEC_B)
                    dve.tensor_tensor(maps[:, 0], maps[:, 0], maps[:, 1], ALU.add).then_inc(s["sum"], 1)

            dve.memset(eps[:, :], EPS).then_inc(s["eps"], 1)
            dve.wait_ge(s["ng"], 16)
            dve.tensor_scalar(ng[:, 1], ng[:, 0], 1.0 - LAM_INIT, None, ALU.mult).then_inc(s["ng_scaled"], 1)
            norm(0, 0)
            for n in range(4):
                dve.wait_ge(s["w_hi"], n + 1)
                ks, cols = slice(n % 2 * 4, n % 2 * 4 + 4), slice(n // 2 * GW, n // 2 * GW + GW)
                dve.tensor_tensor(w_lo[:, ks, cols], stage[:, n // 2, ks], f32(w_hi[:, ks, cols]), ALU.subtract).then_inc(s["w_lo"], 1)
                if n == 1:
                    lo_parts(0, 0)
            over_tiles(dve, step)

        @block.tensor
        def _(pe):
            def columns(i, p, load):
                after(pe, s["mT_lo"], 2 * i)
                pe.wait_ge(s["mr_load"][p], load)
                for b, src in ((0, o_in), (1, mr)):
                    if b == 0:
                        pe.wait_ge(s["gated"], i + 1)
                    for k in range(4):
                        mm = pe.transpose(tps[b][:, k, :], src[:, p, k * P:(k + 1) * P], ident[:, :])
                    mm.then_inc(s["mT_ps"], 1)

            def step(i, p, j, more):
                pe.wait_ge(s["mT_lo"], 2 * i + 2)
                for g in range(2):
                    if isinstance(i, int) and i == 0:
                        pe.wait_ge(s["w_lo"], 2 * g + 2)
                    after(pe, s["y"], 4 * j)
                    product3(pe, yps[p][g][:, :], mT_hi[p], mT_lo[p], w_hi, w_lo, slice(g * GW, (g + 1) * GW)).then_inc(s["y_ps"], 1)
                    if g == 0 and more:
                        columns(i + 1, 1 - p, (j + p) * 16 + 16)

            columns(0, 0, 16)
            over_tiles(pe, step)


def build_program(nc, io):
    with ExitStack() as ctx:
        ident = ctx.enter_context(nc.sbuf_tensor("ident", [P, P], F32))
        rstd = ctx.enter_context(nc.sbuf_tensor("rstd", [P, 32], F32))
        nlam = ctx.enter_context(nc.sbuf_tensor("nlam", [P, 16], F32))
        keep = (ident, rstd, nlam)
        pass_attention_inputs(nc, io, keep)
        pass_hgrn(nc, io, keep)
        pass_attention(nc, io, keep)
        w_out = ctx.enter_context(nc.sbuf_tensor("w_out", [P, 2, KD, GW], F32))
        pass_samples(nc, io, keep + (w_out,))
        pass_output(nc, io, keep + (w_out,))


def rotary_table():
    inv = (np.float32(500000.0) ** (-np.arange(0, 2 * HALF, 2, dtype=np.float32) / np.float32(2 * HALF))).astype(np.float32)
    pos = np.concatenate([np.arange(SEQ), PAST + np.tile(np.arange(DEC_T), DEC_B), np.zeros(P - NS)]).astype(np.float32)
    ang = (pos[:, None] * inv[None, :]).astype(np.float32)
    c, n = np.cos(ang), np.sin(ang)
    table = np.concatenate([c, c, -n, n], axis=1).astype(np.float32)
    return np.ascontiguousarray(table.reshape(NT, P, 4 * HALF).transpose(1, 0, 2))


def shape_constants():
    t = np.arange(P)
    level = np.zeros((P, NL, P), np.float32)
    for n, w in enumerate(BLOCKS):
        same = (t[:, None] // w) == (t[None] // w)
        level[:, n] = same & (t[:, None] % w < w // 2) & (t[None] % w >= w // 2)
    level[:, NL - 1] = (t[:, None] // 2 == t[None] // 2) & (t[:, None] <= t[None])
    causal = np.zeros((P, 4 * P), np.float32)
    causal[:, 3 * P:] = np.where(t[None] > t[:, None], NEG, 0.0)
    new_mask = np.where(np.arange(DEC_T)[None] > (t % DEC_T)[:, None], NEG, 0.0).astype(np.float32)
    is_map = np.stack([(t % 32) // DEC_T == 0, (t % 32) // DEC_T == 1], 1).astype(np.float32)
    return {
        "rope": rotary_table(), "level_mask": level, "causal": causal, "new_mask": new_mask, "is_map": is_map,
        "run_go": np.tile((t % DEC_T != 0).astype(np.float32)[None], (P, 1)),
        "runs": (t[:, None] // DEC_T == np.arange(DEC_B)[None]).astype(np.float32),
        "own": np.tile((t[None] // DEC_T == np.arange(DEC_B)[:, None]).astype(np.float32)[None], (P, 1, 1)),
    }


_OUTS = {"y_p": (SEQ, D), "y_s": (NS, D), "k_p": (SEQ, GW), "v_p": (SEQ, GW), "s_p": (H, P, DV),
         "k_s": (NS, GW), "v_s": (NS, GW), "s_s": (DEC_B, H, P, DV)}
_SCRATCH = {"q_s": (NT * P, GW), "ga_s": (NT * P, GW), "o_s": (NT * P, GW), "mr_s": (NT * P, GW), "part_s": (DEC_B, P, DV),
            "hq_s": (P, GW), "hk_s": (P, GW), "hl_s": (P, GW), "hv_s": (P, GW), "hg_s": (P, GW)}


def kernel(**inputs):
    import concourse.bacc as _bacc
    from concourse.bass_utils import run_bass_kernel_spmd as _run

    a = {k: np.asarray(v) for k, v in inputs.items()}
    arrays = {
        "x": np.concatenate([a["x_prompt"].reshape(SEQ, D), a["x_sample"].reshape(NS, D), np.zeros((P - NS, D), np.float32)]),
        "cache_k": a["cache_k"].reshape(N_POOL * PAGE, GW),
        "cache_v": a["cache_v"].reshape(N_POOL * PAGE, GW),
        "state": a["state_hgrn"].reshape(DEC_B, H, P, DV),
        "page_table": a["page_table"].reshape(1, DEC_B * NPG),
        "norm_g": a["norm_g"].reshape(KD, P).T,
        "w_in": a["w_in"].reshape(D, NG * GW),
        "lb": a["hgrn_lb_logits"].reshape(2, H, P).transpose(2, 0, 1),
        "w_out": a["w_out"].reshape(D, D),
    }
    for name in ("q_norm_g", "k_norm_g", "lambda_q1", "lambda_k1", "lambda_q2", "lambda_k2", "subln_g", "hgrn_norm_g"):
        arrays[name] = a[name]
    arrays.update(shape_constants())
    nc = _bacc.Bacc("TRN2", target_bir_lowering=False, num_devices=1)
    io, fed = {}, {}
    for name, v in arrays.items():
        v = np.ascontiguousarray(v)
        fed[f"in_{name}"] = v
        io[name] = nc.dram_tensor(f"in_{name}", v.shape, mybir.dt.from_np(v.dtype), kind="ExternalInput").ap()
    for name, shape in _OUTS.items():
        io[name] = nc.dram_tensor(f"out_{name}", shape, F32, kind="ExternalOutput").ap()
    for name, shape in _SCRATCH.items():
        io[name] = nc.dram_tensor(f"tmp_{name}", shape, F32, kind="Internal").ap()
    build_program(nc, io)
    r = _run(nc, [fed], core_ids=[0]).results[0]
    o = {name: r[f"out_{name}"] for name in _OUTS}
    return (o["y_p"].reshape(1, SEQ, D), o["y_s"].reshape(DEC_B, DEC_T, D),
            o["k_p"].reshape(1, 1, SEQ, H, P), o["v_p"].reshape(1, 1, SEQ, H, DV), o["s_p"].reshape(1, 1, H, P, DV),
            o["k_s"].reshape(1, DEC_B, DEC_T, H, P), o["v_s"].reshape(1, DEC_B, DEC_T, H, DV),
            o["s_s"].reshape(1, DEC_B, H, P, DV))
```
